# Optimizing a Trainium2 kernel written in Bass

```python
import jax
import jax.numpy as jnp
from jax import lax
import numpy as np

D_MODEL = 2048
BATCH = 1
SEQ = 256
DEPTH = 1
DEC_BATCH = 8
DEC_SEQ = 4
PAST_LEN = 256
PAGE_SIZE = 128

D_MIX = D_MODEL
CONV_CH = D_MIX // 2
CONV_W = 31
N_HEADS = 8
HEAD_DIM = (D_MIX - CONV_CH) // N_HEADS
ATT_W = N_HEADS * HEAD_DIM
ROT_DIM = HEAD_DIM // 4
ROPE_THETA = 500000.0
WINDOWS = (128, 512, 2048)
DILATIONS = (1, 4, 16)
Q_BLOCK = 128
WIN_MAX = max(WINDOWS)
ATT_SCALE = HEAD_DIM ** -0.5
IN_COLS = 2 * CONV_CH + 3 * ATT_W
N_ADA = 6
PEER_HEADS = 8
PEER_NKEYS = 128
PEER_DK = 128
PEER_TOPK = 16
N_EXPERTS = PEER_NKEYS * PEER_NKEYS
TOK_BLOCK = 128
EPS = 1e-6

kernel_name = 'hymba_conformer_dilated_peer_decode_step'

def _rmsnorm(x, g):
    xf = x.astype(jnp.float32)
    y = xf * lax.rsqrt(jnp.mean(xf * xf, axis=-1, keepdims=True) + EPS)
    return (y * g.astype(jnp.float32)).astype(x.dtype)

def _rope(x, pos):
    inv = ROPE_THETA ** (-jnp.arange(0, ROT_DIM, 2, dtype=jnp.float32) / ROT_DIM)
    ang = pos.astype(jnp.float32)[:, None] * inv[None, :]
    cos = jnp.cos(ang)[None, :, None, :]
    sin = jnp.sin(ang)[None, :, None, :]
    xr = x[..., :ROT_DIM].astype(jnp.float32)
    x1, x2 = xr[..., :ROT_DIM // 2], xr[..., ROT_DIM // 2:]
    rot = jnp.concatenate([x1 * cos - x2 * sin, x2 * cos + x1 * sin], axis=-1).astype(x.dtype)
    return jnp.concatenate([rot, x[..., ROT_DIM:]], axis=-1)

def _dwconv(xp, w, b):
    y = lax.conv_general_dilated(xp, w[:, None, :], (1,), 'VALID',
                                 dimension_numbers=('NWC', 'WIO', 'NWC'),
                                 feature_group_count=xp.shape[-1])
    return y + b

def _conv_tail(y, g, b):
    yf = y.astype(jnp.float32)
    mu = jnp.mean(yf, axis=-1, keepdims=True)
    var = jnp.mean(jnp.square(yf - mu), axis=-1, keepdims=True)
    z = (yf - mu) * lax.rsqrt(var + EPS) * g.astype(jnp.float32) + b.astype(jnp.float32)
    return jax.nn.silu(z).astype(y.dtype)

def _dilated_prompt(q, k, v, win, dil):
    B, S, H, E = q.shape
    nk = win // dil
    M = S // dil
    n_blk = -(-M // Q_BLOCK)
    Mp = n_blk * Q_BLOCK

    def by_res(t):
        return t.reshape(B, M, dil, H, E).transpose(0, 2, 1, 3, 4)

    qb = jnp.pad(by_res(q), ((0, 0), (0, 0), (0, Mp - M), (0, 0), (0, 0))).reshape(B, dil, n_blk, Q_BLOCK, H, E)

    def band(t):
        tp = jnp.pad(by_res(t), ((0, 0), (0, 0), (Q_BLOCK, Mp - M), (0, 0), (0, 0)))
        prev = tp[:, :, :Mp].reshape(B, dil, n_blk, Q_BLOCK, H, E)
        cur = tp[:, :, Q_BLOCK:].reshape(B, dil, n_blk, Q_BLOCK, H, E)
        return jnp.concatenate([prev, cur], axis=3)

    kb, vb = band(k), band(v)
    s = jnp.einsum('brnqhe,brnkhe->brnhqk', qb, kb).astype(jnp.float32) * ATT_SCALE
    qi = jnp.arange(Q_BLOCK)[:, None]
    kj = jnp.arange(2 * Q_BLOCK)[None, :]
    dist = qi + Q_BLOCK - kj
    key_m = jnp.arange(n_blk)[:, None, None] * Q_BLOCK - Q_BLOCK + kj[None]
    valid = ((dist >= 0) & (dist <= nk))[None] & (key_m >= 0)
    s = jnp.where(valid[None, None, :, None], s, -jnp.inf)
    lse = jax.nn.logsumexp(s, axis=-1)
    p = jnp.exp(s - lse[..., None]).astype(v.dtype)
    o = jnp.einsum('brnhqk,brnkhe->brnqhe', p, vb)
    o = o.reshape(B, dil, Mp, H, E)[:, :, :M].transpose(0, 2, 1, 3, 4).reshape(B, S, H, E)
    lse = lse.transpose(0, 1, 2, 4, 3).reshape(B, dil, Mp, H)[:, :, :M].transpose(0, 2, 1, 3).reshape(B, S, H)
    return o, lse

def _dilated_sample(q, k_new, v_new, k_buf, v_buf, win, dil):
    B, Sn, H, E = q.shape
    L = k_buf.shape[1]
    nk = win // dil
    idx = L + jnp.arange(Sn)[:, None] - dil * jnp.arange(nk + 1)[None, :]
    sel = (idx >= L)[None, :, :, None, None]
    ic = jnp.clip(idx, 0, L - 1)
    inn = jnp.clip(idx - L, 0, Sn - 1)
    kg = jnp.where(sel, k_new[:, inn], k_buf[:, ic])
    vg = jnp.where(sel, v_new[:, inn], v_buf[:, ic])
    s = jnp.einsum('bshe,bskhe->bhsk', q, kg).astype(jnp.float32) * ATT_SCALE
    s = jnp.where((idx >= 0)[None, None], s, -jnp.inf)
    lse = jax.nn.logsumexp(s, axis=-1)
    p = jnp.exp(s - lse[..., None]).astype(v_new.dtype)
    o = jnp.einsum('bhsk,bskhe->bshe', p, vg)
    return o, lse.transpose(0, 2, 1)

def _merge(outs):
    o = jnp.stack([oo for oo, _ in outs])
    lse = jnp.stack([ll for _, ll in outs])
    w = jax.nn.softmax(lse, axis=0)
    return jnp.einsum('pbsh,pbshe->bshe', w.astype(o.dtype), o)

def _peer(h, wq, keys, u_tab, v_tab):
    shp = h.shape
    t = h.reshape(-1, shp[-1])
    T = t.shape[0]
    n = -(-T // TOK_BLOCK)
    t = jnp.pad(t, ((0, n * TOK_BLOCK - T), (0, 0)))

    def blk(tb):
        q = (tb @ wq).reshape(TOK_BLOCK, PEER_HEADS, 2, PEER_DK)
        s = jnp.einsum('thpd,hpkd->thpk', q, keys).astype(jnp.float32)
        sv, si = lax.top_k(s, PEER_TOPK)
        cand = (sv[:, :, 0, :, None] + sv[:, :, 1, None, :]).reshape(TOK_BLOCK, PEER_HEADS, PEER_TOPK * PEER_TOPK)
        fv, fi = lax.top_k(cand, PEER_TOPK)
        i1 = jnp.take_along_axis(si[:, :, 0], fi // PEER_TOPK, axis=-1)
        i2 = jnp.take_along_axis(si[:, :, 1], fi % PEER_TOPK, axis=-1)
        eid = (i1 * PEER_NKEYS + i2).reshape(TOK_BLOCK, PEER_HEADS * PEER_TOPK)
        g = jax.nn.softmax(fv, axis=-1).reshape(TOK_BLOCK, PEER_HEADS * PEER_TOPK)
        hid = jax.nn.gelu(jnp.einsum('td,ted->te', tb, u_tab[eid]).astype(jnp.float32), approximate=False)
        return jnp.einsum('te,ted->td', (g * hid).astype(tb.dtype), v_tab[eid])

    out = lax.map(blk, t.reshape(n, TOK_BLOCK, shp[-1])).reshape(n * TOK_BLOCK, shp[-1])[:T]
    return out.reshape(shp)

def _mixer_inputs(x, c, pos, w_ada, b_ada, norm1_g, w_in):
    ada = (jax.nn.silu(c) @ w_ada + b_ada)[:, None, :]
    mods = jnp.split(ada, N_ADA, axis=-1)
    h = _rmsnorm(x, norm1_g) * (1.0 + mods[1]) + mods[0]
    z = h @ w_in
    a, gt, q, k, v = jnp.split(z, [CONV_CH, 2 * CONV_CH, 2 * CONV_CH + ATT_W, 2 * CONV_CH + 2 * ATT_W], axis=-1)
    glu = a * jax.nn.sigmoid(gt)

    def heads(t):
        return t.reshape(*t.shape[:-1], N_HEADS, HEAD_DIM)

    return mods, glu, _rope(heads(q), pos), _rope(heads(k), pos), heads(v)

def _finish(x, mods, conv_raw, attn, conv_ln_g, conv_ln_b, attn_out_g, w_out,
            norm2_g, peer_wq, peer_keys, peer_u, peer_v):
    conv_y = _conv_tail(conv_raw, conv_ln_g, conv_ln_b)
    a = _rmsnorm(attn, attn_out_g)
    a = a.reshape(*a.shape[:-2], ATT_W)
    mix = jnp.concatenate([conv_y, a], axis=-1) @ w_out
    x = x + (1.0 + mods[2]) * mix
    h = _rmsnorm(x, norm2_g) * (1.0 + mods[4]) + mods[3]
    return x + (1.0 + mods[5]) * _peer(h, peer_wq, peer_keys, peer_u, peer_v)

def setup_inputs(seed: int = 0) -> dict:
    key = jax.random.key(seed)
    ks = jax.random.split(key, 24)

    def nrm(k, shape, scale):
        return jax.random.normal(k, shape, jnp.float32) * scale

    lw = min(WIN_MAX, PAST_LEN)
    return {
        'x_prompt': nrm(ks[0], (BATCH, SEQ, D_MODEL), 1.0),
        'x_sample': nrm(ks[1], (DEC_BATCH, DEC_SEQ, D_MODEL), 1.0),
        'cache_k': nrm(ks[2], (DEPTH, DEC_BATCH, lw, N_HEADS, HEAD_DIM), 1.0),
        'cache_v': nrm(ks[3], (DEPTH, DEC_BATCH, lw, N_HEADS, HEAD_DIM), 1.0),
        'state_conv': nrm(ks[4], (DEPTH, DEC_BATCH, CONV_W - 1, CONV_CH), 0.5),
        'c_prompt': nrm(ks[5], (BATCH, D_MODEL), 1.0),
        'c_sample': nrm(ks[6], (DEC_BATCH, D_MODEL), 1.0),
        'w_ada': nrm(ks[7], (DEPTH, D_MODEL, N_ADA * D_MODEL), 0.1 * D_MODEL ** -0.5),
        'b_ada': nrm(ks[8], (DEPTH, N_ADA * D_MODEL), 0.01),
        'norm1_g': 1.0 + nrm(ks[9], (DEPTH, D_MODEL), 0.02),
        'w_in': nrm(ks[10], (DEPTH, D_MODEL, IN_COLS), D_MODEL ** -0.5),
        'conv_w': nrm(ks[11], (DEPTH, CONV_W, CONV_CH), CONV_W ** -0.5),
        'conv_b': nrm(ks[12], (DEPTH, CONV_CH), 0.01),
        'conv_ln_g': 1.0 + nrm(ks[13], (DEPTH, CONV_CH), 0.02),
        'conv_ln_b': nrm(ks[14], (DEPTH, CONV_CH), 0.01),
        'attn_out_g': 1.0 + nrm(ks[15], (DEPTH, N_HEADS, HEAD_DIM), 0.02),
        'w_out': nrm(ks[16], (DEPTH, D_MIX, D_MODEL), D_MIX ** -0.5),
        'norm2_g': 1.0 + nrm(ks[17], (DEPTH, D_MODEL), 0.02),
        'peer_wq': nrm(ks[18], (DEPTH, D_MODEL, PEER_HEADS * 2 * PEER_DK), D_MODEL ** -0.5),
        'peer_keys': nrm(ks[19], (DEPTH, PEER_HEADS, 2, PEER_NKEYS, PEER_DK), PEER_DK ** -0.5),
        'peer_u': nrm(ks[20], (DEPTH, N_EXPERTS, D_MODEL), D_MODEL ** -0.5),
        'peer_v': nrm(ks[21], (DEPTH, N_EXPERTS, D_MODEL), PEER_HEADS ** -0.5),
        'final_g': 1.0 + nrm(ks[22], (D_MODEL,), 0.02),
    }

def reference(x_prompt, x_sample, cache_k, cache_v, state_conv, c_prompt, c_sample,
              w_ada, b_ada, norm1_g, w_in, conv_w, conv_b, conv_ln_g, conv_ln_b, attn_out_g, w_out,
              norm2_g, peer_wq, peer_keys, peer_u, peer_v, final_g):
    xp, xs = x_prompt, x_sample
    S = x_prompt.shape[1]
    pos_p = jnp.arange(S)
    pos_s = PAST_LEN + jnp.arange(x_sample.shape[1])
    keep = min(WIN_MAX, S)
    pk, pv, pc, sk, sv, sc = [], [], [], [], [], []
    for l in range(DEPTH):
        mods, glu, q, k, v = _mixer_inputs(xp, c_prompt, pos_p, w_ada[l], b_ada[l], norm1_g[l], w_in[l])
        conv_raw = _dwconv(jnp.pad(glu, ((0, 0), (CONV_W - 1, 0), (0, 0))), conv_w[l], conv_b[l])
        attn = _merge([_dilated_prompt(q, k, v, w, d) for w, d in zip(WINDOWS, DILATIONS)])
        xp = _finish(xp, mods, conv_raw, attn, conv_ln_g[l], conv_ln_b[l], attn_out_g[l], w_out[l],
                     norm2_g[l], peer_wq[l], peer_keys[l], peer_u[l], peer_v[l])
        pk.append(k[:, S - keep:])
        pv.append(v[:, S - keep:])
        pc.append(glu[:, S - (CONV_W - 1):])
        mods, glu, q, k, v = _mixer_inputs(xs, c_sample, pos_s, w_ada[l], b_ada[l], norm1_g[l], w_in[l])
        hist = jnp.concatenate([state_conv[l].astype(glu.dtype), glu], axis=1)
        conv_raw = _dwconv(hist, conv_w[l], conv_b[l])
        attn = _merge([_dilated_sample(q, k, v, cache_k[l], cache_v[l], w, d) for w, d in zip(WINDOWS, DILATIONS)])
        xs = _finish(xs, mods, conv_raw, attn, conv_ln_g[l], conv_ln_b[l], attn_out_g[l], w_out[l],
                     norm2_g[l], peer_wq[l], peer_keys[l], peer_u[l], peer_v[l])
        sk.append(k)
        sv.append(v)
        sc.append(hist[:, hist.shape[1] - (CONV_W - 1):])
    y_prompt = _rmsnorm(xp, final_g)
    y_sample = _rmsnorm(xs, final_g)
    return (y_prompt, y_sample, jnp.stack(pk), jnp.stack(pv), jnp.stack(pc),
            jnp.stack(sk), jnp.stack(sv), jnp.stack(sc))


_drawn_inputs = setup_inputs


def setup_inputs(seed=0):
    import zlib

    import numpy as np

    out = dict(_drawn_inputs(seed))
    spreads = {}
    factors = {'conv_b': 3.907,
     'conv_ln_g': 25.892,
     'conv_ln_b': 52.957,
     'final_g': 22.194,
     'attn_out_g': 18.397,
     'norm2_g': 14.639}
    for name, (base, spread) in spreads.items():
        noise = np.random.default_rng([zlib.crc32(name.encode()), seed]).standard_normal(out[name].shape)
        drawn = base * np.exp(spread * noise) if base else spread * noise
        out[name] = jnp.asarray(drawn.astype(out[name].dtype))
    for name, factor in factors.items():
        out[name] = (out[name] * factor).astype(out[name].dtype)
    return out
```

```python
from contextlib import ExitStack

import concourse.bass as bass
from concourse import mybir

F32 = mybir.dt.float32
F32R = mybir.dt.float32r
U32 = mybir.dt.uint32
ALU = mybir.AluOpType
ACT = mybir.ActivationFunctionType
AX_X = mybir.AxisListType.X

P = 128
D = 2048
KC = D // P
SEQ = 256
DB, DS = 8, 4
TS = DB * DS
T = SEQ + TS
NC = 1 + DB
PAST = 256
CONV_W = 31
HIST = CONV_W - 1
CT = 8
GW_P = HIST + SEQ
GW_S = HIST + DS
GW = GW_P + DB * GW_S
H = 8
E = 128
ROT = 32
SCALE = float(E) ** -0.5
EPS = 1e-6
N_ADA = 6
TOPK = 16
NK = 128
HALF = NK // 2
NEG = -3.0e38
UNIT = 1024
TOK_TILES = ((0, 128), (128, 128), (256, 32))

ADA_TILES = N_ADA * D // 512
ADA_FIRST = 8
ADA_MIXER = 12
Q_GLU = 2 * ADA_FIRST
Q_QKV = Q_GLU + CT
Q_ADA_MIXER = Q_QKV + 12
Q_OUT = Q_ADA_MIXER + 2 * ADA_MIXER
Q_ADA_LAST = Q_OUT + KC // 2
Q_WQ = Q_ADA_LAST + 2 * (ADA_TILES - ADA_FIRST - ADA_MIXER)
Q_PEER = Q_WQ + KC // 2
PAIRS = HALF // 2
KV_PAIRS = 3 * H // 2
G_GROUPS = T // 8

JOBS = [(0, 0), (1, 0), (2, 0), (3, 0), (0, 1), (4, 0), (5, 0), (6, 0), (7, 0), (1, 1)]
ADA_BESIDE = (1, 1, 1, 2, 1, 1, 1, 1, 2, 1)
JOB_COLS = (((0, 128, 0), (128, 384, 1)), ((0, 288, 0),))

V_G1, V_G2, V_GF = 0, 16, 32
V_LNG, V_LNB, V_CB, V_AG = 48, 56, 64, 72
V_CW = 80
V_ADA = V_CW + CT * CONV_W
V_N = V_ADA + N_ADA * KC

K_ID, K_ONE, K_IOTA, K_SEL, K_IO16 = 0, 128, 256, 384, 394
K_EPS = 410
K_N = 411
M_CP, M_NP, M_CS, M_NS, M_RC, M_RS, M_PERM = 0, 384, 768, 1056, 1344, 1632, 1920
M_N = M_PERM + P


def layer_kernel(nc, xT_d, cT_d, glu0_d, w_ada_d, w_in_d, w_out_d, w_q_d, keys_d, u_d, v_d, ck_d, cv_d,
                 vecs_d, consts_d, masks_d, y_d, k_out, v_out, convp_out, convs_out):
    spill_d = nc.dram_tensor("x1_spill", [P, KC * T], F32).ap()

    base = [16512]

    def at(name, shape, dt, offset):
        return nc.alloc_sbuf_tensor_at(name, shape, dt, offset=offset)

    def sb(name, shape, dt=F32):
        n = 4
        for s in shape[1:]:
            n *= s
        t = at(name, shape, dt, base[0])
        base[0] += (n + 63) // 64 * 64
        return t

    raw = [sb(f"raw{s}", [P, UNIT]) for s in range(4)]
    hi = [sb(f"hi{s}", [P, UNIT], F32R) for s in range(4)]
    lo = [sb(f"lo{s}", [P, UNIT], F32R) for s in range(4)]
    act_hi_at = base[0]
    act_hi = sb("act_hi", [P, KC, T], F32R)
    act_lo = sb("act_lo", [P, KC, T], F32R)
    x_at = base[0]
    xT = sb("xT", [P, KC, T])
    mods_at = base[0]
    mods = sb("mods", [P, N_ADA * KC, NC])
    vecs = sb("vecs", [P, V_N])
    consts = sb("consts", [P, K_N])
    rs = sb("rs", [P, T])
    m_a1 = sb("m_a1", [P, KC, NC])
    m_a2 = sb("m_a2", [P, KC, NC])
    m_g2 = sb("m_g2", [P, KC, NC])
    m_g5 = sb("m_g5", [P, KC, NC])
    tmp_s = sb("tmp_s", [P, 2, TS])
    small = sb("small", [P, 64])
    cT = sb("cT", [P, KC, NC])
    c_split = sb("c_split", [P, KC, 2 * NC], F32R)
    ada_row = [sb(f"ada_row{b}", [2 * NC, 512]) for b in range(2)]
    zone = base[0]

    glu = at("glu", [P, CT, GW], F32, zone)
    cache = [at(f"cache{s}", [P, UNIT], F32, zone + 4096 * s) for s in range(4)]
    conv_y = at("conv_y", [P, CT, T], F32, zone + 17920)
    qkvT = at("qkvT", [P, 3 * H, T], F32, zone + 27136)
    v_tok = at("v_tok", [P, 3, H * E], F32, zone + 54784)
    sc = [at(f"sc{b}", [P, 384], F32, zone + 67072 + 1536 * b) for b in range(2)]
    ex = [at(f"ex{b}", [P, 384], F32, zone + 70144 + 1536 * b) for b in range(2)]
    pT = at("pT", [P, 384], F32, zone + 73216)
    sT = at("sT", [P, 384], F32, zone + 74752)
    prod = at("prod", [P, TS, CONV_W], F32, zone + 67072)
    sig = at("sig", [P, T], F32, zone + 71040)
    masks = at("masks", [P, M_N], F32, zone + 76288)
    keysT = at("keysT", [P, 2 * H, NK], F32, zone + 78592)
    r_t = at("r_t", [ROT, 4, T], F32, zone + 54784)
    sq_head = at("sq_head", [P, H, T], F32, zone + 27136)
    sq = at("sq", [P, KC, T], F32, act_hi_at)
    sq_ln = at("sq_ln", [P, CT, T], F32, act_hi_at)
    sq_at = at("sq_at", [P, H, T], F32, act_hi_at + 18432 + 9216)
    hF = at("hF", [P, KC, T], F32, zone + 27136)
    oT = qkvT[:, 2 * H:3 * H, :]
    qpT = at("qpT", [P, KC, T], F32, zone)
    s_tm = at("s_tm", [P, 2 * H, NK], F32, zone + 18432)
    s_work = at("s_work", [P, 2 * H, NK], F32, zone + 45568)
    cand = at("cand", [P, H, 256], F32, zone + 53760)
    c_work = at("c_work", [P, H, 256], F32, zone + 61952)
    oh = at("oh", [P, H * TOPK, TOPK], F32, zone + 26624)
    sv = at("sv", [P, 2 * H, TOPK], F32, zone + 70144)
    si_u = at("si_u", [P, 2 * H, TOPK], U32, zone + 71168)
    si_f = at("si_f", [P, 2 * H, TOPK], F32, zone + 72192)
    fv = at("fv", [P, H, TOPK], F32, zone + 73216)
    fi_u = at("fi_u", [P, H * TOPK], U32, zone + 73728)
    f_au = at("f_au", [P, H * TOPK], U32, zone + 74240)
    f_bu = at("f_bu", [P, H * TOPK], U32, zone + 74752)
    f_a = at("f_a", [P, H * TOPK], F32, zone + 75264)
    f_b = at("f_b", [P, H * TOPK], F32, zone + 75776)
    picks = at("picks", [P, 3, H * TOPK], F32, zone + 76288)
    g_exp = at("g_exp", [P, H, TOPK], F32, zone + 77824)
    G = at("G", [P, T, HALF], F32, zone)
    w_hi = [at(f"w_hi{b}", [P, 2, T], F32R, zone + 73728 + 2304 * b) for b in range(2)]
    w_lo = [at(f"w_lo{b}", [P, 2, T], F32R, zone + 78336 + 2304 * b) for b in range(2)]
    w_f = at("w_f", [P, 2, T], F32, zone + 82944)
    gl = [at(f"gl{b}", [P, 2, T], F32, zone + 85248 + 2304 * b) for b in range(2)]
    one1 = [at(f"one1_{b}", [P, 8, NK], F32, zone + 73728 + 4096 * b) for b in range(2)]
    one2 = [at(f"one2_{b}", [P, 8, HALF], F32, zone + 81920 + 2048 * b) for b in range(2)]
    i1T = at("i1T", [P, T], F32, mods_at)
    i2T = at("i2T", [P, T], F32, mods_at + 4 * T)
    gT = at("gT", [P, T], F32, mods_at + 8 * T)
    acc = at("acc", [P, KC, T], F32, x_at)
    x2 = at("x2", [P, KC, T], F32, zone)
    fin = at("fin", [P, KC, T], F32, zone + 18432)
    assert zone + 89856 <= nc.sbuf_usable_end

    ident, ones = consts[:, K_ID:K_ID + P], consts[:, K_ONE:K_ONE + P]
    iota = consts[:, K_IOTA:K_IOTA + NK]

    with ExitStack() as ctx:
        def sem(name):
            return ctx.enter_context(nc.semaphore(name))

        zb = ctx.enter_context(nc.psum_tensor("zb", [P, 4, 512], F32))
        vb = ctx.enter_context(nc.psum_tensor("vb", [P, 4, 512], F32))

        raw_in = [sem(f"raw_in{s}") for s in range(4)]
        cache_in = [sem(f"cache_in{s}") for s in range(4)]
        hi_ready = sem("hi_ready")
        lo_ready = sem("lo_ready")
        unit_used = sem("unit_used")
        z_free = sem("z_free")
        c_in = sem("c_in")
        consts_in = sem("consts_in")
        vecs_in = sem("vecs_in")
        x_in = sem("x_in")
        glu0_in = sem("glu0_in")
        masks_in = sem("masks_in")
        keys_in = sem("keys_in")
        silu_done = sem("silu_done")
        c_ready = sem("c_ready")
        row_copied = sem("row_copied")
        row_turned = sem("row_turned")
        mods_ready = sem("mods_ready")
        sq_ready = sem("sq_ready")
        stat_ready = sem("stat_ready")
        root_ready = sem("root_ready")
        h_ready = sem("h_ready")
        h_hi = sem("h_hi")
        h_split = sem("h_split")
        sig_ready = sem("sig_ready")
        glu_ready = sem("glu_ready")
        z_half = sem("z_half")
        qkv_evac = sem("qkv_evac")
        rope_perm = sem("rope_perm")
        rope_step = sem("rope_step")
        rope_done = sem("rope_done")
        conv_step = sem("conv_step")
        conv_done = sem("conv_done")
        prod_step = sem("prod_step")
        conv_s_done = sem("conv_s_done")
        hist_out = sem("hist_out")
        v_out_done = sem("v_out_done")
        k_out_done = sem("k_out_done")
        ln_sum = sem("ln_sum")
        ln_centred = sem("ln_centred")
        ln_sq = sem("ln_sq")
        ln_sqsum = sem("ln_sqsum")
        ln_z = sem("ln_z")
        ln_out = sem("ln_out")
        v_turned = sem("v_turned")
        v_copied = sem("v_copied")
        cache_used = sem("cache_used")
        score_ready = sem("score_ready")
        masked = sem("masked")
        neg_max = sem("neg_max")
        exp_done = sem("exp_done")
        prob_ready = sem("prob_ready")
        prob_turned = sem("prob_turned")
        pT_ready = sem("pT_ready")
        sT_ready = sem("sT_ready")
        sT_copied = sem("sT_copied")
        o_ready = sem("o_ready")
        o_copied = sem("o_copied")
        o_sq = sem("o_sq")
        o_sum = sem("o_sum")
        o_normed = sem("o_normed")
        x1_step = sem("x1_step")
        x1_tile = sem("x1_tile")
        qp_copied = sem("qp_copied")
        s_ready = sem("s_ready")
        s_copied = sem("s_copied")
        s_read = sem("s_read")
        gate_in = sem("gate_in")
        gate_out = sem("gate_out")
        picks_ready = sem("picks_ready")
        picks_turned = sem("picks_turned")
        picks_copied = sem("picks_copied")
        spilled = sem("spilled")
        one_ready = sem("one_ready")
        g_ready = sem("g_ready")
        g_copied = sem("g_copied")
        acc_zero = sem("acc_zero")
        gelu_done = sem("gelu_done")
        w_mid = sem("w_mid")
        w_ready = sem("w_ready")
        vb_ready = sem("vb_ready")
        vb_free = sem("vb_free")
        x1_in = sem("x1_in")
        x2_ready = sem("x2_ready")
        y_ready = sem("y_ready")
        y_out = sem("y_out")
        dve_step = sem("dve_step")
        block = ctx.enter_context(nc.Block())

        def over(ap, n):
            return ap.unsqueeze(1).to_broadcast([ap.shape[0], n, ap.shape[1]])

        def per_token(ap, n, width):
            return ap.to_broadcast([P, n, width])

        def load(sp, q, s, dst_src):
            sp.wait_ge(lo_ready, 4 * q + s + 1)
            sp.dma_start(raw[s][:, :] if dst_src[0] is None else dst_src[0], dst_src[1]).then_inc(raw_in[s], 16)

        def split_hi(act, q, s):
            act.wait_ge(raw_in[s], 16 * q + 16)
            act.wait_ge(unit_used, 4 * q + s + 1)
            act.activation(hi[s][:, :], raw[s][:, :], ACT.Copy).then_inc(hi_ready, 1)

        def split_lo(dve, q, s):
            dve.wait_ge(hi_ready, 4 * q + s + 1)
            dve.tensor_tensor(lo[s][:, :], raw[s][:, :], hi[s][:, :].bitcast(F32), ALU.subtract) \
                .then_inc(lo_ready, 1)

        def project(pe, q, parity, tile=None):
            for s in range(4):
                bank = 2 * parity + s // 2
                if s % 2 == 0 and tile is not None:
                    pe.wait_ge(z_free, tile + s // 2 + 1)
                pe.wait_ge(lo_ready, 4 * q + s + 5)
                for j in range(8):
                    k = 8 * (s % 2) + j
                    w_h, w_l = hi[s][:, j * P:(j + 1) * P], lo[s][:, j * P:(j + 1) * P]
                    pe.matmul(zb[:, bank, 0:T], w_h, act_hi[:, k, :], start=(k == 0), stop=False)
                    pe.matmul(zb[:, bank, 0:T], w_h, act_lo[:, k, :], start=False, stop=False)
                    last = pe.matmul(zb[:, bank, 0:T], w_l, act_hi[:, k, :], start=False, stop=(k == KC - 1))
                last.then_inc(unit_used, 1)

        @block.sync
        def _(sp):
            def load_ada(q0, n0, count):
                with sp.Fori(0, count) as n:
                    for k in range(8):
                        load(sp, q0 + 2 * n + k // 4, k % 4, (None, w_ada_d[n + n0, k]))

            load_ada(0, 0, ADA_FIRST)
            with sp.Fori(0, CT) as j:
                for s in range(4):
                    load(sp, Q_GLU + j, s, (None, w_in_d[2 * j + s // 2][:, UNIT * (s % 2):UNIT * (s % 2 + 1)]))
            with sp.Fori(0, 12) as j:
                for s in range(4):
                    load(sp, Q_QKV + j, s,
                         (None, w_in_d[2 * CT + 2 * j + s // 2][:, UNIT * (s % 2):UNIT * (s % 2 + 1)]))
            def load_proj(q0, w_d):
                with sp.Fori(0, KC // 2) as j:
                    for s in range(4):
                        load(sp, q0 + j, s, (None, w_d[2 * j + s // 2][:, UNIT * (s % 2):UNIT * (s % 2 + 1)]))

            load_ada(Q_ADA_MIXER, ADA_FIRST, ADA_MIXER)
            load_proj(Q_OUT, w_out_d)
            load_ada(Q_ADA_LAST, ADA_FIRST + ADA_MIXER, ADA_TILES - ADA_FIRST - ADA_MIXER)
            load_proj(Q_WQ, w_q_d)

            def load_u(half, pair, q):
                for s in range(4):
                    i2 = HALF * half + 2 * pair + s // 2
                    load(sp, q, s, (None, u_d[i2][:, UNIT * (s % 2):UNIT * (s % 2 + 1)]))

            def load_v(half, pair, q):
                for s in range(4):
                    dst = raw[s][:, :].rearrange("p (a d) -> p a d", a=2)
                    load(sp, q, s, (dst, v_d[:, bass.ds(HALF * half + 2 * pair, 2), 512 * s:512 * (s + 1)]))

            for half in range(2):
                q0 = Q_PEER + HALF * half
                load_u(half, 0, q0)
                with sp.Fori(0, PAIRS - 1) as i:
                    load_u(half, i + 1, q0 + 2 * i + 1)
                    load_v(half, i, q0 + 2 * i + 2)
                load_v(half, PAIRS - 1, q0 + HALF - 1)

        @block.gpsimd
        def _(pool):
            pool.wait_ge(vecs_in, 16)
            pool.wait_ge(mods_ready, ADA_FIRST + 2)
            with pool.Fori(0, CT) as ct:
                pool.wait_ge(glu_ready, ct + 2)
                row = glu[:, bass.ds(ct, 1), GW_P:GW]
                window = bass.AP(row.tensor, row.offset, [list(row.ap[0]), [GW_S, DB], [1, DS], [1, CONV_W]])
                taps = vecs[:, bass.ds(V_CW + CONV_W * ct, CONV_W)]
                taps = bass.AP(taps.tensor, taps.offset, [list(taps.ap[0]), [0, DB], [0, DS], [1, CONV_W]])
                out = prod[:, :, :].rearrange("p (b s) w -> p b s w", b=DB)
                pool.tensor_tensor(out, window, taps, ALU.mult).then_inc(prod_step, 1)
                for k, n in enumerate((16, 8, 4, 2)):
                    pool.wait_ge(prod_step, 5 * ct + k + 1)
                    m = min(n, CONV_W - n)
                    pool.tensor_tensor(prod[:, :, 0:m], prod[:, :, 0:m], prod[:, :, n:n + m], ALU.add) \
                        .then_inc(prod_step, 1)
                pool.wait_ge(prod_step, 5 * ct + 5)
                pool.tensor_tensor(conv_y[:, bass.ds(ct, 1), SEQ:T].rearrange("p c t -> p t c"), prod[:, :, 0:1],
                                   prod[:, :, 1:2], ALU.add).then_inc(conv_s_done, 1)
                pool.wait_ge(conv_s_done, ct + 1)
            pool.dma_start(convp_out, glu[:, :, SEQ:GW_P]).then_inc(hist_out, 16)
            for ct in range(CT):
                src = glu[:, ct, GW_P:GW].rearrange("p (b w) -> p b w", b=DB)[:, :, DS:GW_S]
                pool.dma_start(convs_out[:, ct], src).then_inc(hist_out, 16)
            pool.wait_ge(qkv_evac, KV_PAIRS)
            pool.dma_start(v_out, qkvT[:, 2 * H:3 * H, :]).then_inc(v_out_done, 16)
            pool.wait_ge(rope_done, 5)
            pool.dma_start(k_out, qkvT[:, H:2 * H, :]).then_inc(k_out_done, 16)

            pool.wait_ge(prob_ready, len(JOBS))
            pool.dma_start(keysT[:, :, :], keys_d).then_inc(keys_in, 16)

            pool.wait_ge(h_split, 3)
            pool.dma_start(spill_d, xT[:, :, :].rearrange("p k t -> p (k t)")).then_inc(spilled, 16)

            pool.wait_ge(w_ready, 2 * PAIRS + 2)
            pool.dma_start(x2[:, :, :].rearrange("p k t -> p (k t)"), spill_d).then_inc(x1_in, 16)
            for k in range(4):
                pool.wait_ge(y_ready, k + 1)
                pool.dma_start(y_d[:, 4 * k:4 * k + 4], fin[:, 4 * k:4 * k + 4, :]).then_inc(y_out, 16)
            pool.wait_ge(v_out_done, 16)
            pool.wait_ge(k_out_done, 16)
            pool.wait_ge(y_out, 16 * 4)

        @block.scalar
        def _(act):
            def quad_hi(q):
                for s in range(4):
                    split_hi(act, q, s)

            eps = consts[:, K_EPS:K_EPS + 1]

            def root(total, n, ready, k):
                act.wait_ge(ready, k)
                act.activation(rs[:, :], total, ACT.Sqrt, bias=eps, scale=1.0 / n).then_inc(root_ready, 1)

            for dst, src, arrived in ((cT[:, :, :], cT_d, c_in), (xT[:, :, :], xT_d, x_in),
                                      (consts[:, :], consts_d, consts_in), (vecs[:, :], vecs_d, vecs_in),
                                      (glu[:, :, :], glu0_d, glu0_in), (masks[:, :], masks_d, masks_in)):
                act.dma_start(dst, src).then_inc(arrived, 16)
            act.sem_inc(z_free, 4)
            act.sem_inc(row_copied, 2)
            act.sem_inc(g_copied, 2)
            act.sem_inc(gelu_done, 2)
            act.wait_ge(c_in, 16)
            act.activation(cT[:, :, :], cT[:, :, :], ACT.Silu).then_inc(silu_done, 1)
            act.wait_ge(x_in, 16)
            act.activation(sq[:, :, :], xT[:, :, :], ACT.Square).then_inc(sq_ready, 1)
            act.wait_ge(consts_in, 16)
            root(vb[:, 2, 0:T], D, stat_ready, 1)
            quad_hi(0)
            def ada_tile(q, n, b):
                quad_hi(q + 1)
                quad_hi(q + 2)
                act.wait_ge(row_turned, n + 1)
                act.activation(ada_row[b][:, :], zb[0:2 * NC, b, :], ACT.Copy).then_inc(row_copied, 1)

            with act.Fori(0, ADA_FIRST // 2) as m:
                for b in range(2):
                    ada_tile(2 * (2 * m + b), 2 * m + b, b)
            act.wait_ge(h_ready, 1)
            act.activation(act_hi[:, :, :], hF[:, :, :], ACT.Copy).then_inc(h_hi, 1)
            act.wait_ge(mods_ready, ADA_FIRST + 2)
            with act.Fori(0, CT // 2) as m:
                for b in range(2):
                    j = 2 * m + b
                    quad_hi(Q_GLU + 1 + j)
                    act.wait_ge(glu_ready, j + 1)
                    act.activation(sig[:, :], zb[:, 2 * b + 1, 0:T], ACT.Sigmoid).then_inc(sig_ready, 1)
            with act.Fori(0, 2) as m:
                for k in range(6):
                    j = 6 * m + k
                    quad_hi(Q_QKV + 1 + j)
                    pair = zb[:, 2 * (k % 2):2 * (k % 2) + 2, 0:T]
                    act.activation(qkvT[:, bass.ds(2 * j, 2), :], pair, ACT.Copy).then_inc(qkv_evac, 1)
            act.wait_ge(rope_done, 5)
            for g in range(6):
                n = TOK_TILES[g // 2][1]
                act.wait_ge(v_turned, g + 1)
                act.activation(v_tok[0:n, g // 2, 512 * (g % 2):512 * (g % 2) + 512], vb[0:n, g % 4, :], ACT.Copy) \
                    .then_inc(v_copied, 1)
            act.wait_ge(ln_centred, 1)
            act.activation(sq_ln[:, :, :], conv_y[:, :, :], ACT.Square).then_inc(ln_sq, 1)
            act.wait_ge(v_out_done, 16)

            def load_cache(first, last):
                for n in range(first, min(last, 32)):
                    if n >= 4:
                        act.wait_ge(cache_used, n - 3)
                    src = (ck_d, cv_d)[n // 8 % 2][4 * (n // 16) + n % 8 // 2, n % 2]
                    act.dma_start(cache[n % 4][:, :], src).then_inc(cache_in[n % 4], 16)

            def exps(n):
                g, sample = JOBS[n]
                if sample:
                    load_cache(16 * g + 4, 16 * g + 12)
                    act.wait_ge(sT_ready, g + 1)
                    act.activation(sT[:, 0:256], zb[:, 2, 0:256], ACT.Copy)
                    act.activation(sT[0:TS, 256:384], zb[0:TS, 2, 256:384], ACT.Copy).then_inc(sT_copied, 1)
                act.wait_ge(neg_max, n + 1)
                if n >= 2:
                    act.wait_ge(prob_turned, n - 1)
                for lo_c, hi_c, c in JOB_COLS[sample]:
                    last = act.activation(ex[n % 2][:, lo_c:hi_c], sc[n % 2][:, lo_c:hi_c], ACT.Exp,
                                          bias=small[:, 6 * n + c:6 * n + c + 1])
                last.then_inc(exp_done, 1)

            act.wait_ge(conv_done, 1)
            act.wait_ge(hist_out, 16 * (1 + CT))
            load_cache(0, 4)
            exps(0)
            root(zb[:, 1, 0:T], CT * P, ln_sqsum, 1)
            for n, (g, sample) in enumerate(JOBS):
                if n + 1 < len(JOBS):
                    exps(n + 1)
                for t in range(sum(ADA_BESIDE[:n]), sum(ADA_BESIDE[:n + 1])):
                    ada_tile(Q_ADA_MIXER + 2 * t, ADA_FIRST + t, t % 2)
                act.wait_ge(prob_turned, n + 1)
                if n:
                    act.wait_ge(o_ready, n)
                if sample:
                    act.activation(pT[:, 0:256], vb[:, 2, 0:256], ACT.Copy)
                    act.activation(pT[0:TS, 256:384], vb[0:TS, 2, 256:384], ACT.Copy).then_inc(pT_ready, 1)
                else:
                    act.activation(pT[:, :], vb[:, 2, 0:384], ACT.Copy).then_inc(pT_ready, 1)
                if sample:
                    load_cache(16 * g + 12, 16 * g + 20)
                act.wait_ge(o_ready, n + 1)
                if sample:
                    act.activation(oT[:, 4 * g:4 * g + 4, SEQ:T],
                                   vb[:, 3, 256:384].rearrange("p (h t) -> p h t", h=4), ACT.Copy) \
                        .then_inc(o_copied, 1)
                else:
                    act.activation(oT[:, g, 0:SEQ], vb[:, 3, 0:256], ACT.Copy).then_inc(o_copied, 1)
            act.wait_ge(o_copied, len(JOBS))
            act.activation(sq_at[:, :, :], oT, ACT.Square).then_inc(o_sq, 1)
            act.wait_ge(o_sum, 1)
            act.activation(sq_head[:, 0:4, :], zb[:, :, 0:T], ACT.Sqrt, bias=eps, scale=1.0 / E)
            act.activation(sq_head[:, 4:8, :], vb[:, :, 0:T], ACT.Sqrt, bias=eps, scale=1.0 / E) \
                .then_inc(root_ready, 1)
            act.wait_ge(ln_z, 1)
            for ct in range(CT):
                last = act.activation(conv_y[:, ct, :], conv_y[:, ct, :], ACT.Silu,
                                      bias=vecs[:, V_LNB + ct:V_LNB + ct + 1],
                                      scale=vecs[:, V_LNG + ct:V_LNG + ct + 1])
            last.then_inc(ln_out, 1)
            act.wait_ge(ln_out, 1)
            act.activation(act_hi[:, 0:CT, :], conv_y[:, :, :], ACT.Copy).then_inc(h_hi, 1)
            act.wait_ge(o_normed, 1)
            act.activation(act_hi[:, CT:KC, :], oT, ACT.Copy).then_inc(h_hi, 1)
            with act.Fori(0, KC // 2) as j:
                quad_hi(Q_OUT + 1 + j)
            act.wait_ge(x1_tile, KC // 2 + 1)
            act.activation(sq[:, :, :], xT[:, :, :], ACT.Square).then_inc(sq_ready, 1)
            root(vb[:, 0, 0:T], D, stat_ready, 2)
            with act.Fori(0, (ADA_TILES - ADA_FIRST - ADA_MIXER) // 2) as m:
                for b in range(2):
                    ada_tile(Q_ADA_LAST + 2 * (2 * m + b), ADA_FIRST + ADA_MIXER + 2 * m + b, b)
            act.wait_ge(h_ready, 2)
            act.activation(act_hi[:, :, :], hF[:, :, :], ACT.Copy).then_inc(h_hi, 1)
            act.wait_ge(h_split, 3)
            with act.Fori(0, KC // 4) as m:
                for b in range(2):
                    quad_hi(Q_WQ + 1 + 2 * m + b)
                    act.activation(qpT[:, bass.ds(4 * m + 2 * b, 2), :], zb[:, 2 * b:2 * b + 2, 0:T], ACT.Copy) \
                        .then_inc(qp_copied, 1)
            def score_copy(tt):
                n = TOK_TILES[tt][1]
                act.wait_ge(s_ready, tt + 1)
                if tt:
                    act.wait_ge(s_read, tt)
                act.activation(s_tm[0:n, :, :].rearrange("p (b k) d -> p b (k d)", b=4), vb[0:n, :, :], ACT.Copy) \
                    .then_inc(s_copied, 1)

            def gate_exp(tt):
                n = TOK_TILES[tt][1]
                act.wait_ge(gate_in, tt + 1)
                act.activation(g_exp[0:n, :, :], g_exp[0:n, :, :], ACT.Exp).then_inc(gate_out, 1)

            score_copy(0)
            for tt, (t0, n) in enumerate(TOK_TILES):
                gate_exp(tt)
                if tt + 1 < 3:
                    score_copy(tt + 1)
                act.wait_ge(picks_turned, tt + 1)
                for c, dst in enumerate((i1T, i2T, gT)):
                    act.activation(dst[:, t0:t0 + n], zb[:, tt, c * P:c * P + n], ACT.Copy) \
                        .then_inc(picks_copied, 1)

            for half in range(2):
                q0, p0 = Q_PEER + HALF * half, PAIRS * half
                with act.Fori(0, T // 16) as i:
                    for b in range(2):
                        g = 2 * i + b
                        act.wait_ge(g_ready, G_GROUPS * half + g + 3)
                        act.activation(G[:, bass.ds(8 * g, 8), :], vb[:, b, :].rearrange("p (t k) -> p t k", t=8),
                                       ACT.Copy).then_inc(g_copied, 1)

                def gelu(pair, b):
                    act.wait_ge(w_ready, p0 + pair + 1)
                    act.activation(gl[b][:, :, :], zb[:, 2 * b:2 * b + 2, 0:T], ACT.Gelu).then_inc(gelu_done, 1)

                def body(i, b):
                    quad_hi(q0 + 2 * i + 2)
                    gelu(i + 1, (b + 1) % 2)
                    quad_hi(q0 + 2 * i + 3)

                quad_hi(q0 + 1)
                gelu(0, 0)
                with act.Fori(0, (PAIRS - 2) // 2) as m:
                    body(2 * m, 0)
                    body(2 * m + 1, 1)
                body(PAIRS - 2, 0)
                if half == 0:
                    quad_hi(q0 + HALF)
            act.wait_ge(x2_ready, 1)
            act.activation(sq[:, :, :], x2[:, :, :], ACT.Square).then_inc(sq_ready, 1)
            root(zb[:, 0, 0:T], D, stat_ready, 3)

        @block.tensor
        def _(pe):
            pe.sem_inc(unit_used, 4)
            pe.sem_inc(row_turned, 2)
            pe.sem_inc(g_ready, 2)

            def channel_sum(out, src, chunks, done):
                for k in range(chunks):
                    last = pe.matmul(out, ones, src[:, k, :], start=(k == 0), stop=(k == chunks - 1))
                last.then_inc(done, 1)

            pe.wait_ge(consts_in, 16)
            pe.wait_ge(sq_ready, 1)
            channel_sum(vb[:, 2, 0:T], sq, KC, stat_ready)
            pe.wait_ge(c_ready, 2)
            sel = consts[0:2 * NC, K_SEL:K_SEL + NC]

            def ada_tile(q, n, b):
                pe.wait_ge(row_copied, n + 1)
                for k in range(8):
                    s = k % 4
                    pe.wait_ge(lo_ready, 4 * q + k + 5)
                    for j in range(2):
                        first, final = k == 0 and j == 0, k == 7 and j == 1
                        c = c_split[:, 2 * k + j, :]
                        pe.matmul(zb[0:2 * NC, b, :], c, hi[s][:, 512 * j:512 * j + 512], start=first, stop=False)
                        last = pe.matmul(zb[0:2 * NC, b, :], c, lo[s][:, 512 * j:512 * j + 512],
                                         start=False, stop=final)
                    last.then_inc(unit_used, 1)
                pe.wait_ge(row_copied, n + 3)
                pe.wait_ge(mods_ready, n + 1)
                for c in range(4):
                    at_c = 64 * b + NC * c
                    last = pe.matmul(zb[:, 3, at_c:at_c + NC], ada_row[b][:, c * P:(c + 1) * P], sel,
                                     start=True, stop=True)
                last.then_inc(row_turned, 1)

            with pe.Fori(0, ADA_FIRST // 2) as m:
                for b in range(2):
                    ada_tile(2 * (2 * m + b), 2 * m + b, b)

            pe.wait_ge(h_split, 1)
            with pe.Fori(0, CT // 2) as m:
                for b in range(2):
                    project(pe, Q_GLU + 2 * m + b, b, 2 * (2 * m + b))
            with pe.Fori(0, 6) as m:
                for b in range(2):
                    project(pe, Q_QKV + 2 * m + b, b, 2 * CT + 2 * (2 * m + b))

            pe.wait_ge(masks_in, 16)
            with pe.Fori(0, 4) as i:
                pe.wait_ge(qkv_evac, 2 * i + 2)
                pe.wait_ge(rope_done, i + 1)
                for t in range(4):
                    last = pe.matmul(vb[:, t, 0:T], masks[0:ROT, M_PERM:M_PERM + P],
                                     qkvT[0:ROT, 4 * i + t, :], start=True, stop=True)
                last.then_inc(rope_perm, 1)
            pe.wait_ge(qkv_evac, KV_PAIRS)
            pe.wait_ge(rope_done, 5)
            for g in range(6):
                t0, n = TOK_TILES[g // 2]
                if g >= 4:
                    pe.wait_ge(v_copied, g - 3)
                for h in range(4):
                    last = pe.transpose(vb[0:n, g % 4, P * h:P * h + P],
                                        qkvT[:, 2 * H + 4 * (g % 2) + h, t0:t0 + n], ident)
                last.then_inc(v_turned, 1)
            pe.wait_ge(conv_done, 1)
            channel_sum(zb[:, 0, 0:T], conv_y, CT, ln_sum)
            pe.wait_ge(v_copied, 6)

            def scores(n):
                g, sample = JOBS[n]
                if not sample:
                    if n >= 2:
                        pe.wait_ge(masked, n - 1)
                    q, k = qkvT[:, g, :], qkvT[:, H + g, :]
                    pe.matmul(vb[:, n % 2, 0:128], q[:, 0:128], k[:, 0:128], start=True, stop=True)
                    pe.matmul(vb[:, n % 2, 128:384], q[:, 128:256], k[:, 0:256], start=True, stop=True) \
                        .then_inc(score_ready, 1)
                    return
                if g:
                    pe.wait_ge(sT_copied, g)
                for hb in range(8):
                    u = 16 * g + hb
                    pe.wait_ge(cache_in[u % 4], 16 * (u // 4) + 16)
                    h, b0 = hb // 2, 4 * (hb % 2)
                    for b in range(4):
                        for c in range(2):
                            col = 128 * c + TS * h + DS * (b0 + b)
                            last = pe.matmul(zb[:, 2, col:col + DS], cache[u % 4][:, 256 * b + P * c:256 * b + P * c + P],
                                             qkvT[:, 4 * g + h, SEQ + DS * (b0 + b):SEQ + DS * (b0 + b) + DS],
                                             start=True, stop=True)
                    last.then_inc(cache_used, 1)
                for h in range(4):
                    last = pe.matmul(zb[0:TS, 2, 256 + TS * h:256 + TS * h + TS], qkvT[:, H + 4 * g + h, SEQ:T],
                                     qkvT[:, 4 * g + h, SEQ:T], start=True, stop=True)
                last.then_inc(sT_ready, 1)
                pe.wait_ge(sT_copied, g + 1)
                pe.wait_ge(masked, n - 1)
                pe.transpose(vb[:, n % 2, 0:128], sT[:, 0:128], ident)
                pe.transpose(vb[:, n % 2, 128:256], sT[:, 128:256], ident)
                pe.transpose(vb[:, n % 2, 256:288], sT[0:TS, 256:384], ident[0:TS, 0:TS]).then_inc(score_ready, 1)

            def turn(n):
                sample = JOBS[n][1]
                pe.wait_ge(prob_ready, n + 1)
                if n:
                    pe.wait_ge(pT_ready, n)
                pe.transpose(vb[:, 2, 0:128], ex[n % 2][:, 0:128], ident)
                pe.transpose(vb[:, 2, 128:256], ex[n % 2][:, 128:256], ident)
                if sample:
                    last = pe.transpose(vb[0:TS, 2, 256:384], ex[n % 2][:, 256:288], ident)
                else:
                    last = pe.transpose(vb[:, 2, 256:384], ex[n % 2][:, 256:384], ident)
                last.then_inc(prob_turned, 1)

            def mix_values(n):
                g, sample = JOBS[n]
                pe.wait_ge(pT_ready, n + 1)
                if n:
                    pe.wait_ge(o_copied, n)
                if not sample:
                    v = v_tok[:, :, P * g:P * g + P]
                    pe.matmul(vb[:, 3, 0:256], v[:, 0, :], pT[:, 0:256], start=True, stop=False)
                    pe.matmul(vb[:, 3, 128:256], v[:, 1, :], pT[:, 256:384], start=False, stop=True) \
                        .then_inc(o_ready, 1)
                    return
                for h in range(4):
                    out = 256 + TS * h
                    for bh in range(2):
                        u = 16 * g + 8 + 2 * h + bh
                        pe.wait_ge(cache_in[u % 4], 16 * (u // 4) + 16)
                        for b in range(4):
                            at_b = DS * (4 * bh + b)
                            for c in range(2):
                                col = 128 * c + TS * h + at_b
                                last = pe.matmul(vb[:, 3, out + at_b:out + at_b + DS],
                                                 cache[u % 4][:, 512 * c + P * b:512 * c + P * b + P],
                                                 pT[:, col:col + DS], start=(bh == 0 and b == 0 and c == 0),
                                                 stop=False)
                        last.then_inc(cache_used, 1)
                    last = pe.matmul(vb[:, 3, out:out + TS], v_tok[0:TS, 2, P * (4 * g + h):P * (4 * g + h) + P],
                                     pT[0:TS, 256 + TS * h:256 + TS * h + TS], start=False, stop=True)
                last.then_inc(o_ready, 1)

            scores(0)
            pe.wait_ge(ln_sq, 1)
            channel_sum(zb[:, 1, 0:T], sq_ln, CT, ln_sqsum)
            pe.wait_ge(root_ready, 2)
            for n in range(len(JOBS)):
                if n + 1 < len(JOBS):
                    scores(n + 1)
                for t in range(sum(ADA_BESIDE[:n]), sum(ADA_BESIDE[:n + 1])):
                    ada_tile(Q_ADA_MIXER + 2 * t, ADA_FIRST + t, t % 2)
                turn(n)
                mix_values(n)
            pe.wait_ge(o_sq, 1)
            pe.wait_ge(mods_ready, ADA_FIRST + ADA_MIXER + 2)
            for h in range(H):
                bank = (zb if h < 4 else vb)[:, h % 4, 0:T]
                last = pe.matmul(bank, ones, sq_at[:, h, :], start=True, stop=True)
            last.then_inc(o_sum, 1)

            pe.wait_ge(h_split, 2)
            with pe.Fori(0, KC // 4) as m:
                for b in range(2):
                    project(pe, Q_OUT + 2 * m + b, b, 2 * (CT + 12) + 2 * (2 * m + b))
            pe.wait_ge(sq_ready, 2)
            channel_sum(vb[:, 0, 0:T], sq, KC, stat_ready)
            with pe.Fori(0, (ADA_TILES - ADA_FIRST - ADA_MIXER) // 2) as m:
                for b in range(2):
                    ada_tile(Q_ADA_LAST + 2 * (2 * m + b), ADA_FIRST + ADA_MIXER + 2 * m + b, b)
            pe.wait_ge(h_split, 3)
            pe.wait_ge(mods_ready, ADA_TILES + 2)
            with pe.Fori(0, KC // 4) as m:
                for b in range(2):
                    project(pe, Q_WQ + 2 * m + b, b, 2 * (CT + 12 + KC // 2) + 2 * (2 * m + b))

            def key_scores(tt):
                t0, n = TOK_TILES[tt]
                if tt:
                    pe.wait_ge(s_copied, tt)
                for hp in range(2 * H):
                    last = pe.matmul(vb[0:n, hp // 4, P * (hp % 4):P * (hp % 4) + P], qpT[:, hp, t0:t0 + n],
                                     keysT[:, hp, :], start=True, stop=True)
                last.then_inc(s_ready, 1)

            pe.wait_ge(qp_copied, KC // 2)
            pe.wait_ge(keys_in, 16)
            key_scores(0)
            for tt, (t0, n) in enumerate(TOK_TILES):
                if tt + 1 < 3:
                    key_scores(tt + 1)
                pe.wait_ge(picks_ready, tt + 1)
                for c in range(3):
                    last = pe.transpose(zb[:, tt, c * P:c * P + n], picks[0:n, c, :], ident[0:n, 0:n])
                last.then_inc(picks_turned, 1)
            pe.wait_ge(picks_copied, 3 * 3)

            for half in range(2):
                q0, p0 = Q_PEER + HALF * half, PAIRS * half
                if half:
                    pe.wait_ge(vb_free, 16 * PAIRS + 4)
                with pe.Fori(0, T // 16) as i:
                    for b in range(2):
                        g = G_GROUPS * half + 2 * i + b
                        pe.wait_ge(g_copied, g + 1)
                        pe.wait_ge(one_ready, g + 1)
                        for t in range(8):
                            last = pe.matmul(vb[:, b, HALF * t:HALF * t + HALF], one1[b][:, t, :], one2[b][:, t, :],
                                             start=True, stop=True)
                        last.then_inc(g_ready, 1)

                def mix_experts(i, b, q):
                    pe.wait_ge(w_ready, p0 + i + 3)
                    for s in range(4):
                        pe.wait_ge(lo_ready, 4 * q + s + 5)
                        for d in range(4):
                            if d % 2 == 0:
                                pe.wait_ge(vb_free, 16 * (p0 + i) + 4 * s + d + 1)
                            for e in range(2):
                                v_h = hi[s][:, 512 * e + P * d:512 * e + P * d + P]
                                v_l = lo[s][:, 512 * e + P * d:512 * e + P * d + P]
                                pe.matmul(vb[:, d, 0:T], v_h, w_hi[b][:, e, :], start=(e == 0), stop=False)
                                pe.matmul(vb[:, d, 0:T], v_h, w_lo[b][:, e, :], start=False, stop=False)
                                last = pe.matmul(vb[:, d, 0:T], v_l, w_hi[b][:, e, :], start=False, stop=(e == 1))
                            if d == 1:
                                last.then_inc(vb_ready, 1)
                        last.then_inc(unit_used, 1)

                def body(i, b):
                    pe.wait_ge(gelu_done, p0 + i + 2)
                    project(pe, q0 + 2 * i + 1, (b + 1) % 2)
                    mix_experts(i, b, q0 + 2 * i + 2)

                pe.wait_ge(g_copied, G_GROUPS * (half + 1) + 2)
                pe.wait_ge(gelu_done, p0 + 1)
                project(pe, q0, 0)
                with pe.Fori(0, (PAIRS - 2) // 2) as m:
                    body(2 * m, 0)
                    body(2 * m + 1, 1)
                body(PAIRS - 2, 0)
                mix_experts(PAIRS - 1, 1, q0 + HALF - 1)
            pe.wait_ge(sq_ready, 3)
            channel_sum(zb[:, 0, 0:T], sq, KC, stat_ready)

        @block.vector
        def _(dve):
            steps = [0]

            def mark(ins):
                steps[0] += 1
                return ins.then_inc(dve_step, 1)

            def settle():
                dve.wait_ge(dve_step, steps[0])

            def quad_lo(q):
                for s in range(4):
                    split_lo(dve, q, s)

            def inverse_rms(k):
                dve.wait_ge(root_ready, k)
                mark(dve.reciprocal(rs[:, :], rs[:, :]))
                settle()

            def times_rms():
                mark(dve.tensor_tensor(hF[:, :, :], xT[:, :, :], over(rs[:, :], KC), ALU.mult))
                settle()

            def modulate(op, by):
                mark(dve.tensor_tensor(hF[:, :, 0:SEQ], hF[:, :, 0:SEQ], by[:, :, 0:1].to_broadcast([P, KC, SEQ]), op))
                view = hF[:, :, SEQ:T].rearrange("p k (b s) -> p k b s", b=DB)
                return dve.tensor_tensor(view, view, by[:, :, 1:NC].unsqueeze(3).to_broadcast([P, KC, DB, DS]), op)

            def part_lo(k0, k1, src):
                return dve.tensor_tensor(act_lo[:, k0:k1, :], src, act_hi[:, k0:k1, :].bitcast(F32), ALU.subtract)

            dve.sem_inc(lo_ready, 4)
            dve.sem_inc(mods_ready, 2)
            dve.sem_inc(glu_ready, 1)
            dve.sem_inc(rope_done, 1)
            dve.sem_inc(vb_free, 4)
            dve.sem_inc(w_ready, 2)
            dve.sem_inc(x1_tile, 1)
            dve.wait_ge(silu_done, 1)
            dve.tensor_copy(c_split[:, :, 0:NC], cT[:, :, :]).then_inc(c_ready, 1)
            dve.wait_ge(c_ready, 1)
            dve.tensor_tensor(c_split[:, :, NC:2 * NC], cT[:, :, :], c_split[:, :, 0:NC].bitcast(F32), ALU.subtract) \
                .then_inc(c_ready, 1)
            dve.wait_ge(x_in, 16)
            inverse_rms(1)
            times_rms()
            quad_lo(0)
            dve.wait_ge(vecs_in, 16)

            def ada_tile(q, n, b):
                quad_lo(q + 1)
                quad_lo(q + 2)
                dve.wait_ge(row_turned, n + 3)
                dve.tensor_tensor(mods[:, bass.ds(4 * n, 4), :],
                                  zb[:, 3, 64 * b:64 * b + 4 * NC].rearrange("p (c r) -> p c r", c=4),
                                  vecs[:, bass.ds(V_ADA + 4 * n, 4)].unsqueeze(2).to_broadcast([P, 4, NC]),
                                  ALU.add).then_inc(mods_ready, 1)

            with dve.Fori(0, ADA_FIRST // 2) as m:
                for b in range(2):
                    ada_tile(2 * (2 * m + b), 2 * m + b, b)
            dve.wait_ge(mods_ready, ADA_FIRST + 2)

            def mod(i):
                return mods[:, KC * i:KC * i + KC, :]

            def scale_rows(out, i, g):
                mark(dve.scalar_tensor_tensor(out[:, :, :], mod(i), 1.0,
                                              vecs[:, g:g + KC].unsqueeze(2).to_broadcast([P, KC, NC]),
                                              ALU.add, ALU.mult))

            def gate_rows(out, i):
                mark(dve.tensor_scalar(out[:, :, :], mod(i), 1.0, None, ALU.add))

            scale_rows(m_a1, 1, V_G1)
            settle()
            mark(modulate(ALU.mult, m_a1))
            settle()
            modulate(ALU.add, mod(0)).then_inc(h_ready, 1)
            dve.wait_ge(h_hi, 1)
            part_lo(0, KC, hF[:, :, :]).then_inc(h_split, 1)

            dve.wait_ge(glu0_in, 16)
            with dve.Fori(0, CT // 2) as m:
                for b in range(2):
                    j = 2 * m + b
                    quad_lo(Q_GLU + 1 + j)
                    dve.wait_ge(sig_ready, j + 1)
                    row = glu[:, bass.ds(j, 1), :]
                    dve.tensor_tensor(row[:, :, HIST:GW_P], zb[:, 2 * b:2 * b + 1, 0:SEQ],
                                      sig[:, 0:SEQ].unsqueeze(1), ALU.mult).then_inc(z_half, 1)
                    new = row[:, :, GW_P:GW].rearrange("p c (b w) -> p (c b) w", b=DB)[:, :, HIST:GW_S]
                    dve.tensor_tensor(new, zb[:, 2 * b, SEQ:T].rearrange("p (b s) -> p b s", b=DB),
                                      sig[:, SEQ:T].rearrange("p (b s) -> p b s", b=DB), ALU.mult) \
                        .then_inc(glu_ready, 1)
                    dve.wait_ge(glu_ready, j + 2)
                    dve.sem_inc(z_free, 2)

            dve.wait_ge(z_half, CT)
            with dve.Fori(0, 2) as m:
                for k in range(6):
                    j = 6 * m + k
                    quad_lo(Q_QKV + 1 + j)
                    dve.wait_ge(qkv_evac, j + 1)
                    dve.sem_inc(z_free, 2)
                    for n in range(21 * k, min(21 * k + 21, 4 * CONV_W)):
                        w, c = n % (2 * CONV_W) // 2, 2 * (n // (2 * CONV_W)) + n % 2
                        ct = 4 * m + c
                        out = conv_y[:, bass.ds(ct, 1), 0:SEQ]
                        window = glu[:, bass.ds(ct, 1), w:w + SEQ]
                        tap = vecs[:, bass.ds(V_CW + CONV_W * ct + w, 1)]
                        if w == 0:
                            dve.tensor_scalar(out, window, tap, vecs[:, bass.ds(V_CB + ct, 1)], ALU.mult, ALU.add) \
                                .then_inc(conv_step, 1)
                        else:
                            dve.wait_ge(conv_step, 4 * CONV_W * m + n - 1)
                            dve.scalar_tensor_tensor(out, window, tap, out, ALU.mult, ALU.add).then_inc(conv_step, 1)
            dve.wait_ge(conv_s_done, CT)
            dve.tensor_tensor(conv_y[:, :, SEQ:T], conv_y[:, :, SEQ:T],
                              vecs[:, V_CB:V_CB + CT].unsqueeze(2).to_broadcast([P, CT, TS]), ALU.add) \
                .then_inc(conv_done, 1)

            dve.wait_ge(masks_in, 16)
            cos, sin = (over(masks[0:ROT, c:c + T], 4) for c in (M_RC, M_RS))
            with dve.Fori(0, 4) as i:
                rows = qkvT[0:ROT, bass.ds(4 * i, 4), :]
                dve.wait_ge(rope_perm, i + 1)
                dve.tensor_tensor(r_t[:, :, :], vb[0:ROT, :, 0:T], sin, ALU.mult).then_inc(rope_step, 1)
                dve.tensor_tensor(rows, rows, cos, ALU.mult).then_inc(rope_step, 1)
                dve.wait_ge(rope_step, 2 * i + 2)
                dve.tensor_tensor(rows, rows, r_t[:, :, :], ALU.add).then_inc(rope_done, 1)

            dve.wait_ge(ln_sum, 1)
            mark(dve.tensor_scalar(rs[:, :], zb[:, 0, 0:T], 1.0 / (CT * P), None, ALU.mult))
            settle()
            dve.tensor_tensor(conv_y[:, :, :], conv_y[:, :, :], over(rs[:, :], CT), ALU.subtract) \
                .then_inc(ln_centred, 1)

            def front(n):
                sample = JOBS[n][1]
                width, neg = (288, M_NS) if sample else (384, M_NP)
                if n >= 2:
                    dve.wait_ge(exp_done, n - 1)
                dve.wait_ge(score_ready, n + 1)
                dve.scalar_tensor_tensor(sc[n % 2][:, 0:width], vb[:, n % 2, 0:width], SCALE,
                                         masks[:, neg:neg + width], ALU.mult, ALU.add).then_inc(masked, 1)
                dve.wait_ge(masked, n + 1)
                for c0, c1, c in JOB_COLS[sample]:
                    last = dve.tensor_reduce(small[:, 6 * n + c:6 * n + c + 1], sc[n % 2][:, c0:c1], AX_X, ALU.max,
                                             negate=True)
                last.then_inc(neg_max, 1)

            def back(n):
                sample = JOBS[n][1]
                cnt = M_CS if sample else M_CP
                dve.wait_ge(exp_done, n + 1)
                for c0, c1, c in JOB_COLS[sample]:
                    col = small[:, 6 * n + c + 2:6 * n + c + 3]
                    mark(dve.tensor_tensor_reduce(ex[n % 2][:, c0:c1], ex[n % 2][:, c0:c1],
                                                  masks[:, cnt + c0:cnt + c1], 1.0, 0.0, ALU.mult, ALU.add, col))
                settle()
                for c0, c1, c in JOB_COLS[sample]:
                    mark(dve.reciprocal(small[:, 6 * n + c + 4:6 * n + c + 5], small[:, 6 * n + c + 2:6 * n + c + 3]))
                settle()
                for c0, c1, c in JOB_COLS[sample]:
                    last = dve.tensor_scalar(ex[n % 2][:, c0:c1], ex[n % 2][:, c0:c1],
                                             small[:, 6 * n + c + 4:6 * n + c + 5], None, ALU.mult)
                last.then_inc(prob_ready, 1)

            front(0)
            inverse_rms(2)
            dve.tensor_tensor(conv_y[:, :, :], conv_y[:, :, :], over(rs[:, :], CT), ALU.mult).then_inc(ln_z, 1)
            for n in range(len(JOBS)):
                if n + 1 < len(JOBS):
                    front(n + 1)
                back(n)
                for t in range(sum(ADA_BESIDE[:n]), sum(ADA_BESIDE[:n + 1])):
                    ada_tile(Q_ADA_MIXER + 2 * t, ADA_FIRST + t, t % 2)
            dve.wait_ge(mods_ready, ADA_FIRST + ADA_MIXER + 2)
            scale_rows(m_a2, 4, V_G2)
            gate_rows(m_g2, 2)
            dve.wait_ge(root_ready, 3)
            mark(dve.reciprocal(sq_head[:, :, :], sq_head[:, :, :]))
            settle()
            for h in range(H):
                last = dve.scalar_tensor_tensor(oT[:, h, :], oT[:, h, :], vecs[:, V_AG + h:V_AG + h + 1],
                                                sq_head[:, h, :], ALU.mult, ALU.mult)
            last.then_inc(o_normed, 1)
            dve.wait_ge(h_hi, 2)
            part_lo(0, CT, conv_y[:, :, :])
            dve.wait_ge(h_hi, 3)
            dve.wait_ge(o_normed, 1)
            part_lo(CT, KC, oT).then_inc(h_split, 1)

            with dve.Fori(0, KC // 4) as m:
                for b in range(2):
                    j = 2 * m + b
                    quad_lo(Q_OUT + 1 + j)
                    dve.wait_ge(unit_used, 4 * (Q_OUT + j) + 8)
                    for t in range(2):
                        gate = m_g2[:, bass.ds(2 * j + t, 1), 0]
                        x = xT[:, bass.ds(2 * j + t, 1), 0:SEQ]
                        dve.scalar_tensor_tensor(x, zb[:, 2 * b + t:2 * b + t + 1, 0:SEQ], gate, x, ALU.mult, ALU.add)
                    dve.wait_ge(x1_tile, j + 1)
                    for t in range(2):
                        gate = m_g2[:, bass.ds(2 * j + t, 1), 1:NC].rearrange("p k b -> p (k b)")
                        last = dve.tensor_tensor(tmp_s[:, t, :].rearrange("p (b s) -> p b s", b=DB),
                                                 zb[:, 2 * b + t, SEQ:T].rearrange("p (b s) -> p b s", b=DB),
                                                 gate.unsqueeze(2).to_broadcast([P, DB, DS]), ALU.mult)
                    last.then_inc(x1_step, 1)
                    dve.wait_ge(x1_step, j + 1)
                    dve.sem_inc(z_free, 2)
                    x = xT[:, bass.ds(2 * j, 2), SEQ:T]
                    dve.tensor_tensor(x, x, tmp_s[:, :, :], ALU.add).then_inc(x1_tile, 1)
            dve.wait_ge(x1_tile, KC // 2 + 1)
            dve.wait_ge(k_out_done, 16)
            inverse_rms(4)
            times_rms()
            mark(modulate(ALU.mult, m_a2))
            settle()
            modulate(ALU.add, mod(3)).then_inc(h_ready, 1)
            with dve.Fori(0, (ADA_TILES - ADA_FIRST - ADA_MIXER) // 2) as m:
                for b in range(2):
                    ada_tile(Q_ADA_LAST + 2 * (2 * m + b), ADA_FIRST + ADA_MIXER + 2 * m + b, b)
            dve.wait_ge(h_hi, 4)
            dve.wait_ge(h_ready, 2)
            part_lo(0, KC, hF[:, :, :]).then_inc(h_split, 1)
            dve.wait_ge(mods_ready, ADA_TILES + 2)
            gate_rows(m_g5, 5)
            with dve.Fori(0, KC // 2) as j:
                quad_lo(Q_WQ + 1 + j)
                dve.wait_ge(qp_copied, j + 1)
                dve.sem_inc(z_free, 2)

            for tt, (t0, n) in enumerate(TOK_TILES):
                dve.wait_ge(s_copied, tt + 1)
                for hp in range(2 * H):
                    mark(dve.max(sv[0:n, hp, 0:8], s_tm[0:n, hp, :]))
                settle()
                for hp in range(2 * H):
                    dve.max_index(si_u[0:n, hp, 0:8], sv[0:n, hp, 0:8], s_tm[0:n, hp, :])
                    last = dve.match_replace(s_work[0:n, hp, :], sv[0:n, hp, 0:8], s_tm[0:n, hp, :], NEG)
                last.then_inc(s_read, 1)
                dve.wait_ge(s_read, tt + 1)
                for hp in range(2 * H):
                    mark(dve.max(sv[0:n, hp, 8:16], s_work[0:n, hp, :]))
                settle()
                for hp in range(2 * H):
                    last = dve.max_index(si_u[0:n, hp, 8:16], sv[0:n, hp, 8:16], s_work[0:n, hp, :])
                mark(last)
                s4 = sv[0:n, :, :].rearrange("n (h p) k -> n h p k", p=2)
                mark(dve.tensor_tensor(cand[0:n, :, :].rearrange("n h (a b) -> n h a b", a=TOPK),
                                       s4[:, :, 0, :].unsqueeze(3).to_broadcast([n, H, TOPK, TOPK]),
                                       s4[:, :, 1, :].unsqueeze(2).to_broadcast([n, H, TOPK, TOPK]), ALU.add))
                settle()
                mark(dve.tensor_copy(si_f[0:n, :, :], si_u[0:n, :, :]))
                fi3 = fi_u[0:n, :].rearrange("n (h k) -> n h k", h=H)
                for h in range(H):
                    mark(dve.max(fv[0:n, h, 0:8], cand[0:n, h, :]))
                settle()
                for h in range(H):
                    dve.max_index(fi3[:, h, 0:8], fv[0:n, h, 0:8], cand[0:n, h, :])
                    mark(dve.match_replace(c_work[0:n, h, :], fv[0:n, h, 0:8], cand[0:n, h, :], NEG))
                settle()
                for h in range(H):
                    mark(dve.max(fv[0:n, h, 8:16], c_work[0:n, h, :]))
                settle()
                for h in range(H):
                    mark(dve.max_index(fi3[:, h, 8:16], fv[0:n, h, 8:16], c_work[0:n, h, :]))
                dve.tensor_tensor(g_exp[0:n, :, :], fv[0:n, :, :], fv[0:n, :, 0:1].to_broadcast([n, H, TOPK]),
                                  ALU.subtract).then_inc(gate_in, 1)
                settle()
                mark(dve.tensor_single_scalar(f_au[0:n, :], fi_u[0:n, :], 4, ALU.logical_shift_right))
                mark(dve.tensor_single_scalar(f_bu[0:n, :], fi_u[0:n, :], 15, ALU.bitwise_and))
                settle()
                mark(dve.tensor_copy(f_a[0:n, :], f_au[0:n, :]))
                mark(dve.tensor_copy(f_b[0:n, :], f_bu[0:n, :]))
                if tt:
                    dve.wait_ge(picks_turned, tt)
                settle()
                io16 = over(consts[0:n, K_IO16:K_IO16 + TOPK], H * TOPK)
                si4 = si_f[0:n, :, :].rearrange("n (h p) k -> n h p k", p=2)
                for p, f in enumerate((f_a, f_b)):
                    mark(dve.tensor_tensor(oh[0:n, :, :], f[0:n, :].unsqueeze(2).to_broadcast([n, H * TOPK, TOPK]),
                                           io16, ALU.is_equal))
                    settle()
                    oh4 = oh[0:n, :, :].rearrange("n (h k) a -> n h k a", h=H)
                    mark(dve.tensor_tensor(oh4, oh4, si4[:, :, p, :].unsqueeze(2).to_broadcast([n, H, TOPK, TOPK]),
                                           ALU.mult))
                    settle()
                    mark(dve.tensor_reduce(picks[0:n, p, :], oh[0:n, :, :], AX_X, ALU.add))
                    settle()
                dve.wait_ge(gate_out, tt + 1)
                mark(dve.tensor_reduce(small[0:n, 0:H], g_exp[0:n, :, :], AX_X, ALU.add))
                settle()
                mark(dve.reciprocal(small[0:n, H:2 * H], small[0:n, 0:H]))
                settle()
                dve.tensor_tensor(picks[0:n, 2, :].rearrange("n (h k) -> n h k", h=H), g_exp[0:n, :, :],
                                  small[0:n, H:2 * H].unsqueeze(2).to_broadcast([n, H, TOPK]), ALU.mult) \
                    .then_inc(picks_ready, 1)

            dve.wait_ge(spilled, 16)
            dve.memset(acc[:, :, :], 0.0).then_inc(acc_zero, 1)
            dve.wait_ge(acc_zero, 1)
            dve.wait_ge(picks_copied, 3 * 3)
            for half in range(2):
                q0, p0 = Q_PEER + HALF * half, PAIRS * half
                if half:
                    dve.wait_ge(unit_used, 4 * (Q_PEER + HALF) + 4)
                ks = consts[:, K_IOTA + HALF * half:K_IOTA + HALF * (half + 1)]
                with dve.Fori(0, T // 16) as i:
                    for b in range(2):
                        g = 2 * i + b
                        dve.wait_ge(g_ready, G_GROUPS * half + g + 1)
                        for t in range(8):
                            dve.tensor_scalar(one1[b][:, t, :], iota, i1T[:, bass.ds(8 * g + t, 1)],
                                              gT[:, bass.ds(8 * g + t, 1)], ALU.is_equal, ALU.mult)
                        dve.tensor_tensor(one2[b][:, :, :], over(ks, 8),
                                          i2T[:, bass.ds(8 * g, 8)].unsqueeze(2).to_broadcast([P, 8, HALF]),
                                          ALU.is_equal).then_inc(one_ready, 1)

                def weigh(pair, b):
                    k = p0 + pair
                    dve.wait_ge(gelu_done, k + 3)
                    dve.wait_ge(w_ready, k + 2)
                    gates = G[:, :, bass.ds(2 * pair, 2)].rearrange("p t e -> p e t")
                    dve.tensor_tensor(w_f[:, :, :], gl[b][:, :, :], gates, ALU.mult)
                    dve.tensor_tensor(w_hi[b][:, :, :], gl[b][:, :, :], gates, ALU.mult).then_inc(w_mid, 1)
                    dve.wait_ge(w_mid, k + 1)
                    dve.tensor_tensor(w_lo[b][:, :, :], w_f[:, :, :], w_hi[b][:, :, :].bitcast(F32), ALU.subtract) \
                        .then_inc(w_ready, 1)

                def add_sums(pair, q, s, q_next):
                    for d in range(2):
                        if d == 0:
                            dve.wait_ge(vb_ready, 4 * (p0 + pair) + s + 1)
                        else:
                            if s and q_next is not None:
                                split_lo(dve, q_next, s - 1)
                            dve.wait_ge(unit_used, 4 * q + s + 5)
                        out = acc[:, 4 * s + 2 * d:4 * s + 2 * d + 2, :]
                        dve.tensor_tensor(out, out, vb[:, 2 * d:2 * d + 2, 0:T], ALU.add).then_inc(vb_free, 2)

                def body(i, b):
                    weigh(i, b)
                    quad_lo(q0 + 2 * i + 2)
                    for s in range(4):
                        add_sums(i, q0 + 2 * i + 2, s, q0 + 2 * i + 3)
                    split_lo(dve, q0 + 2 * i + 3, 3)

                dve.wait_ge(g_copied, G_GROUPS * (half + 1) + 2)
                quad_lo(q0 + 1)
                with dve.Fori(0, (PAIRS - 2) // 2) as m:
                    body(2 * m, 0)
                    body(2 * m + 1, 1)
                body(PAIRS - 2, 0)
                weigh(PAIRS - 1, 1)
                for s in range(4):
                    add_sums(PAIRS - 1, q0 + HALF - 1, s, q0 + HALF if half == 0 else None)
                if half == 0:
                    split_lo(dve, q0 + HALF, 3)

            dve.wait_ge(x1_in, 16)
            dve.wait_ge(vb_free, 32 * PAIRS + 4)
            for view, spread in ((acc[:, :, 0:SEQ], m_g5[:, :, 0:1].to_broadcast([P, KC, SEQ])),
                                 (acc[:, :, SEQ:T].rearrange("p k (b s) -> p k b s", b=DB),
                                  m_g5[:, :, 1:NC].unsqueeze(3).to_broadcast([P, KC, DB, DS]))):
                mark(dve.tensor_tensor(view, view, spread, ALU.mult))
            settle()
            dve.tensor_tensor(x2[:, :, :], x2[:, :, :], acc[:, :, :], ALU.add).then_inc(x2_ready, 1)
            inverse_rms(5)
            for k in range(KC):
                last = dve.scalar_tensor_tensor(fin[:, k, :], x2[:, k, :], vecs[:, V_GF + k:V_GF + k + 1], rs[:, :],
                                                ALU.mult, ALU.mult)
                if k % 4 == 3:
                    last.then_inc(y_ready, 1)


_OUTS = [("y", (P, KC, T)), ("k", (P, H, T)), ("v", (P, H, T)), ("conv_p", (P, CT, HIST)),
         ("conv_s", (P, CT, DB, HIST))]


def kernel(**a):
    import numpy as np
    import concourse.bacc as bacc
    from concourse.bass_utils import run_bass_kernel_spmd

    a = {k: np.asarray(v) for k, v in a.items()}

    def channels(x, *rest):
        return x.reshape(-1, x.shape[-1] // P, P).transpose(2, 1, 0)

    def tiles(w):
        return w.reshape(KC, P, -1, P).transpose(2, 1, 0, 3).reshape(-1, P, KC * P)

    x = np.concatenate([a["x_prompt"].reshape(SEQ, D), a["x_sample"].reshape(TS, D)])
    c = np.concatenate([a["c_prompt"], a["c_sample"]])
    glu0 = np.zeros((P, CT, GW), np.float32)
    hist = a["state_conv"][0].reshape(DB, HIST, CT, P).transpose(3, 2, 0, 1)
    glu0[:, :, GW_P:].reshape(P, CT, DB, GW_S)[..., :HIST] = hist
    w_in = tiles(a["w_in"][0])
    order = [t for j in range(CT) for t in (j, CT + j)] + list(range(2 * CT, 2 * CT + 3 * H))
    ck = a["cache_k"][0].reshape(2, 4, PAST, H, E).transpose(3, 0, 4, 1, 2).reshape(H, 2, E, UNIT)
    cv = a["cache_v"][0].reshape(2, 4, 2, P, H, E).transpose(4, 0, 3, 2, 1, 5).reshape(H, 2, P, UNIT)
    u = a["peer_u"][0].reshape(NK, NK, KC, P).transpose(1, 3, 2, 0).reshape(NK, P, KC * P)

    vecs = np.zeros((P, V_N), np.float32)
    for at, v in ((V_G1, a["norm1_g"]), (V_G2, a["norm2_g"]), (V_GF, a["final_g"]), (V_LNG, a["conv_ln_g"]),
                  (V_LNB, a["conv_ln_b"]), (V_CB, a["conv_b"]), (V_AG, a["attn_out_g"]), (V_ADA, a["b_ada"])):
        n = v.size // P
        vecs[:, at:at + n] = v.reshape(n, P).T
    vecs[:, V_CW:V_ADA] = a["conv_w"][0].reshape(CONV_W, CT, P).transpose(2, 1, 0).reshape(P, -1)

    consts = np.zeros((P, K_N), np.float32)
    consts[:, K_ID:K_ID + P] = np.eye(P)
    consts[:, K_ONE:K_ONE + P] = 1.0
    consts[:, K_IOTA:K_IOTA + NK] = np.arange(NK)
    consts[:2 * NC, K_SEL:K_SEL + NC] = np.tile(np.eye(NC), (2, 1))
    consts[:, K_IO16:K_IO16 + TOPK] = np.arange(TOPK)
    consts[:, K_EPS] = EPS

    def patterns(d):
        return sum(((d >= 0) & (d % dil == 0) & (d // dil <= win // dil)).astype(np.float32)
                   for win, dil in ((128, 1), (512, 4), (2048, 16)))

    masks = np.zeros((P, M_N), np.float32)
    r = np.arange(P)[:, None]
    prompt = np.concatenate([patterns(r - r.T), patterns(128 + r - np.arange(256)[None])], axis=1)
    b, s = r // DS % DB, r % DS
    new = np.arange(TS)[None]
    sample = np.concatenate([patterns(PAST + s - np.arange(PAST)[None]),
                             patterns(s - new % DS) * (b == new // DS)], axis=1)
    for cnt, neg, m in ((M_CP, M_NP, prompt), (M_CS, M_NS, sample)):
        masks[:, cnt:cnt + m.shape[1]] = m
        masks[:, neg:neg + m.shape[1]] = np.where(m > 0, 0.0, -1e30)
    pos = np.concatenate([np.arange(SEQ), PAST + np.arange(TS) % DS]).astype(np.float32)
    inv = np.float32(500000.0) ** (-np.arange(0, ROT, 2, dtype=np.float32) / np.float32(ROT))
    ang = (pos[None] * inv[:, None]).astype(np.float32)
    masks[:ROT, M_RC:M_RC + T] = np.tile(np.cos(ang), (2, 1))
    masks[:ROT // 2, M_RS:M_RS + T] = -np.sin(ang)
    masks[ROT // 2:ROT, M_RS:M_RS + T] = np.sin(ang)
    masks[np.arange(ROT), M_PERM + (np.arange(ROT) + ROT // 2) % ROT] = 1.0

    ins = {
        "xT": channels(x), "cT": channels(c), "glu0": glu0,
        "w_ada": a["w_ada"][0].reshape(8, 2, P, ADA_TILES, 512).transpose(3, 0, 2, 1, 4).reshape(ADA_TILES, 8, P, UNIT),
        "w_in": w_in[order], "w_out": tiles(a["w_out"][0]), "w_q": tiles(a["peer_wq"][0]),
        "keys": a["peer_keys"][0].reshape(2 * H, NK, P).transpose(2, 0, 1),
        "u": u, "v": a["peer_v"][0].reshape(NK, NK, D), "ck": ck, "cv": cv,
        "vecs": vecs, "consts": consts, "masks": masks,
    }
    nc = bacc.Bacc("TRN2", target_bir_lowering=False, num_devices=1)
    ins = {f"in_{k}": np.ascontiguousarray(v) for k, v in ins.items()}
    args = [nc.dram_tensor(k, v.shape, F32, kind="ExternalInput").ap() for k, v in ins.items()]
    args += [nc.dram_tensor(f"out_{k}", s, F32, kind="ExternalOutput").ap() for k, s in _OUTS]
    layer_kernel(nc, *args)
    got = run_bass_kernel_spmd(nc, [ins], core_ids=[0]).results[0]

    y = got["out_y"].transpose(2, 1, 0).reshape(T, D)
    k, v = (got[f"out_{n}"].transpose(2, 1, 0) for n in "kv")
    conv_p = got["out_conv_p"].transpose(2, 1, 0).reshape(1, 1, HIST, CT * P)
    conv_s = got["out_conv_s"].transpose(2, 3, 1, 0).reshape(1, DB, HIST, CT * P)
    y, k, v, conv_p, conv_s = (np.ascontiguousarray(z) for z in (y, k, v, conv_p, conv_s))
    return (y[:SEQ].reshape(1, SEQ, D), y[SEQ:].reshape(DB, DS, D),
            k[:SEQ].reshape(1, 1, SEQ, H, E), v[:SEQ].reshape(1, 1, SEQ, H, E), conv_p,
            k[SEQ:].reshape(1, DB, DS, H, E), v[SEQ:].reshape(1, DB, DS, H, E), conv_s)
```

```python
from contextlib import ExitStack

import concourse.bass as bass
from concourse import mybir

F32 = mybir.dt.float32
F32R = mybir.dt.float32r
U32 = mybir.dt.uint32
ALU = mybir.AluOpType
ACT = mybir.ActivationFunctionType
AX_X = mybir.AxisListType.X

P = 128
D = 2048
KC = D // P
SEQ = 256
DB, DS = 8, 4
TS = DB * DS
T = SEQ + TS
NC = 1 + DB
PAST = 256
CONV_W = 31
HIST = CONV_W - 1
CT = 8
GW_P = HIST + SEQ
GW_S = HIST + DS
GW = GW_P + DB * GW_S
H = 8
E = 128
ROT = 32
SCALE = float(E) ** -0.5
EPS = 1e-6
N_ADA = 6
TOPK = 16
NK = 128
HALF = NK // 2
TB = 32
TBLKS = T // TB
CHUNK = 4
CHUNKS = HALF // CHUNK
NEG = -3.0e38
UNIT = 1024
TOK_TILES = ((0, 128), (128, 128), (256, 32))
TOPK_HEADS = (8, 8, 2)

ADA_TILES = N_ADA * D // 512
ADA_FIRST = 8
ADA_MIXER = 12
ADA_LAST = ADA_TILES - ADA_FIRST - ADA_MIXER
Q_GLU = 2 * ADA_FIRST
Q_QKV = Q_GLU + CT
Q_ADA_MIXER = Q_QKV + 12
Q_OUT = Q_ADA_MIXER + 2 * ADA_MIXER
Q_WQ = Q_OUT + KC // 2
Q_ADA_LAST = Q_WQ + KC // 2
Q_PEER = Q_ADA_LAST + 2 * ADA_LAST
PAIRS = NK // 2
KV_PAIRS = 3 * H // 2
G_GROUPS = T // 8
ON_ACT = 2

ZB = TS + DS

JOBS = [(0, 0), (1, 0), (2, 0), (3, 0), (0, 1), (4, 0), (5, 0), (6, 0), (7, 0), (1, 1)]
ADA_BESIDE = (1, 1, 1, 2, 1, 1, 1, 1, 2, 1)


def ada_steps(n):
    return range(2 * sum(ADA_BESIDE[:n]), 2 * sum(ADA_BESIDE[:n + 1]))


JOB_COLS = (((0, 128, 0), (128, 384, 1)), ((0, 288, 0),))

V_G1, V_G2, V_GF = 0, 16, 32
V_LNG, V_LNB, V_CB, V_AG = 48, 56, 64, 72
V_CW = 80
V_ADA = V_CW + CT * CONV_W
V_N = V_ADA + N_ADA * KC

K_ID, K_ONE, K_IOTA, K_SEL, K_IO16 = 0, 128, 256, 384, 394
K_EPS = 410
K_N = 411
M_CP, M_NP, M_CS, M_NS, M_RC, M_RS, M_PERM = 0, 384, 768, 1056, 1344, 1632, 1920
M_N = M_PERM + P


def layer_kernel(nc, xT_d, cT_d, glu0_d, w_ada_d, w_in_d, w_out_d, w_q_d, keys_d, u_d, v_d, ck_d, cv_d,
                 vecs_d, consts_d, masks_d, y_d, k_out, v_out, convp_out, convs_out):
    spill_d = nc.dram_tensor("x1_spill", [P, KC * T], F32).ap()
    gates_d = nc.dram_tensor("gates_2nd", [TBLKS, P, CHUNKS, CHUNK * TB], F32).ap()

    base = [16512]

    def at(name, shape, dt, offset):
        return nc.alloc_sbuf_tensor_at(name, shape, dt, offset=offset)

    def sb(name, shape, dt=F32):
        n = 4
        for s in shape[1:]:
            n *= s
        t = at(name, shape, dt, base[0])
        base[0] += (n + 63) // 64 * 64
        return t

    raw = [sb(f"raw{s}", [P, UNIT]) for s in range(4)]
    hi = [sb(f"hi{s}", [P, UNIT], F32R) for s in range(4)]
    lo = [sb(f"lo{s}", [P, UNIT], F32R) for s in range(4)]
    act_hi_at = base[0]
    act_hi = sb("act_hi", [P, KC, T], F32R)
    act_lo = sb("act_lo", [P, KC, T], F32R)
    x_at = base[0]
    xT = sb("xT", [P, KC, T])
    mods_at = base[0]
    mods = sb("mods", [P, N_ADA * KC, NC])
    vecs = sb("vecs", [P, V_N])
    consts = sb("consts", [P, K_N])
    rs = sb("rs", [P, T])
    m_a1 = sb("m_a1", [P, KC, NC])
    m_a2 = sb("m_a2", [P, KC, NC])
    m_g2 = sb("m_g2", [P, KC, NC])
    m_g5 = sb("m_g5", [P, KC, NC])
    tmp_s = sb("tmp_s", [P, 2, TS])
    small = sb("small", [P, 64])
    cT = sb("cT", [P, KC, NC])
    c_split = sb("c_split", [P, KC, 2 * NC], F32R)
    ada_row = [sb(f"ada_row{b}", [2 * NC, 512]) for b in range(2)]
    zone = base[0]

    glu = at("glu", [P, CT, GW], F32, zone)
    cache = [at(f"cache{s}", [P, UNIT], F32, zone + 4096 * s) for s in range(4)]
    conv_y = at("conv_y", [P, CT, T], F32, zone + 17920)
    qkvT = at("qkvT", [P, 3 * H, T], F32, zone + 27136)
    v_tok = at("v_tok", [P, 3, H * E], F32, zone + 54784)
    sc = [at(f"sc{b}", [P, 384], F32, zone + 67072 + 1536 * b) for b in range(2)]
    ex = [at(f"ex{b}", [P, 384], F32, zone + 70144 + 1536 * b) for b in range(2)]
    pT = at("pT", [P, 384], F32, zone + 73216)
    o_row = at("o_row", [P, P], F32, zone + 74752)
    prod = at("prod", [P, TS, CONV_W], F32, zone + 67072)
    sig = at("sig", [P, T], F32, zone + 71040)
    masks = at("masks", [P, M_N], F32, zone + 76288)
    zq = at("zq", [P, 4, DB * ZB], F32, zone + 84480)
    keysT = at("keysT", [P, 2 * H, NK], F32, zone + 78592)
    r_t = at("r_t", [ROT, 4, T], F32, zone + 54784)
    sq_head = at("sq_head", [P, H, T], F32, zone + 27136)
    sq = at("sq", [P, KC, T], F32, act_hi_at)
    sq_ln = at("sq_ln", [P, CT, T], F32, act_hi_at)
    zp = at("zp", [P, 2 * 4, DB * ZB], F32, act_hi_at + 9216)
    sq_at = at("sq_at", [P, H, T], F32, act_hi_at + 18432 + 9216)
    hF = at("hF", [P, KC, T], F32, zone + 27136)
    oT = qkvT[:, 2 * H:3 * H, :]
    qpT = at("qpT", [P, KC, T], F32, zone)
    s_tm = at("s_tm", [P, 2 * H, NK], F32, zone + 18432)
    s_work = at("s_work", [P, 2 * H, NK], F32, zone + 45568)
    cand = at("cand", [P, H, 256], F32, zone + 53760)
    c_work = at("c_work", [P, H, 256], F32, zone + 61952)
    oh = at("oh", [P, H * TOPK, TOPK], F32, zone + 26624)
    sv = at("sv", [P, 2 * H, TOPK], F32, zone + 70144)
    si_u = at("si_u", [P, 2 * H, TOPK], U32, zone + 71168)
    si_f = at("si_f", [P, 2 * H, TOPK], F32, zone + 72192)
    fv = at("fv", [P, H, TOPK], F32, zone + 73216)
    fi_u = at("fi_u", [P, H * TOPK], U32, zone + 73728)
    f_au = at("f_au", [P, H * TOPK], U32, zone + 74240)
    f_bu = at("f_bu", [P, H * TOPK], U32, zone + 74752)
    f_a = at("f_a", [P, H * TOPK], F32, zone + 75264)
    f_b = at("f_b", [P, H * TOPK], F32, zone + 75776)
    picks = at("picks", [P, 3, H * TOPK], F32, zone + 76288)
    g_exp = at("g_exp", [P, H, TOPK], F32, zone + 77824)
    G = at("G", [P, CHUNKS, TBLKS, CHUNK, TB], F32, zone)
    w_hi = [at(f"w_hi{b}", [P, 2, T], F32R, zone + 73728 + 2304 * b) for b in range(2)]
    w_lo = [at(f"w_lo{b}", [P, 2, T], F32R, zone + 78336 + 2304 * b) for b in range(2)]
    w_f = at("w_f", [P, 2, T], F32, zone + 82944)
    gl = [at(f"gl{b}", [P, 2, T], F32, zone + 85248 + 2304 * b) for b in range(2)]
    one1 = [at(f"one1_{b}", [P, 8, NK], F32, zone + 73728 + 4096 * b) for b in range(2)]
    one2 = [at(f"one2_{b}", [P, 8, NK], F32, zone + 81920 + 4096 * b) for b in range(2)]
    stage = [at(f"stage{b}", [P, CHUNKS, CHUNK, TB], F32, x_at + 8192 * b) for b in range(2)]
    i1T = at("i1T", [P, T], F32, mods_at)
    i2T = at("i2T", [P, T], F32, mods_at + 4 * T)
    gT = at("gT", [P, T], F32, mods_at + 8 * T)
    minus_gT = at("minus_gT", [P, T], F32, zone + 90112)
    acc = at("acc", [P, KC, T], F32, x_at)
    x2 = at("x2", [P, KC, T], F32, zone)
    fin = at("fin", [P, KC, T], F32, zone + 18432)
    assert zone + 91264 <= nc.sbuf_usable_end

    ident, ones = consts[:, K_ID:K_ID + P], consts[:, K_ONE:K_ONE + P]
    iota = consts[:, K_IOTA:K_IOTA + NK]

    with ExitStack() as ctx:
        def sem(name):
            return ctx.enter_context(nc.semaphore(name))

        zb = ctx.enter_context(nc.psum_tensor("zb", [P, 4, 512], F32))
        vb = ctx.enter_context(nc.psum_tensor("vb", [P, 4, 512], F32))

        raw_in = [sem(f"raw_in{s}") for s in range(4)]
        cache_in = [sem(f"cache_in{s}") for s in range(4)]
        hi_ready = sem("hi_ready")
        lo_ready = sem("lo_ready")
        unit_used = sem("unit_used")
        z_free = sem("z_free")
        c_in = sem("c_in")
        consts_in = sem("consts_in")
        vecs_in = sem("vecs_in")
        x_in = sem("x_in")
        glu0_in = sem("glu0_in")
        masks_in = sem("masks_in")
        keys_in = sem("keys_in")
        silu_done = sem("silu_done")
        c_ready = sem("c_ready")
        row_copied = sem("row_copied")
        row_turned = sem("row_turned")
        mods_ready = sem("mods_ready")
        sq_ready = sem("sq_ready")
        stat_ready = sem("stat_ready")
        root_ready = sem("root_ready")
        h_ready = sem("h_ready")
        h_hi = sem("h_hi")
        h_split = sem("h_split")
        sig_ready = sem("sig_ready")
        glu_ready = sem("glu_ready")
        z_half = sem("z_half")
        qkv_evac = sem("qkv_evac")
        rope_perm = sem("rope_perm")
        rope_step = sem("rope_step")
        rope_done = sem("rope_done")
        conv_step = sem("conv_step")
        conv_done = sem("conv_done")
        prod_step = sem("prod_step")
        conv_s_done = sem("conv_s_done")
        hist_out = sem("hist_out")
        v_out_done = sem("v_out_done")
        k_out_done = sem("k_out_done")
        ln_sum = sem("ln_sum")
        ln_centred = sem("ln_centred")
        ln_sq = sem("ln_sq")
        ln_sqsum = sem("ln_sqsum")
        ln_z = sem("ln_z")
        ln_out = sem("ln_out")
        v_turned = sem("v_turned")
        v_copied = sem("v_copied")
        cache_used = sem("cache_used")
        score_ready = sem("score_ready")
        masked = sem("masked")
        neg_max = sem("neg_max")
        exp_done = sem("exp_done")
        prob_ready = sem("prob_ready")
        prob_turned = sem("prob_turned")
        pT_ready = sem("pT_ready")
        zero_ready = sem("zero_ready")
        zq_ready = sem("zq_ready")
        o_rows = sem("o_rows")
        o_rows_copied = sem("o_rows_copied")
        o_ready = sem("o_ready")
        o_copied = sem("o_copied")
        o_sq = sem("o_sq")
        o_sum = sem("o_sum")
        o_normed = sem("o_normed")
        x1_step = sem("x1_step")
        x1_tile = sem("x1_tile")
        qp_copied = sem("qp_copied")
        s_ready = sem("s_ready")
        s_copied = sem("s_copied")
        s_read = sem("s_read")
        gate_in = sem("gate_in")
        gate_out = sem("gate_out")
        picks_ready = sem("picks_ready")
        picks_turned = sem("picks_turned")
        picks_copied = sem("picks_copied")
        spilled = sem("spilled")
        one_ready = sem("one_ready")
        distance = sem("distance")
        one_act_ready = sem("one_act_ready")
        g_ready = sem("g_ready")
        g_copied = sem("g_copied")
        g2_copied = sem("g2_copied")
        g2_out = [sem(f"g2_out{b}") for b in range(2)]
        g2_in = sem("g2_in")
        acc_zero = sem("acc_zero")
        gelu_done = sem("gelu_done")
        w_mid = sem("w_mid")
        w_ready = sem("w_ready")
        vb_ready = sem("vb_ready")
        vb_free = sem("vb_free")
        x1_in = sem("x1_in")
        x2_ready = sem("x2_ready")
        y_ready = sem("y_ready")
        y_out = sem("y_out")
        dve_step = sem("dve_step")
        block = ctx.enter_context(nc.Block())

        def over(ap, n):
            return ap.unsqueeze(1).to_broadcast([ap.shape[0], n, ap.shape[1]])

        def per_token(ap, n, width):
            return ap.to_broadcast([P, n, width])

        def load(sp, q, s, dst_src):
            sp.wait_ge(lo_ready, 4 * q + s + 1)
            sp.dma_start(raw[s][:, :] if dst_src[0] is None else dst_src[0], dst_src[1]).then_inc(raw_in[s], 16)

        def split_hi(act, q, s):
            act.wait_ge(raw_in[s], 16 * q + 16)
            act.wait_ge(unit_used, 4 * q + s + 1)
            act.activation(hi[s][:, :], raw[s][:, :], ACT.Copy).then_inc(hi_ready, 1)

        def split_lo(dve, q, s):
            dve.wait_ge(hi_ready, 4 * q + s + 1)
            dve.tensor_tensor(lo[s][:, :], raw[s][:, :], hi[s][:, :].bitcast(F32), ALU.subtract) \
                .then_inc(lo_ready, 1)

        def project(pe, q, parity, tile=None):
            for s in range(4):
                bank = 2 * parity + s // 2
                if s % 2 == 0 and tile is not None:
                    pe.wait_ge(z_free, tile + s // 2 + 1)
                pe.wait_ge(lo_ready, 4 * q + s + 5)
                for j in range(8):
                    k = 8 * (s % 2) + j
                    w_h, w_l = hi[s][:, j * P:(j + 1) * P], lo[s][:, j * P:(j + 1) * P]
                    pe.matmul(zb[:, bank, 0:T], w_h, act_hi[:, k, :], start=(k == 0), stop=False)
                    pe.matmul(zb[:, bank, 0:T], w_h, act_lo[:, k, :], start=False, stop=False)
                    last = pe.matmul(zb[:, bank, 0:T], w_l, act_hi[:, k, :], start=False, stop=(k == KC - 1))
                last.then_inc(unit_used, 1)

        @block.sync
        def _(sp):
            def load_ada(q0, n0, count):
                with sp.Fori(0, count) as n:
                    for k in range(8):
                        load(sp, q0 + 2 * n + k // 4, k % 4, (None, w_ada_d[n + n0, k]))

            load_ada(0, 0, ADA_FIRST)
            with sp.Fori(0, CT) as j:
                for s in range(4):
                    load(sp, Q_GLU + j, s, (None, w_in_d[2 * j + s // 2][:, UNIT * (s % 2):UNIT * (s % 2 + 1)]))
            with sp.Fori(0, 12) as j:
                for s in range(4):
                    load(sp, Q_QKV + j, s,
                         (None, w_in_d[2 * CT + 2 * j + s // 2][:, UNIT * (s % 2):UNIT * (s % 2 + 1)]))
            def load_proj(q0, w_d):
                with sp.Fori(0, KC // 2) as j:
                    for s in range(4):
                        load(sp, q0 + j, s, (None, w_d[2 * j + s // 2][:, UNIT * (s % 2):UNIT * (s % 2 + 1)]))

            load_ada(Q_ADA_MIXER, ADA_FIRST, ADA_MIXER)
            load_proj(Q_OUT, w_out_d)
            load_proj(Q_WQ, w_q_d)
            load_ada(Q_ADA_LAST, ADA_FIRST + ADA_MIXER, ADA_LAST)

            def load_u(pair, q):
                for s in range(4):
                    i2 = 2 * pair + s // 2
                    load(sp, q, s, (None, u_d[i2][:, UNIT * (s % 2):UNIT * (s % 2 + 1)]))

            def load_v(pair, q):
                for s in range(4):
                    dst = raw[s][:, :].rearrange("p (a d) -> p a d", a=2)
                    load(sp, q, s, (dst, v_d[:, bass.ds(2 * pair, 2), 512 * s:512 * (s + 1)]))

            load_u(0, Q_PEER)
            with sp.Fori(0, PAIRS - 1) as i:
                load_u(i + 1, Q_PEER + 2 * i + 1)
                load_v(i, Q_PEER + 2 * i + 2)
            load_v(PAIRS - 1, Q_PEER + NK - 1)

        @block.gpsimd
        def _(pool):
            pool.wait_ge(vecs_in, 16)
            pool.wait_ge(mods_ready, ADA_FIRST + 2)
            with pool.Fori(0, CT) as ct:
                pool.wait_ge(glu_ready, ct + 2)
                row = glu[:, bass.ds(ct, 1), GW_P:GW]
                window = bass.AP(row.tensor, row.offset, [list(row.ap[0]), [GW_S, DB], [1, DS], [1, CONV_W]])
                taps = vecs[:, bass.ds(V_CW + CONV_W * ct, CONV_W)]
                taps = bass.AP(taps.tensor, taps.offset, [list(taps.ap[0]), [0, DB], [0, DS], [1, CONV_W]])
                out = prod[:, :, :].rearrange("p (b s) w -> p b s w", b=DB)
                pool.tensor_tensor(out, window, taps, ALU.mult).then_inc(prod_step, 1)
                for k, n in enumerate((16, 8, 4, 2)):
                    pool.wait_ge(prod_step, 5 * ct + k + 1)
                    m = min(n, CONV_W - n)
                    pool.tensor_tensor(prod[:, :, 0:m], prod[:, :, 0:m], prod[:, :, n:n + m], ALU.add) \
                        .then_inc(prod_step, 1)
                pool.wait_ge(prod_step, 5 * ct + 5)
                pool.tensor_tensor(conv_y[:, bass.ds(ct, 1), SEQ:T].rearrange("p c t -> p t c"), prod[:, :, 0:1],
                                   prod[:, :, 1:2], ALU.add).then_inc(conv_s_done, 1)
                pool.wait_ge(conv_s_done, ct + 1)
            pool.dma_start(convp_out, glu[:, :, SEQ:GW_P]).then_inc(hist_out, 16)
            for ct in range(CT):
                src = glu[:, ct, GW_P:GW].rearrange("p (b w) -> p b w", b=DB)[:, :, DS:GW_S]
                pool.dma_start(convs_out[:, ct], src).then_inc(hist_out, 16)
            pool.wait_ge(qkv_evac, KV_PAIRS)
            pool.dma_start(v_out, qkvT[:, 2 * H:3 * H, :]).then_inc(v_out_done, 16)
            pool.wait_ge(rope_done, 5)
            pool.dma_start(k_out, qkvT[:, H:2 * H, :]).then_inc(k_out_done, 16)

            pool.wait_ge(unit_used, 4 * Q_ADA_MIXER + 4)
            pool.memset(zq[:, :, :], 0.0).then_inc(zero_ready, 1)
            pool.memset(zp[:, :, :], 0.0).then_inc(zero_ready, 1)
            pool.wait_ge(conv_done, 1)
            pool.wait_ge(hist_out, 16 * (1 + CT))
            pool.wait_ge(zero_ready, 2)
            for n in range(32):
                if n in (4, 12):
                    g = n // 8
                    if g:
                        pool.wait_ge(score_ready, 5)
                    pool.tensor_copy(zq[:, :, :].rearrange("p h (b x) -> p h b x", x=ZB)[:, :, :, 0:DS],
                                     qkvT[:, 4 * g:4 * g + 4, SEQ:T].rearrange("p h (b s) -> p h b s", b=DB)) \
                        .then_inc(zq_ready, 1)
                if n >= 4:
                    pool.wait_ge(cache_used, n - 3)
                src = (ck_d, cv_d)[n // 8 % 2][4 * (n // 16) + n % 8 // 2, n % 2]
                pool.dma_start(cache[n % 4][:, :], src).then_inc(cache_in[n % 4], 16)

            pool.wait_ge(prob_ready, len(JOBS))
            pool.dma_start(keysT[:, :, :], keys_d).then_inc(keys_in, 16)

            pool.wait_ge(h_split, 3)
            pool.dma_start(spill_d, xT[:, :, :].rearrange("p k t -> p (k t)")).then_inc(spilled, 16)

            pool.wait_ge(lo_ready, 4 * Q_ADA_LAST + 8)
            with pool.Fori(0, 2 * ADA_LAST) as q:
                for s in range(4):
                    split_lo(pool, Q_ADA_LAST + 1 + q, s)

            for b in range(2):
                pool.wait_ge(g2_out[b], 16 * ((TBLKS + 1 - b) // 2))
            pool.memset(acc[:, :, :], 0.0).then_inc(acc_zero, 1)
            with pool.Fori(0, CHUNKS) as c:
                pool.wait_ge(w_ready, 2 * c + 4)
                pool.dma_start(G[:, bass.ds(c, 1), :, :, :].rearrange("p c b e t -> p (c b) (e t)"),
                               gates_d[:, :, bass.ds(c, 1), :].rearrange("b p c x -> p (b c) x")).then_inc(g2_in, 16)
                pool.wait_ge(g2_in, 16 * c + 16)

            pool.wait_ge(w_ready, PAIRS // 2 + PAIRS // 4 + 2)
            pool.dma_start(x2[:, :, :].rearrange("p k t -> p (k t)"), spill_d).then_inc(x1_in, 16)
            pool.wait_ge(v_out_done, 16)
            pool.wait_ge(k_out_done, 16)
            pool.wait_ge(y_out, 16 * 4)

        @block.scalar
        def _(act):
            def quad_hi(q):
                for s in range(4):
                    split_hi(act, q, s)

            eps = consts[:, K_EPS:K_EPS + 1]

            def root(total, n, ready, k):
                act.wait_ge(ready, k)
                act.activation(rs[:, :], total, ACT.Sqrt, bias=eps, scale=1.0 / n).then_inc(root_ready, 1)

            for dst, src, arrived in ((cT[:, :, :], cT_d, c_in), (xT[:, :, :], xT_d, x_in),
                                      (consts[:, :], consts_d, consts_in), (vecs[:, :], vecs_d, vecs_in),
                                      (glu[:, :, :], glu0_d, glu0_in), (masks[:, :], masks_d, masks_in)):
                act.dma_start(dst, src).then_inc(arrived, 16)
            act.sem_inc(z_free, 4)
            act.sem_inc(row_copied, 2)
            act.sem_inc(g_copied, 2)
            act.sem_inc(gelu_done, 2)
            act.wait_ge(c_in, 16)
            act.activation(cT[:, :, :], cT[:, :, :], ACT.Silu).then_inc(silu_done, 1)
            act.wait_ge(x_in, 16)
            act.activation(sq[:, :, :], xT[:, :, :], ACT.Square).then_inc(sq_ready, 1)
            act.wait_ge(consts_in, 16)
            root(vb[:, 2, 0:T], D, stat_ready, 1)
            quad_hi(0)
            def ada_out(n, b):
                act.wait_ge(row_turned, n + 1)
                act.activation(ada_row[b][:, :], zb[0:2 * NC, b, :], ACT.Copy).then_inc(row_copied, 1)

            def ada_tiles(q0, n0, count):
                with act.Fori(0, count // 2) as m:
                    for b in range(2):
                        quad_hi(q0 + 4 * m + 2 * b + 1)
                        quad_hi(q0 + 4 * m + 2 * b + 2)
                        ada_out(n0 + 2 * m + b, b)

            ada_tiles(0, 0, ADA_FIRST)
            act.wait_ge(h_ready, 1)
            act.activation(act_hi[:, :, :], hF[:, :, :], ACT.Copy).then_inc(h_hi, 1)
            act.wait_ge(mods_ready, ADA_FIRST + 2)
            with act.Fori(0, CT // 2) as m:
                for b in range(2):
                    j = 2 * m + b
                    quad_hi(Q_GLU + 1 + j)
                    act.wait_ge(glu_ready, j + 1)
                    act.activation(sig[:, :], zb[:, 2 * b + 1, 0:T], ACT.Sigmoid).then_inc(sig_ready, 1)
            with act.Fori(0, 2) as m:
                for k in range(6):
                    j = 6 * m + k
                    quad_hi(Q_QKV + 1 + j)
                    pair = zb[:, 2 * (k % 2):2 * (k % 2) + 2, 0:T]
                    act.activation(qkvT[:, bass.ds(2 * j, 2), :], pair, ACT.Copy).then_inc(qkv_evac, 1)
            act.wait_ge(rope_done, 5)
            for g in range(6):
                n = TOK_TILES[g // 2][1]
                act.wait_ge(v_turned, g + 1)
                act.activation(v_tok[0:n, g // 2, 512 * (g % 2):512 * (g % 2) + 512], vb[0:n, g % 4, :], ACT.Copy) \
                    .then_inc(v_copied, 1)
            act.wait_ge(ln_centred, 1)
            act.activation(sq_ln[:, :, :], conv_y[:, :, :], ACT.Square).then_inc(ln_sq, 1)
            act.wait_ge(v_out_done, 16)

            def exps(n):
                sample = JOBS[n][1]
                act.wait_ge(neg_max, n + 1)
                if n >= 2:
                    act.wait_ge(prob_turned, n - 1)
                for lo_c, hi_c, c in JOB_COLS[sample]:
                    last = act.activation(ex[n % 2][:, lo_c:hi_c], sc[n % 2][:, lo_c:hi_c], ACT.Exp,
                                          bias=small[:, 6 * n + c:6 * n + c + 1])
                last.then_inc(exp_done, 1)

            def probs_out(n):
                sample = JOBS[n][1]
                act.wait_ge(prob_turned, n + 1)
                if n:
                    act.wait_ge(o_ready, n)
                if sample:
                    act.wait_ge(zero_ready, 2)
                    act.activation(zp[:, :, :].rearrange("p h (b x) -> p h b x", x=ZB)[:, :, :, 0:DS],
                                   vb[:, 2, 0:256].rearrange("p (h b s) -> p h b s", h=8, b=DB), ACT.Copy)
                    act.activation(pT[0:TS, 256:384], vb[0:TS, 2, 256:384], ACT.Copy).then_inc(pT_ready, 1)
                else:
                    act.activation(pT[:, :], vb[:, 2, 0:384], ACT.Copy).then_inc(pT_ready, 1)

            def attention_out(n):
                g, sample = JOBS[n]
                if sample:
                    act.wait_ge(o_rows, g + 1)
                    act.activation(o_row[:, :], vb[:, 3, 256:384], ACT.Copy).then_inc(o_rows_copied, 1)
                act.wait_ge(o_ready, n + 1)
                if sample:
                    act.activation(oT[:, 4 * g:4 * g + 4, SEQ:T],
                                   vb[:, 3, 256:384].rearrange("p (h t) -> p h t", h=4), ACT.Copy) \
                        .then_inc(o_copied, 1)
                else:
                    act.activation(oT[:, g, 0:SEQ], vb[:, 3, 0:256], ACT.Copy).then_inc(o_copied, 1)

            def ada_step(k):
                quad_hi(Q_ADA_MIXER + k + 1)
                if k % 2:
                    ada_out(ADA_FIRST + k // 2, k // 2 % 2)

            exps(0)
            root(zb[:, 1, 0:T], CT * P, ln_sqsum, 1)
            for n in range(len(JOBS)):
                ada = ada_steps(n)
                ada_step(ada[0])
                probs_out(n)
                ada_step(ada[1])
                if n + 1 < len(JOBS):
                    exps(n + 1)
                for k in ada[2:3]:
                    ada_step(k)
                attention_out(n)
                for k in ada[3:4]:
                    ada_step(k)
            act.wait_ge(o_copied, len(JOBS))
            act.activation(sq_at[:, :, :], oT, ACT.Square).then_inc(o_sq, 1)
            act.wait_ge(o_sum, 1)
            act.activation(sq_head[:, 0:4, :], zb[:, :, 0:T], ACT.Sqrt, bias=eps, scale=1.0 / E)
            act.activation(sq_head[:, 4:8, :], vb[:, :, 0:T], ACT.Sqrt, bias=eps, scale=1.0 / E) \
                .then_inc(root_ready, 1)
            act.wait_ge(ln_z, 1)
            for ct in range(CT):
                last = act.activation(conv_y[:, ct, :], conv_y[:, ct, :], ACT.Silu,
                                      bias=vecs[:, V_LNB + ct:V_LNB + ct + 1],
                                      scale=vecs[:, V_LNG + ct:V_LNG + ct + 1])
            last.then_inc(ln_out, 1)
            act.wait_ge(ln_out, 1)
            act.activation(act_hi[:, 0:CT, :], conv_y[:, :, :], ACT.Copy).then_inc(h_hi, 1)
            act.wait_ge(o_normed, 1)
            act.activation(act_hi[:, CT:KC, :], oT, ACT.Copy).then_inc(h_hi, 1)
            with act.Fori(0, KC // 2) as j:
                quad_hi(Q_OUT + 1 + j)
            act.wait_ge(x1_tile, KC // 2 + 1)
            act.activation(sq[:, :, :], xT[:, :, :], ACT.Square).then_inc(sq_ready, 1)
            root(vb[:, 0, 0:T], D, stat_ready, 2)
            act.wait_ge(h_ready, 2)
            act.activation(act_hi[:, :, :], hF[:, :, :], ACT.Copy).then_inc(h_hi, 1)
            act.wait_ge(h_split, 3)
            with act.Fori(0, KC // 4) as m:
                for b in range(2):
                    quad_hi(Q_WQ + 1 + 2 * m + b)
                    act.activation(qpT[:, bass.ds(4 * m + 2 * b, 2), :], zb[:, 2 * b:2 * b + 2, 0:T], ACT.Copy) \
                        .then_inc(qp_copied, 1)
            def score_copy(tt):
                n, banks = min(P, TOK_TILES[tt][1] * H // TOPK_HEADS[tt]), TOPK_HEADS[tt] // 2
                act.wait_ge(s_ready, tt + 1)
                if tt:
                    act.wait_ge(s_read, tt)
                act.activation(s_tm[0:n, 0:4 * banks, :].rearrange("p (b k) d -> p b (k d)", b=banks),
                               vb[0:n, 0:banks, :], ACT.Copy).then_inc(s_copied, 1)

            def gate_exp(tt):
                hn = TOPK_HEADS[tt]
                act.wait_ge(gate_in, tt + 1)
                act.activation(g_exp[:, 0:hn, :], g_exp[:, 0:hn, :], ACT.Exp).then_inc(gate_out, 1)

            def picks_out(tt):
                t0, n = TOK_TILES[tt]
                act.wait_ge(picks_turned, tt + 1)
                for c, dst, sign in ((0, i1T, 1.0), (1, i2T, 1.0), (2, gT, 1.0), (2, minus_gT, -1.0)):
                    act.activation(dst[:, t0:t0 + n], zb[:, 2, c * P:c * P + n], ACT.Copy, scale=sign) \
                        .then_inc(picks_copied, 1)

            def last_mods(k):
                n, b = ADA_FIRST + ADA_MIXER + k, k % 2
                act.wait_ge(row_turned, n + 3)
                for c in range(4):
                    last = act.activation(m_g5[:, 4 * k + c, :], zb[:, 3, 64 * b + NC * c:64 * b + NC * c + NC],
                                          ACT.Identity, bias=vecs[:, V_ADA + 4 * n + c:V_ADA + 4 * n + c + 1])
                last.then_inc(mods_ready, 1)

            def last_tile(k):
                quad_hi(Q_ADA_LAST + 2 * k + 1)
                if k:
                    last_mods(k - 1)
                quad_hi(Q_ADA_LAST + 2 * k + 2)
                ada_out(ADA_FIRST + ADA_MIXER + k, k % 2)

            score_copy(0)
            last_tile(0)
            score_copy(1)
            gate_exp(0)
            last_tile(1)
            picks_out(0)
            last_tile(2)
            score_copy(2)
            gate_exp(1)
            picks_out(1)
            last_tile(3)
            gate_exp(2)
            last_mods(3)
            picks_out(2)

            def one_hots(g, b):
                for t in range(8 - ON_ACT, 8):
                    last = act.activation(one1[b][:, t, :], iota, ACT.Abs, bias=i1T[:, bass.ds(8 * g + t, 1)],
                                          scale=-1.0)
                last.then_inc(distance, 1)
                act.wait_ge(distance, g + 1)
                for t in range(8 - ON_ACT, 8):
                    last = act.activation(one1[b][:, t, :], one1[b][:, t, :], ACT.Relu,
                                          bias=gT[:, bass.ds(8 * g + t, 1)], scale=minus_gT[:, bass.ds(8 * g + t, 1)])
                last.then_inc(one_act_ready, 1)

            def gate_block(blk, b, first, final=False):
                if not first:
                    act.wait_ge(g2_out[b], 8 * blk - 8 * b)
                for k in range(4):
                    g = 4 * blk + k
                    if not (final and k == 3):
                        act.wait_ge(g_ready, g + 2)
                        one_hots(g + 1, (k + 1) % 2)
                    act.wait_ge(g_ready, g + 3)
                    rows = vb[:, 2 * (k % 2):2 * (k % 2) + 2, :].rearrange("p a (t i) -> p (a t) i", t=4)
                    for half, out in enumerate((G[:, :, bass.ds(blk, 1), :, 8 * k:8 * k + 8]
                                                .rearrange("p c b e t -> p t (c b) e"),
                                                stage[b][:, :, :, 8 * k:8 * k + 8].rearrange("p c e t -> p t c e"))):
                        src = rows[:, :, HALF * half:HALF * (half + 1)].rearrange("p t (c e) -> p t c e", e=CHUNK)
                        last = act.activation(out, src, ACT.Copy)
                    last.then_inc(g_copied, 1)
                act.wait_ge(g_copied, 4 * blk + 6)
                act.dma_start(gates_d[blk], stage[b][:, :, :, :].rearrange("p c e t -> p c (e t)")) \
                    .then_inc(g2_out[b], 16)

            act.wait_ge(spilled, 16)
            act.wait_ge(picks_copied, 4 * 3)
            one_hots(0, 0)
            gate_block(0, 0, True)
            gate_block(1, 1, True)
            with act.Fori(0, (TBLKS - 3) // 2) as m:
                gate_block(2 * m + 2, 0, False)
                gate_block(2 * m + 3, 1, False)
            gate_block(TBLKS - 1, 0, False, True)

            def gelu(pair, b):
                act.wait_ge(w_ready, pair + 1)
                act.activation(gl[b][:, :, :], zb[:, 2 * b:2 * b + 2, 0:T], ACT.Gelu).then_inc(gelu_done, 1)

            def body(i, b):
                quad_hi(Q_PEER + 2 * i + 2)
                gelu(i + 1, (b + 1) % 2)
                quad_hi(Q_PEER + 2 * i + 3)

            quad_hi(Q_PEER + 1)
            gelu(0, 0)
            with act.Fori(0, (PAIRS - 2) // 2) as m:
                body(2 * m, 0)
                body(2 * m + 1, 1)
            body(PAIRS - 2, 0)
            for k in range(4):
                act.wait_ge(x2_ready, k + 1)
                act.activation(sq[:, 4 * k:4 * k + 4, :], x2[:, 4 * k:4 * k + 4, :], ACT.Square).then_inc(sq_ready, 1)
            root(zb[:, 0, 0:T], D, stat_ready, 3)
            for k in range(4):
                act.wait_ge(y_ready, k + 1)
                act.dma_start(y_d[:, 4 * k:4 * k + 4], fin[:, 4 * k:4 * k + 4, :]).then_inc(y_out, 16)

        @block.tensor
        def _(pe):
            pe.sem_inc(unit_used, 4)
            pe.sem_inc(row_turned, 2)
            pe.sem_inc(g_ready, 2)

            def channel_sum(out, src, chunks, done):
                for k in range(chunks):
                    last = pe.matmul(out, ones, src[:, k, :], start=(k == 0), stop=(k == chunks - 1))
                last.then_inc(done, 1)

            pe.wait_ge(consts_in, 16)
            pe.wait_ge(sq_ready, 1)
            channel_sum(vb[:, 2, 0:T], sq, KC, stat_ready)
            pe.wait_ge(c_ready, 2)
            sel = consts[0:2 * NC, K_SEL:K_SEL + NC]

            def ada_quad(q, n, b, part):
                if part == 0:
                    pe.wait_ge(row_copied, n + 1)
                for s in range(4):
                    k = 4 * part + s
                    pe.wait_ge(lo_ready, 4 * q + s + 5)
                    for j in range(2):
                        c = c_split[:, 2 * k + j, :]
                        pe.matmul(zb[0:2 * NC, b, :], c, hi[s][:, 512 * j:512 * j + 512],
                                  start=(k == 0 and j == 0), stop=False)
                        last = pe.matmul(zb[0:2 * NC, b, :], c, lo[s][:, 512 * j:512 * j + 512],
                                         start=False, stop=(k == 7 and j == 1))
                    last.then_inc(unit_used, 1)

            def turn_row(n, b):
                pe.wait_ge(row_copied, n + 3)
                pe.wait_ge(mods_ready, n + 2)
                for c in range(4):
                    at_c = 64 * b + NC * c
                    last = pe.matmul(zb[:, 3, at_c:at_c + NC], ada_row[b][:, c * P:(c + 1) * P], sel,
                                     start=True, stop=True)
                last.then_inc(row_turned, 1)

            def ada_tiles(q0, n0, count):
                def tile(n, b, first):
                    ada_quad(q0 + 2 * n, n0 + n, b, 0)
                    if not first:
                        turn_row(n0 + n - 1, 1 - b)
                    ada_quad(q0 + 2 * n + 1, n0 + n, b, 1)

                tile(0, 0, True)
                with pe.Fori(0, count // 2 - 1) as m:
                    tile(2 * m + 1, 1, False)
                    tile(2 * m + 2, 0, False)
                tile(count - 1, 1, False)
                turn_row(n0 + count - 1, 1)

            ada_tiles(0, 0, ADA_FIRST)
            pe.wait_ge(h_split, 1)
            with pe.Fori(0, CT // 2) as m:
                for b in range(2):
                    project(pe, Q_GLU + 2 * m + b, b, 2 * (2 * m + b))
            with pe.Fori(0, 6) as m:
                for b in range(2):
                    project(pe, Q_QKV + 2 * m + b, b, 2 * CT + 2 * (2 * m + b))

            pe.wait_ge(masks_in, 16)
            with pe.Fori(0, 4) as i:
                pe.wait_ge(qkv_evac, 2 * i + 2)
                pe.wait_ge(rope_done, i + 1)
                for t in range(4):
                    last = pe.matmul(vb[:, t, 0:T], masks[0:ROT, M_PERM:M_PERM + P],
                                     qkvT[0:ROT, 4 * i + t, :], start=True, stop=True)
                last.then_inc(rope_perm, 1)
            pe.wait_ge(qkv_evac, KV_PAIRS)
            pe.wait_ge(rope_done, 5)
            for g in range(6):
                t0, n = TOK_TILES[g // 2]
                if g >= 4:
                    pe.wait_ge(v_copied, g - 3)
                for h in range(4):
                    last = pe.transpose(vb[0:n, g % 4, P * h:P * h + P],
                                        qkvT[:, 2 * H + 4 * (g % 2) + h, t0:t0 + n], ident)
                last.then_inc(v_turned, 1)
            pe.wait_ge(conv_done, 1)
            channel_sum(zb[:, 0, 0:T], conv_y, CT, ln_sum)
            pe.wait_ge(v_copied, 6)

            def scores(n, part):
                g, sample = JOBS[n]
                if part == 0 and n >= 2:
                    pe.wait_ge(masked, n - 1)
                if not sample:
                    if part == 0:
                        q, k = qkvT[:, g, :], qkvT[:, H + g, :]
                        pe.matmul(vb[:, n % 2, 0:128], q[:, 0:128], k[:, 0:128], start=True, stop=True)
                        pe.matmul(vb[:, n % 2, 128:384], q[:, 128:256], k[:, 0:256], start=True, stop=True) \
                            .then_inc(score_ready, 1)
                    return
                pe.wait_ge(zq_ready, g + 1)
                for hb in range(4 * part, 4 * part + 4):
                    u = 16 * g + hb
                    pe.wait_ge(cache_in[u % 4], 16 * (u // 4) + 16)
                    h = hb // 2
                    for j in range(4):
                        b = 4 * (hb % 2) + j
                        last = pe.matmul(vb[TS * h:TS * h + TS, n % 2, 0:PAST], zq[:, h, TS * b:TS * b + TS],
                                         cache[u % 4][:, PAST * j:PAST * j + PAST],
                                         start=(b == 0), stop=(b == DB - 1))
                    last.then_inc(cache_used, 1)
                for h in range(2 * part, 2 * part + 2):
                    last = pe.matmul(vb[TS * h:TS * h + TS, n % 2, PAST:PAST + TS], qkvT[:, 4 * g + h, SEQ:T],
                                     qkvT[:, H + 4 * g + h, SEQ:T], start=True, stop=True)
                if part:
                    last.then_inc(score_ready, 1)

            def turn(n):
                sample = JOBS[n][1]
                pe.wait_ge(prob_ready, n + 1)
                if n:
                    pe.wait_ge(pT_ready, n)
                pe.transpose(vb[:, 2, 0:128], ex[n % 2][:, 0:128], ident)
                pe.transpose(vb[:, 2, 128:256], ex[n % 2][:, 128:256], ident)
                if sample:
                    last = pe.transpose(vb[0:TS, 2, 256:384], ex[n % 2][:, 256:288], ident)
                else:
                    last = pe.transpose(vb[:, 2, 256:384], ex[n % 2][:, 256:384], ident)
                last.then_inc(prob_turned, 1)

            def mix_values(n, part):
                g, sample = JOBS[n]
                if part == 0:
                    pe.wait_ge(pT_ready, n + 1)
                    if n:
                        pe.wait_ge(o_copied, n)
                if not sample:
                    if part == 0:
                        v = v_tok[:, :, P * g:P * g + P]
                        pe.matmul(vb[:, 3, 0:256], v[:, 0, :], pT[:, 0:256], start=True, stop=False)
                        pe.matmul(vb[:, 3, 128:256], v[:, 1, :], pT[:, 256:384], start=False, stop=True) \
                            .then_inc(o_ready, 1)
                    return
                for h in range(2 * part, 2 * part + 2):
                    out = vb[TS * h:TS * h + TS, 3, 256:384]
                    for bh in range(2):
                        u = 16 * g + 8 + 2 * h + bh
                        pe.wait_ge(cache_in[u % 4], 16 * (u // 4) + 16)
                        for j in range(4):
                            b = 4 * bh + j
                            for c in range(2):
                                last = pe.matmul(out, zp[:, 4 * c + h, TS * b:TS * b + TS],
                                                 cache[u % 4][:, 512 * c + P * j:512 * c + P * j + P],
                                                 start=(b == 0 and c == 0), stop=False)
                        last.then_inc(cache_used, 1)
                    last = pe.matmul(out, pT[0:TS, 256 + TS * h:256 + TS * h + TS],
                                     v_tok[0:TS, 2, P * (4 * g + h):P * (4 * g + h) + P], start=False, stop=True)
                if part:
                    last.then_inc(o_rows, 1)
                    pe.wait_ge(o_rows_copied, g + 1)
                    pe.transpose(vb[:, 3, 256:384], o_row[:, :], ident).then_inc(o_ready, 1)

            def ada_step(k):
                t = k // 2
                ada_quad(Q_ADA_MIXER + k, ADA_FIRST + t, t % 2, k % 2)
                if k and k % 2 == 0:
                    turn_row(ADA_FIRST + t - 1, (t - 1) % 2)

            scores(0, 0)
            pe.wait_ge(ln_sq, 1)
            channel_sum(zb[:, 1, 0:T], sq_ln, CT, ln_sqsum)
            pe.wait_ge(root_ready, 2)
            for n in range(len(JOBS)):
                ada, more = ada_steps(n), n + 1 < len(JOBS)
                if more:
                    scores(n + 1, 0)
                ada_step(ada[0])
                if more:
                    scores(n + 1, 1)
                turn(n)
                ada_step(ada[1])
                mix_values(n, 0)
                for k in ada[2:3]:
                    ada_step(k)
                mix_values(n, 1)
                for k in ada[3:4]:
                    ada_step(k)
            turn_row(ADA_FIRST + ADA_MIXER - 1, 1)
            pe.wait_ge(o_sq, 1)
            pe.wait_ge(mods_ready, ADA_FIRST + ADA_MIXER + 2)
            for h in range(H):
                bank = (zb if h < 4 else vb)[:, h % 4, 0:T]
                last = pe.matmul(bank, ones, sq_at[:, h, :], start=True, stop=True)
            last.then_inc(o_sum, 1)

            pe.wait_ge(h_split, 2)
            with pe.Fori(0, KC // 4) as m:
                for b in range(2):
                    project(pe, Q_OUT + 2 * m + b, b, 2 * (CT + 12) + 2 * (2 * m + b))
            pe.wait_ge(sq_ready, 2)
            channel_sum(vb[:, 0, 0:T], sq, KC, stat_ready)
            pe.wait_ge(h_split, 3)
            with pe.Fori(0, KC // 4) as m:
                for b in range(2):
                    project(pe, Q_WQ + 2 * m + b, b, 2 * (CT + 12 + KC // 2) + 2 * (2 * m + b))

            def key_scores(tt):
                t0, n = TOK_TILES[tt]
                per_row = 2 * TOPK_HEADS[tt]
                if tt:
                    pe.wait_ge(s_copied, tt)
                for hp in range(2 * H):
                    r0, at_hp = n * (hp // per_row), hp % per_row
                    last = pe.matmul(vb[r0:r0 + n, at_hp // 4, P * (at_hp % 4):P * (at_hp % 4) + P],
                                     qpT[:, hp, t0:t0 + n], keysT[:, hp, :], start=True, stop=True)
                last.then_inc(s_ready, 1)

            def turn_picks(tt):
                n, groups = TOK_TILES[tt][1], H // TOPK_HEADS[tt]
                m = P // groups
                pe.wait_ge(picks_ready, tt + 1)
                if tt:
                    pe.wait_ge(picks_copied, 4 * tt)
                for c in range(3):
                    for g in range(groups):
                        rows = slice(n * g, n * g + n)
                        last = pe.matmul(zb[m * g:m * g + m, 2, c * P:c * P + n], picks[rows, c, 0:m],
                                         ident[rows, rows], start=True, stop=True)
                last.then_inc(picks_turned, 1)

            def last_tile(k):
                n = ADA_FIRST + ADA_MIXER + k
                ada_quad(Q_ADA_LAST + 2 * k, n, k % 2, 0)
                if k:
                    turn_row(n - 1, 1 - k % 2)
                ada_quad(Q_ADA_LAST + 2 * k + 1, n, k % 2, 1)

            pe.wait_ge(qp_copied, KC // 2)
            pe.wait_ge(keys_in, 16)
            key_scores(0)
            key_scores(1)
            last_tile(0)
            key_scores(2)
            last_tile(1)
            turn_picks(0)
            last_tile(2)
            turn_picks(1)
            last_tile(3)
            turn_row(ADA_TILES - 1, 1)
            turn_picks(2)
            pe.wait_ge(picks_copied, 4 * 3)

            with pe.Fori(0, G_GROUPS // 2) as i:
                for b in range(2):
                    g = 2 * i + b
                    pe.wait_ge(g_copied, g + 1)
                    pe.wait_ge(one_ready, g + 1)
                    pe.wait_ge(one_act_ready, g + 1)
                    for t in range(8):
                        last = pe.matmul(vb[:, 2 * b + t // 4, NK * (t % 4):NK * (t % 4) + NK], one1[b][:, t, :],
                                         one2[b][:, t, :], start=True, stop=True)
                    last.then_inc(g_ready, 1)

            def mix_experts(i, b, q):
                pe.wait_ge(w_ready, i + 3)
                for s in range(4):
                    pe.wait_ge(lo_ready, 4 * q + s + 5)
                    for d in range(4):
                        if d % 2 == 0:
                            pe.wait_ge(vb_free, 16 * i + 4 * s + d + 1)
                        for e in range(2):
                            v_h = hi[s][:, 512 * e + P * d:512 * e + P * d + P]
                            v_l = lo[s][:, 512 * e + P * d:512 * e + P * d + P]
                            pe.matmul(vb[:, d, 0:T], v_h, w_hi[b][:, e, :], start=(e == 0), stop=False)
                            pe.matmul(vb[:, d, 0:T], v_h, w_lo[b][:, e, :], start=False, stop=False)
                            last = pe.matmul(vb[:, d, 0:T], v_l, w_hi[b][:, e, :], start=False, stop=(e == 1))
                        if d == 1:
                            last.then_inc(vb_ready, 1)
                    last.then_inc(unit_used, 1)

            def body(i, b):
                pe.wait_ge(gelu_done, i + 2)
                project(pe, Q_PEER + 2 * i + 1, (b + 1) % 2)
                mix_experts(i, b, Q_PEER + 2 * i + 2)

            pe.wait_ge(g_copied, G_GROUPS + 2)
            pe.wait_ge(gelu_done, 1)
            project(pe, Q_PEER, 0)
            with pe.Fori(0, (PAIRS - 2) // 2) as m:
                body(2 * m, 0)
                body(2 * m + 1, 1)
            body(PAIRS - 2, 0)
            mix_experts(PAIRS - 1, 1, Q_PEER + NK - 1)
            for k in range(KC):
                if k % 4 == 0:
                    pe.wait_ge(sq_ready, 3 + k // 4)
                last = pe.matmul(zb[:, 0, 0:T], ones, sq[:, k, :], start=(k == 0), stop=(k == KC - 1))
            last.then_inc(stat_ready, 1)

        @block.vector
        def _(dve):
            steps = [0]

            def mark(ins):
                steps[0] += 1
                return ins.then_inc(dve_step, 1)

            def settle():
                dve.wait_ge(dve_step, steps[0])

            def quad_lo(q):
                for s in range(4):
                    split_lo(dve, q, s)

            def inverse_rms(k):
                dve.wait_ge(root_ready, k)
                mark(dve.reciprocal(rs[:, :], rs[:, :]))
                settle()

            def times_rms():
                mark(dve.tensor_tensor(hF[:, :, :], xT[:, :, :], over(rs[:, :], KC), ALU.mult))
                settle()

            def modulate(op, by):
                mark(dve.tensor_tensor(hF[:, :, 0:SEQ], hF[:, :, 0:SEQ], by[:, :, 0:1].to_broadcast([P, KC, SEQ]), op))
                view = hF[:, :, SEQ:T].rearrange("p k (b s) -> p k b s", b=DB)
                return dve.tensor_tensor(view, view, by[:, :, 1:NC].unsqueeze(3).to_broadcast([P, KC, DB, DS]), op)

            def part_lo(k0, k1, src):
                return dve.tensor_tensor(act_lo[:, k0:k1, :], src, act_hi[:, k0:k1, :].bitcast(F32), ALU.subtract)

            dve.sem_inc(lo_ready, 4)
            dve.sem_inc(mods_ready, 2)
            dve.sem_inc(glu_ready, 1)
            dve.sem_inc(rope_done, 1)
            dve.sem_inc(vb_free, 4)
            dve.sem_inc(w_ready, 2)
            dve.sem_inc(x1_tile, 1)
            dve.wait_ge(silu_done, 1)
            dve.tensor_copy(c_split[:, :, 0:NC], cT[:, :, :]).then_inc(c_ready, 1)
            dve.wait_ge(c_ready, 1)
            dve.tensor_tensor(c_split[:, :, NC:2 * NC], cT[:, :, :], c_split[:, :, 0:NC].bitcast(F32), ALU.subtract) \
                .then_inc(c_ready, 1)
            dve.wait_ge(x_in, 16)
            inverse_rms(1)
            times_rms()
            quad_lo(0)
            dve.wait_ge(vecs_in, 16)

            def take_mods(n, b):
                dve.wait_ge(row_turned, n + 3)
                dve.tensor_tensor(mods[:, bass.ds(4 * n, 4), :],
                                  zb[:, 3, 64 * b:64 * b + 4 * NC].rearrange("p (c r) -> p c r", c=4),
                                  vecs[:, bass.ds(V_ADA + 4 * n, 4)].unsqueeze(2).to_broadcast([P, 4, NC]),
                                  ALU.add).then_inc(mods_ready, 1)

            def ada_tiles(q0, n0, count):
                def tile(n, b, first):
                    quad_lo(q0 + 2 * n + 1)
                    if not first:
                        take_mods(n0 + n - 1, 1 - b)
                    quad_lo(q0 + 2 * n + 2)

                tile(0, 0, True)
                with dve.Fori(0, count // 2 - 1) as m:
                    tile(2 * m + 1, 1, False)
                    tile(2 * m + 2, 0, False)
                tile(count - 1, 1, False)
                take_mods(n0 + count - 1, 1)

            ada_tiles(0, 0, ADA_FIRST)
            dve.wait_ge(mods_ready, ADA_FIRST + 2)

            def mod(i):
                return mods[:, KC * i:KC * i + KC, :]

            def scale_rows(out, i, g):
                mark(dve.scalar_tensor_tensor(out[:, :, :], mod(i), 1.0,
                                              vecs[:, g:g + KC].unsqueeze(2).to_broadcast([P, KC, NC]),
                                              ALU.add, ALU.mult))

            def gate_rows(out, i):
                mark(dve.tensor_scalar(out[:, :, :], mod(i), 1.0, None, ALU.add))

            scale_rows(m_a1, 1, V_G1)
            settle()
            mark(modulate(ALU.mult, m_a1))
            settle()
            modulate(ALU.add, mod(0)).then_inc(h_ready, 1)
            dve.wait_ge(h_hi, 1)
            part_lo(0, KC, hF[:, :, :]).then_inc(h_split, 1)

            dve.wait_ge(glu0_in, 16)
            with dve.Fori(0, CT // 2) as m:
                for b in range(2):
                    j = 2 * m + b
                    quad_lo(Q_GLU + 1 + j)
                    dve.wait_ge(sig_ready, j + 1)
                    row = glu[:, bass.ds(j, 1), :]
                    dve.tensor_tensor(row[:, :, HIST:GW_P], zb[:, 2 * b:2 * b + 1, 0:SEQ],
                                      sig[:, 0:SEQ].unsqueeze(1), ALU.mult).then_inc(z_half, 1)
                    new = row[:, :, GW_P:GW].rearrange("p c (b w) -> p (c b) w", b=DB)[:, :, HIST:GW_S]
                    dve.tensor_tensor(new, zb[:, 2 * b, SEQ:T].rearrange("p (b s) -> p b s", b=DB),
                                      sig[:, SEQ:T].rearrange("p (b s) -> p b s", b=DB), ALU.mult) \
                        .then_inc(glu_ready, 1)
                    dve.wait_ge(glu_ready, j + 2)
                    dve.sem_inc(z_free, 2)

            dve.wait_ge(z_half, CT)
            with dve.Fori(0, 2) as m:
                for k in range(6):
                    j = 6 * m + k
                    quad_lo(Q_QKV + 1 + j)
                    dve.wait_ge(qkv_evac, j + 1)
                    dve.sem_inc(z_free, 2)
                    for n in range(21 * k, min(21 * k + 21, 4 * CONV_W)):
                        w, c = n % (2 * CONV_W) // 2, 2 * (n // (2 * CONV_W)) + n % 2
                        ct = 4 * m + c
                        out = conv_y[:, bass.ds(ct, 1), 0:SEQ]
                        window = glu[:, bass.ds(ct, 1), w:w + SEQ]
                        tap = vecs[:, bass.ds(V_CW + CONV_W * ct + w, 1)]
                        if w == 0:
                            dve.tensor_scalar(out, window, tap, vecs[:, bass.ds(V_CB + ct, 1)], ALU.mult, ALU.add) \
                                .then_inc(conv_step, 1)
                        else:
                            dve.wait_ge(conv_step, 4 * CONV_W * m + n - 1)
                            dve.scalar_tensor_tensor(out, window, tap, out, ALU.mult, ALU.add).then_inc(conv_step, 1)
            dve.wait_ge(conv_s_done, CT)
            dve.tensor_tensor(conv_y[:, :, SEQ:T], conv_y[:, :, SEQ:T],
                              vecs[:, V_CB:V_CB + CT].unsqueeze(2).to_broadcast([P, CT, TS]), ALU.add) \
                .then_inc(conv_done, 1)

            dve.wait_ge(masks_in, 16)
            cos, sin = (over(masks[0:ROT, c:c + T], 4) for c in (M_RC, M_RS))
            with dve.Fori(0, 4) as i:
                rows = qkvT[0:ROT, bass.ds(4 * i, 4), :]
                dve.wait_ge(rope_perm, i + 1)
                dve.tensor_tensor(r_t[:, :, :], vb[0:ROT, :, 0:T], sin, ALU.mult).then_inc(rope_step, 1)
                dve.tensor_tensor(rows, rows, cos, ALU.mult).then_inc(rope_step, 1)
                dve.wait_ge(rope_step, 2 * i + 2)
                dve.tensor_tensor(rows, rows, r_t[:, :, :], ALU.add).then_inc(rope_done, 1)

            dve.wait_ge(ln_sum, 1)
            mark(dve.tensor_scalar(rs[:, :], zb[:, 0, 0:T], 1.0 / (CT * P), None, ALU.mult))
            settle()
            dve.tensor_tensor(conv_y[:, :, :], conv_y[:, :, :], over(rs[:, :], CT), ALU.subtract) \
                .then_inc(ln_centred, 1)

            def front(n):
                sample = JOBS[n][1]
                width, neg = (288, M_NS) if sample else (384, M_NP)
                if n >= 2:
                    dve.wait_ge(exp_done, n - 1)
                dve.wait_ge(score_ready, n + 1)
                dve.scalar_tensor_tensor(sc[n % 2][:, 0:width], vb[:, n % 2, 0:width], SCALE,
                                         masks[:, neg:neg + width], ALU.mult, ALU.add).then_inc(masked, 1)
                dve.wait_ge(masked, n + 1)
                for c0, c1, c in JOB_COLS[sample]:
                    last = dve.tensor_reduce(small[:, 6 * n + c:6 * n + c + 1], sc[n % 2][:, c0:c1], AX_X, ALU.max,
                                             negate=True)
                last.then_inc(neg_max, 1)

            def back(n):
                sample = JOBS[n][1]
                cnt = M_CS if sample else M_CP
                dve.wait_ge(exp_done, n + 1)
                for c0, c1, c in JOB_COLS[sample]:
                    col = small[:, 6 * n + c + 2:6 * n + c + 3]
                    mark(dve.tensor_tensor_reduce(ex[n % 2][:, c0:c1], ex[n % 2][:, c0:c1],
                                                  masks[:, cnt + c0:cnt + c1], 1.0, 0.0, ALU.mult, ALU.add, col))
                settle()
                for c0, c1, c in JOB_COLS[sample]:
                    mark(dve.reciprocal(small[:, 6 * n + c + 4:6 * n + c + 5], small[:, 6 * n + c + 2:6 * n + c + 3]))
                settle()
                for c0, c1, c in JOB_COLS[sample]:
                    last = dve.tensor_scalar(ex[n % 2][:, c0:c1], ex[n % 2][:, c0:c1],
                                             small[:, 6 * n + c + 4:6 * n + c + 5], None, ALU.mult)
                last.then_inc(prob_ready, 1)

            front(0)
            inverse_rms(2)
            dve.tensor_tensor(conv_y[:, :, :], conv_y[:, :, :], over(rs[:, :], CT), ALU.mult).then_inc(ln_z, 1)
            def ada_step(k):
                quad_lo(Q_ADA_MIXER + k + 1)
                if k and k % 2 == 0:
                    take_mods(ADA_FIRST + k // 2 - 1, (k // 2 - 1) % 2)

            for n in range(len(JOBS)):
                ada = ada_steps(n)
                ada_step(ada[0])
                back(n)
                ada_step(ada[1])
                if n + 1 < len(JOBS):
                    front(n + 1)
                for k in ada[2:4]:
                    ada_step(k)
            take_mods(ADA_FIRST + ADA_MIXER - 1, 1)
            dve.wait_ge(mods_ready, ADA_FIRST + ADA_MIXER + 2)
            scale_rows(m_a2, 4, V_G2)
            gate_rows(m_g2, 2)
            dve.wait_ge(root_ready, 3)
            mark(dve.reciprocal(sq_head[:, :, :], sq_head[:, :, :]))
            settle()
            for h in range(H):
                last = dve.scalar_tensor_tensor(oT[:, h, :], oT[:, h, :], vecs[:, V_AG + h:V_AG + h + 1],
                                                sq_head[:, h, :], ALU.mult, ALU.mult)
            last.then_inc(o_normed, 1)
            dve.wait_ge(h_hi, 2)
            part_lo(0, CT, conv_y[:, :, :])
            dve.wait_ge(h_hi, 3)
            dve.wait_ge(o_normed, 1)
            part_lo(CT, KC, oT).then_inc(h_split, 1)

            with dve.Fori(0, KC // 4) as m:
                for b in range(2):
                    j = 2 * m + b
                    quad_lo(Q_OUT + 1 + j)
                    dve.wait_ge(unit_used, 4 * (Q_OUT + j) + 8)
                    for t in range(2):
                        gate = m_g2[:, bass.ds(2 * j + t, 1), 0]
                        x = xT[:, bass.ds(2 * j + t, 1), 0:SEQ]
                        dve.scalar_tensor_tensor(x, zb[:, 2 * b + t:2 * b + t + 1, 0:SEQ], gate, x, ALU.mult, ALU.add)
                    dve.wait_ge(x1_tile, j + 1)
                    for t in range(2):
                        gate = m_g2[:, bass.ds(2 * j + t, 1), 1:NC].rearrange("p k b -> p (k b)")
                        last = dve.tensor_tensor(tmp_s[:, t, :].rearrange("p (b s) -> p b s", b=DB),
                                                 zb[:, 2 * b + t, SEQ:T].rearrange("p (b s) -> p b s", b=DB),
                                                 gate.unsqueeze(2).to_broadcast([P, DB, DS]), ALU.mult)
                    last.then_inc(x1_step, 1)
                    dve.wait_ge(x1_step, j + 1)
                    dve.sem_inc(z_free, 2)
                    x = xT[:, bass.ds(2 * j, 2), SEQ:T]
                    dve.tensor_tensor(x, x, tmp_s[:, :, :], ALU.add).then_inc(x1_tile, 1)
            dve.wait_ge(x1_tile, KC // 2 + 1)
            dve.wait_ge(k_out_done, 16)
            inverse_rms(4)
            times_rms()
            mark(modulate(ALU.mult, m_a2))
            settle()
            modulate(ALU.add, mod(3)).then_inc(h_ready, 1)
            dve.wait_ge(h_hi, 4)
            dve.wait_ge(h_ready, 2)
            part_lo(0, KC, hF[:, :, :]).then_inc(h_split, 1)
            with dve.Fori(0, KC // 2) as j:
                quad_lo(Q_WQ + 1 + j)
                dve.wait_ge(qp_copied, j + 1)
                dve.sem_inc(z_free, 2)

            for tt, hn in enumerate(TOPK_HEADS):
                dve.wait_ge(s_copied, tt + 1)
                for hp in range(2 * hn):
                    mark(dve.max(sv[:, hp, 0:8], s_tm[:, hp, :]))
                settle()
                for hp in range(2 * hn):
                    dve.max_index(si_u[:, hp, 0:8], sv[:, hp, 0:8], s_tm[:, hp, :])
                    last = dve.match_replace(s_work[:, hp, :], sv[:, hp, 0:8], s_tm[:, hp, :], NEG)
                last.then_inc(s_read, 1)
                dve.wait_ge(s_read, tt + 1)
                for hp in range(2 * hn):
                    mark(dve.max(sv[:, hp, 8:16], s_work[:, hp, :]))
                settle()
                for hp in range(2 * hn):
                    last = dve.max_index(si_u[:, hp, 8:16], sv[:, hp, 8:16], s_work[:, hp, :])
                mark(last)
                s4 = sv[:, 0:2 * hn, :].rearrange("n (h p) k -> n h p k", p=2)
                mark(dve.tensor_tensor(cand[:, 0:hn, :].rearrange("n h (a b) -> n h a b", a=TOPK),
                                       s4[:, :, 0, :].unsqueeze(3).to_broadcast([P, hn, TOPK, TOPK]),
                                       s4[:, :, 1, :].unsqueeze(2).to_broadcast([P, hn, TOPK, TOPK]), ALU.add))
                settle()
                mark(dve.tensor_copy(si_f[:, 0:2 * hn, :], si_u[:, 0:2 * hn, :]))
                fi3 = fi_u[:, :].rearrange("n (h k) -> n h k", h=H)
                for h in range(hn):
                    mark(dve.max(fv[:, h, 0:8], cand[:, h, :]))
                settle()
                for h in range(hn):
                    dve.max_index(fi3[:, h, 0:8], fv[:, h, 0:8], cand[:, h, :])
                    mark(dve.match_replace(c_work[:, h, :], fv[:, h, 0:8], cand[:, h, :], NEG))
                settle()
                for h in range(hn):
                    mark(dve.max(fv[:, h, 8:16], c_work[:, h, :]))
                settle()
                for h in range(hn):
                    mark(dve.max_index(fi3[:, h, 8:16], fv[:, h, 8:16], c_work[:, h, :]))
                dve.tensor_tensor(g_exp[:, 0:hn, :], fv[:, 0:hn, :], fv[:, 0:hn, 0:1].to_broadcast([P, hn, TOPK]),
                                  ALU.subtract).then_inc(gate_in, 1)
                settle()
                mark(dve.tensor_single_scalar(f_au[:, 0:hn * TOPK], fi_u[:, 0:hn * TOPK], 4, ALU.logical_shift_right))
                mark(dve.tensor_single_scalar(f_bu[:, 0:hn * TOPK], fi_u[:, 0:hn * TOPK], 15, ALU.bitwise_and))
                settle()
                mark(dve.tensor_copy(f_a[:, 0:hn * TOPK], f_au[:, 0:hn * TOPK]))
                mark(dve.tensor_copy(f_b[:, 0:hn * TOPK], f_bu[:, 0:hn * TOPK]))
                if tt:
                    dve.wait_ge(picks_turned, tt)
                settle()
                io16 = over(consts[:, K_IO16:K_IO16 + TOPK], hn * TOPK)
                si4 = si_f[:, 0:2 * hn, :].rearrange("n (h p) k -> n h p k", p=2)
                for p, f in enumerate((f_a, f_b)):
                    mark(dve.tensor_tensor(oh[:, 0:hn * TOPK, :], f[:, 0:hn * TOPK].unsqueeze(2).to_broadcast([P, hn * TOPK, TOPK]),
                                           io16, ALU.is_equal))
                    settle()
                    oh4 = oh[:, 0:hn * TOPK, :].rearrange("n (h k) a -> n h k a", h=hn)
                    mark(dve.tensor_tensor(oh4, oh4, si4[:, :, p, :].unsqueeze(2).to_broadcast([P, hn, TOPK, TOPK]),
                                           ALU.mult))
                    settle()
                    mark(dve.tensor_reduce(picks[:, p, 0:hn * TOPK], oh[:, 0:hn * TOPK, :], AX_X, ALU.add))
                    settle()
                dve.wait_ge(gate_out, tt + 1)
                mark(dve.tensor_reduce(small[:, 0:hn], g_exp[:, 0:hn, :], AX_X, ALU.add))
                settle()
                mark(dve.reciprocal(small[:, H:H + hn], small[:, 0:hn]))
                settle()
                dve.tensor_tensor(picks[:, 2, 0:hn * TOPK].rearrange("n (h k) -> n h k", h=hn), g_exp[:, 0:hn, :],
                                  small[:, H:H + hn].unsqueeze(2).to_broadcast([P, hn, TOPK]), ALU.mult) \
                    .then_inc(picks_ready, 1)

            dve.wait_ge(mods_ready, ADA_TILES + 2)
            mark(dve.tensor_scalar(m_g5[:, :, :], m_g5[:, :, :], 1.0, None, ALU.add))
            dve.wait_ge(picks_copied, 4 * 3)
            with dve.Fori(0, G_GROUPS // 2) as i:
                for b in range(2):
                    g = 2 * i + b
                    dve.wait_ge(g_ready, g + 1)
                    for t in range(8 - ON_ACT):
                        dve.tensor_scalar(one1[b][:, t, :], iota, i1T[:, bass.ds(8 * g + t, 1)],
                                          gT[:, bass.ds(8 * g + t, 1)], ALU.is_equal, ALU.mult)
                    dve.tensor_tensor(one2[b][:, :, :], over(iota, 8),
                                      i2T[:, bass.ds(8 * g, 8)].unsqueeze(2).to_broadcast([P, 8, NK]),
                                      ALU.is_equal).then_inc(one_ready, 1)

            def weigh(pair, b, chunk):
                dve.wait_ge(gelu_done, pair + 3)
                dve.wait_ge(w_ready, pair + 2)
                gates = G[:, bass.ds(chunk, 1), :, 2 * b:2 * b + 2, :].rearrange("p c b e t -> p e (c b) t")
                values = gl[b][:, :, :].rearrange("p e (b t) -> p e b t", t=TB)
                for out in (w_f, w_hi[b]):
                    last = dve.tensor_tensor(out[:, :, :].rearrange("p e (b t) -> p e b t", t=TB), values, gates,
                                             ALU.mult)
                last.then_inc(w_mid, 1)
                dve.wait_ge(w_mid, pair + 1)
                dve.tensor_tensor(w_lo[b][:, :, :], w_f[:, :, :], w_hi[b][:, :, :].bitcast(F32), ALU.subtract) \
                    .then_inc(w_ready, 1)

            def add_sums(pair, q, s, q_next):
                for d in range(2):
                    if d == 0:
                        dve.wait_ge(vb_ready, 4 * pair + s + 1)
                    else:
                        if s and q_next is not None:
                            split_lo(dve, q_next, s - 1)
                        dve.wait_ge(unit_used, 4 * q + s + 5)
                    out = acc[:, 4 * s + 2 * d:4 * s + 2 * d + 2, :]
                    dve.tensor_tensor(out, out, vb[:, 2 * d:2 * d + 2, 0:T], ALU.add).then_inc(vb_free, 2)

            def body(i, b, chunk):
                weigh(i, b, chunk)
                quad_lo(Q_PEER + 2 * i + 2)
                for s in range(4):
                    add_sums(i, Q_PEER + 2 * i + 2, s, Q_PEER + 2 * i + 3)
                split_lo(dve, Q_PEER + 2 * i + 3, 3)

            dve.wait_ge(g_copied, G_GROUPS + 2)
            dve.wait_ge(lo_ready, 4 * Q_PEER + 8)
            quad_lo(Q_PEER + 1)
            dve.wait_ge(acc_zero, 1)
            with dve.Fori(0, CHUNKS) as c:
                body(2 * c, 0, c)
                body(2 * c + 1, 1, c)
            with dve.Fori(0, CHUNKS - 1) as c:
                dve.wait_ge(g2_in, 16 * c + 16)
                body(2 * c + 2 * CHUNKS, 0, c)
                body(2 * c + 2 * CHUNKS + 1, 1, c)
            dve.wait_ge(g2_in, 16 * CHUNKS)
            body(PAIRS - 2, 0, CHUNKS - 1)
            weigh(PAIRS - 1, 1, CHUNKS - 1)
            dve.wait_ge(x1_in, 16)
            for s in range(4):
                add_sums(PAIRS - 1, Q_PEER + NK - 1, s, None)
                dve.wait_ge(vb_free, 16 * (PAIRS - 1) + 4 * s + 8)
                ks = slice(4 * s, 4 * s + 4)
                for k in range(4 * s, 4 * s + 4):
                    mark(dve.scalar_tensor_tensor(x2[:, k, 0:SEQ], acc[:, k, 0:SEQ], m_g5[:, k, 0:1], x2[:, k, 0:SEQ],
                                                  ALU.mult, ALU.add))
                new = acc[:, ks, SEQ:T].rearrange("p k (b s) -> p k b s", b=DB)
                mark(dve.tensor_tensor(new, new, m_g5[:, ks, 1:NC].unsqueeze(3).to_broadcast([P, 4, DB, DS]), ALU.mult))
                settle()
                dve.tensor_tensor(x2[:, ks, SEQ:T], x2[:, ks, SEQ:T], acc[:, ks, SEQ:T], ALU.add).then_inc(x2_ready, 1)
            inverse_rms(5)
            for k in range(KC):
                last = dve.scalar_tensor_tensor(fin[:, k, :], x2[:, k, :], vecs[:, V_GF + k:V_GF + k + 1], rs[:, :],
                                                ALU.mult, ALU.mult)
                if k % 4 == 3:
                    last.then_inc(y_ready, 1)


_OUTS = [("y", (P, KC, T)), ("k", (P, H, T)), ("v", (P, H, T)), ("conv_p", (P, CT, HIST)),
         ("conv_s", (P, CT, DB, HIST))]


def kernel(**a):
    import numpy as np
    import concourse.bacc as bacc
    from concourse.bass_utils import run_bass_kernel_spmd

    a = {k: np.asarray(v) for k, v in a.items()}

    def channels(x, *rest):
        return x.reshape(-1, x.shape[-1] // P, P).transpose(2, 1, 0)

    def tiles(w):
        return w.reshape(KC, P, -1, P).transpose(2, 1, 0, 3).reshape(-1, P, KC * P)

    x = np.concatenate([a["x_prompt"].reshape(SEQ, D), a["x_sample"].reshape(TS, D)])
    c = np.concatenate([a["c_prompt"], a["c_sample"]])
    glu0 = np.zeros((P, CT, GW), np.float32)
    hist = a["state_conv"][0].reshape(DB, HIST, CT, P).transpose(3, 2, 0, 1)
    glu0[:, :, GW_P:].reshape(P, CT, DB, GW_S)[..., :HIST] = hist
    w_in = tiles(a["w_in"][0])
    order = [t for j in range(CT) for t in (j, CT + j)] + list(range(2 * CT, 2 * CT + 3 * H))
    ck = a["cache_k"][0].reshape(2, 4, PAST, H, E).transpose(3, 0, 4, 1, 2).reshape(H, 2, E, UNIT)
    cv = a["cache_v"][0].reshape(2, 4, 2, P, H, E).transpose(4, 0, 3, 2, 1, 5).reshape(H, 2, P, UNIT)
    u = a["peer_u"][0].reshape(NK, NK, KC, P).transpose(1, 3, 2, 0).reshape(NK, P, KC * P)

    vecs = np.zeros((P, V_N), np.float32)
    for at, v in ((V_G1, a["norm1_g"]), (V_G2, a["norm2_g"]), (V_GF, a["final_g"]), (V_LNG, a["conv_ln_g"]),
                  (V_LNB, a["conv_ln_b"]), (V_CB, a["conv_b"]), (V_AG, a["attn_out_g"]), (V_ADA, a["b_ada"])):
        n = v.size // P
        vecs[:, at:at + n] = v.reshape(n, P).T
    vecs[:, V_CW:V_ADA] = a["conv_w"][0].reshape(CONV_W, CT, P).transpose(2, 1, 0).reshape(P, -1)

    consts = np.zeros((P, K_N), np.float32)
    consts[:, K_ID:K_ID + P] = np.eye(P)
    consts[:, K_ONE:K_ONE + P] = 1.0
    consts[:, K_IOTA:K_IOTA + NK] = np.arange(NK)
    consts[:2 * NC, K_SEL:K_SEL + NC] = np.tile(np.eye(NC), (2, 1))
    consts[:, K_IO16:K_IO16 + TOPK] = np.arange(TOPK)
    consts[:, K_EPS] = EPS

    def patterns(d):
        return sum(((d >= 0) & (d % dil == 0) & (d // dil <= win // dil)).astype(np.float32)
                   for win, dil in ((128, 1), (512, 4), (2048, 16)))

    masks = np.zeros((P, M_N), np.float32)
    r = np.arange(P)[:, None]
    prompt = np.concatenate([patterns(r - r.T), patterns(128 + r - np.arange(256)[None])], axis=1)
    b, s = r // DS % DB, r % DS
    new = np.arange(TS)[None]
    sample = np.concatenate([patterns(PAST + s - np.arange(PAST)[None]),
                             patterns(s - new % DS) * (b == new // DS)], axis=1)
    for cnt, neg, m in ((M_CP, M_NP, prompt), (M_CS, M_NS, sample)):
        masks[:, cnt:cnt + m.shape[1]] = m
        masks[:, neg:neg + m.shape[1]] = np.where(m > 0, 0.0, -1e30)
    pos = np.concatenate([np.arange(SEQ), PAST + np.arange(TS) % DS]).astype(np.float32)
    inv = np.float32(500000.0) ** (-np.arange(0, ROT, 2, dtype=np.float32) / np.float32(ROT))
    ang = (pos[None] * inv[:, None]).astype(np.float32)
    masks[:ROT, M_RC:M_RC + T] = np.tile(np.cos(ang), (2, 1))
    masks[:ROT // 2, M_RS:M_RS + T] = -np.sin(ang)
    masks[ROT // 2:ROT, M_RS:M_RS + T] = np.sin(ang)
    masks[np.arange(ROT), M_PERM + (np.arange(ROT) + ROT // 2) % ROT] = 1.0

    ins = {
        "xT": channels(x), "cT": channels(c), "glu0": glu0,
        "w_ada": a["w_ada"][0].reshape(8, 2, P, ADA_TILES, 512).transpose(3, 0, 2, 1, 4).reshape(ADA_TILES, 8, P, UNIT),
        "w_in": w_in[order], "w_out": tiles(a["w_out"][0]), "w_q": tiles(a["peer_wq"][0]),
        "keys": a["peer_keys"][0].reshape(2 * H, NK, P).transpose(2, 0, 1),
        "u": u, "v": a["peer_v"][0].reshape(NK, NK, D), "ck": ck, "cv": cv,
        "vecs": vecs, "consts": consts, "masks": masks,
    }
    nc = bacc.Bacc("TRN2", target_bir_lowering=False, num_devices=1)
    ins = {f"in_{k}": np.ascontiguousarray(v) for k, v in ins.items()}
    args = [nc.dram_tensor(k, v.shape, F32, kind="ExternalInput").ap() for k, v in ins.items()]
    args += [nc.dram_tensor(f"out_{k}", s, F32, kind="ExternalOutput").ap() for k, s in _OUTS]
    layer_kernel(nc, *args)
    got = run_bass_kernel_spmd(nc, [ins], core_ids=[0]).results[0]

    y = got["out_y"].transpose(2, 1, 0).reshape(T, D)
    k, v = (got[f"out_{n}"].transpose(2, 1, 0) for n in "kv")
    conv_p = got["out_conv_p"].transpose(2, 1, 0).reshape(1, 1, HIST, CT * P)
    conv_s = got["out_conv_s"].transpose(2, 3, 1, 0).reshape(1, DB, HIST, CT * P)
    y, k, v, conv_p, conv_s = (np.ascontiguousarray(z) for z in (y, k, v, conv_p, conv_s))
    return (y[:SEQ].reshape(1, SEQ, D), y[SEQ:].reshape(DB, DS, D),
            k[:SEQ].reshape(1, 1, SEQ, H, E), v[:SEQ].reshape(1, 1, SEQ, H, E), conv_p,
            k[SEQ:].reshape(1, DB, DS, H, E), v[SEQ:].reshape(1, DB, DS, H, E), conv_s)
```

```python
from contextlib import ExitStack

import concourse.bass as bass
from concourse import mybir

F32 = mybir.dt.float32
F32R = mybir.dt.float32r
U32 = mybir.dt.uint32
ALU = mybir.AluOpType
ACT = mybir.ActivationFunctionType
AX_X = mybir.AxisListType.X

P = 128
D = 2048
KC = D // P
SEQ = 256
DB, DS = 8, 4
TS = DB * DS
T = SEQ + TS
NC = 1 + DB
PAST = 256
CONV_W = 31
HIST = CONV_W - 1
CT = 8
CT_POOL = 2
CT_TURN = (CT - CT_POOL) // 2
GW_P = HIST + SEQ
GW_S = HIST + DS
GW = GW_P + DB * GW_S
H = 8
E = 128
ROT = 32
SCALE = float(E) ** -0.5
EPS = 1e-6
N_ADA = 6
TOPK = 16
NK = 128
HALF = NK // 2
TB = 32
TBLKS = T // TB
CHUNK = 4
CHUNKS = HALF // CHUNK
NEG = -3.0e38
UNIT = 1024
TOK_TILES = ((0, 128), (128, 128), (256, 32))
TOPK_HEADS = (8, 8, 2)

ADA_TILES = N_ADA * D // 512
ADA_FIRST = 8
ADA_MIXER = 12
ADA_LAST = ADA_TILES - ADA_FIRST - ADA_MIXER
Q_GLU = 2 * ADA_FIRST
Q_QKV = Q_GLU + CT
Q_ADA_MIXER = Q_QKV + 12
Q_OUT = Q_ADA_MIXER + 2 * ADA_MIXER
Q_WQ = Q_OUT + KC // 2
Q_ADA_LAST = Q_WQ + KC // 2
Q_PEER = Q_ADA_LAST + 2 * ADA_LAST
PAIRS = NK // 2
KV_PAIRS = 3 * H // 2
G_GROUPS = T // 8
ON_ACT = 2

ZB = TS + DS

JOBS = [(0, 0), (1, 0), (2, 0), (3, 0), (0, 1), (4, 0), (5, 0), (6, 0), (7, 0), (1, 1)]
SILU_JOBS = 4
ADA_BESIDE = (1, 1, 1, 1, 2, 1, 1, 1, 1, 2)


def ada_steps(n):
    return range(2 * sum(ADA_BESIDE[:n]), 2 * sum(ADA_BESIDE[:n + 1]))


JOB_COLS = (((0, 128, 0), (128, 384, 1)), ((0, 288, 0),))

V_G1, V_G2, V_GF = 0, 16, 32
V_LNG, V_LNB, V_CB, V_AG = 48, 56, 64, 72
V_CW = 80
V_ADA = V_CW + CT * CONV_W
V_N = V_ADA + N_ADA * KC

K_ID, K_ONE, K_IOTA, K_SEL, K_IO16 = 0, 128, 256, 384, 394
K_EPS = 410
K_HEAD = 411
K_N = K_HEAD + 2 * H - 1
M_CP, M_NP, M_CS, M_NS, M_RC, M_RS, M_PERM = 0, 384, 768, 1056, 1344, 1632, 1920
M_N = M_PERM + P


def layer_kernel(nc, xT_d, cT_d, glu0_d, w_ada_d, w_in_d, w_out_d, w_q_d, keys_d, u_d, v_d, ck_d, cv_d,
                 vecs_d, consts_d, masks_d, y_d, k_out, v_out, convp_out, convs_out):
    spill_d = nc.dram_tensor("x1_spill", [P, KC * T], F32).ap()
    gates_d = nc.dram_tensor("gates_2nd", [TBLKS, P, CHUNKS, CHUNK * TB], F32).ap()

    base = [16512]

    def at(name, shape, dt, offset):
        return nc.alloc_sbuf_tensor_at(name, shape, dt, offset=offset)

    def sb(name, shape, dt=F32):
        n = 4
        for s in shape[1:]:
            n *= s
        t = at(name, shape, dt, base[0])
        base[0] += (n + 63) // 64 * 64
        return t

    raw = [sb(f"raw{s}", [P, UNIT]) for s in range(4)]
    hi = [sb(f"hi{s}", [P, UNIT], F32R) for s in range(4)]
    lo = [sb(f"lo{s}", [P, UNIT], F32R) for s in range(4)]
    act_hi_at = base[0]
    act_hi = sb("act_hi", [P, KC, T], F32R)
    act_lo = sb("act_lo", [P, KC, T], F32R)
    x_at = base[0]
    xT = sb("xT", [P, KC, T])
    mods_at = base[0]
    mods = sb("mods", [P, N_ADA * KC, NC])
    vecs = sb("vecs", [P, V_N])
    consts = sb("consts", [P, K_N])
    rs = sb("rs", [P, T])
    m_a1 = sb("m_a1", [P, KC, NC])
    m_a2 = sb("m_a2", [P, KC, NC])
    m_g2 = sb("m_g2", [P, KC, NC])
    m_g5 = sb("m_g5", [P, KC, NC])
    tmp_s = sb("tmp_s", [P, 2, TS])
    small = sb("small", [P, 64])
    cT = sb("cT", [P, KC, NC])
    c_split = sb("c_split", [P, KC, 2 * NC], F32R)
    ada_row = [sb(f"ada_row{b}", [2 * NC, 512]) for b in range(2)]
    zone = base[0]

    glu = at("glu", [P, CT, GW], F32, zone)
    cache = [at(f"cache{s}", [P, UNIT], F32, zone + 4096 * s) for s in range(4)]
    conv_y = at("conv_y", [P, CT, T], F32, zone + 17920)
    qkvT = at("qkvT", [P, 3 * H, T], F32, zone + 27136)
    v_tok = at("v_tok", [P, 3, H * E], F32, zone + 54784)
    sc = [at(f"sc{b}", [P, 384], F32, zone + 67072 + 1536 * b) for b in range(2)]
    ex = [at(f"ex{b}", [P, 384], F32, zone + 70144 + 1536 * b) for b in range(2)]
    pT = at("pT", [P, 384], F32, zone + 73216)
    o_row = at("o_row", [P, P], F32, zone + 74752)
    prod = at("prod", [P, TS, CONV_W], F32, zone + 67072)
    sig = at("sig", [P, T], F32, zone + 71040)
    conv_p = [at(f"conv_p{b}", [P, CT_POOL, SEQ], F32, zone + 72192 + 2048 * b) for b in range(2)]
    masks = at("masks", [P, M_N], F32, zone + 76288)
    zq = at("zq", [P, 4, DB * ZB], F32, zone + 84480)
    keysT = at("keysT", [P, 2 * H, NK], F32, zone + 78592)
    r_t = at("r_t", [ROT, 4, T], F32, zone + 84480)
    head_inv = at("head_inv", [H, T], F32, zone + 27136)
    head_rows = at("head_rows", [H, H, P], F32, zone + 67072)
    sq = at("sq", [P, KC, T], F32, act_hi_at)
    sq_ln = at("sq_ln", [P, CT, T], F32, act_hi_at)
    zp = at("zp", [P, 2 * 4, DB * ZB], F32, act_hi_at + 9216)
    sq_at = at("sq_at", [P, H, T], F32, act_hi_at + 18432 + 9216)
    hF = at("hF", [P, KC, T], F32, zone + 27136)
    oT = qkvT[:, 2 * H:3 * H, :]
    qpT = at("qpT", [P, KC, T], F32, zone)
    s_tm = at("s_tm", [P, 2 * H, NK], F32, zone + 18432)
    s_work = at("s_work", [P, 2 * H, NK], F32, zone + 45568)
    cand = at("cand", [P, H, 256], F32, zone + 53760)
    c_work = at("c_work", [P, H, 256], F32, zone + 61952)
    oh = at("oh", [P, H * TOPK, TOPK], F32, zone + 26624)
    sv = at("sv", [P, 2 * H, TOPK], F32, zone + 70144)
    si_u = at("si_u", [P, 2 * H, TOPK], U32, zone + 71168)
    si_f = at("si_f", [P, 2 * H, TOPK], F32, zone + 72192)
    fv = at("fv", [P, H, TOPK], F32, zone + 73216)
    fi_u = at("fi_u", [P, H * TOPK], U32, zone + 73728)
    f_au = at("f_au", [P, H * TOPK], U32, zone + 74240)
    f_bu = at("f_bu", [P, H * TOPK], U32, zone + 74752)
    f_a = at("f_a", [P, H * TOPK], F32, zone + 75264)
    f_b = at("f_b", [P, H * TOPK], F32, zone + 75776)
    picks = at("picks", [P, 3, H * TOPK], F32, zone + 76288)
    g_exp = at("g_exp", [P, H, TOPK], F32, zone + 77824)
    G = at("G", [P, CHUNKS, TBLKS, CHUNK, TB], F32, zone)
    w_hi = [at(f"w_hi{b}", [P, 2, T], F32R, zone + 73728 + 2304 * b) for b in range(2)]
    w_lo = [at(f"w_lo{b}", [P, 2, T], F32R, zone + 78336 + 2304 * b) for b in range(2)]
    w_f = at("w_f", [P, 2, T], F32, zone + 82944)
    gl = [at(f"gl{b}", [P, 2, T], F32, zone + 85248 + 2304 * b) for b in range(2)]
    one1 = [at(f"one1_{b}", [P, 8, NK], F32, zone + 73728 + 4096 * b) for b in range(2)]
    one2 = [at(f"one2_{b}", [P, 8, NK], F32, zone + 81920 + 4096 * b) for b in range(2)]
    stage = [at(f"stage{b}", [P, CHUNKS, CHUNK, TB], F32, x_at + 8192 * b) for b in range(2)]
    i1T = at("i1T", [P, T], F32, mods_at)
    i2T = at("i2T", [P, T], F32, mods_at + 4 * T)
    gT = at("gT", [P, T], F32, mods_at + 8 * T)
    minus_gT = at("minus_gT", [P, T], F32, zone + 90112)
    acc = at("acc", [P, KC, T], F32, x_at)
    x2 = at("x2", [P, KC, T], F32, zone)
    fin = at("fin", [P, KC, T], F32, zone + 18432)
    assert zone + 91264 <= nc.sbuf_usable_end

    ident, ones = consts[:, K_ID:K_ID + P], consts[:, K_ONE:K_ONE + P]
    iota = consts[:, K_IOTA:K_IOTA + NK]

    with ExitStack() as ctx:
        def sem(name):
            return ctx.enter_context(nc.semaphore(name))

        zb = ctx.enter_context(nc.psum_tensor("zb", [P, 4, 512], F32))
        vb = ctx.enter_context(nc.psum_tensor("vb", [P, 4, 512], F32))

        raw_in = [sem(f"raw_in{s}") for s in range(4)]
        cache_in = [sem(f"cache_in{s}") for s in range(4)]
        hi_ready = sem("hi_ready")
        lo_ready = sem("lo_ready")
        unit_used = sem("unit_used")
        z_free = sem("z_free")
        c_in = sem("c_in")
        consts_in = sem("consts_in")
        vecs_in = sem("vecs_in")
        x_in = sem("x_in")
        glu0_in = sem("glu0_in")
        masks_in = sem("masks_in")
        keys_in = sem("keys_in")
        silu_done = sem("silu_done")
        c_ready = sem("c_ready")
        row_copied = sem("row_copied")
        row_turned = sem("row_turned")
        mods_ready = sem("mods_ready")
        sq_ready = sem("sq_ready")
        stat_ready = sem("stat_ready")
        root_ready = sem("root_ready")
        h_ready = sem("h_ready")
        h_mod = sem("h_mod")
        h_hi = sem("h_hi")
        h_half = sem("h_half")
        h_split = sem("h_split")
        sig_ready = sem("sig_ready")
        glu_ready = sem("glu_ready")
        z_half = sem("z_half")
        qkv_evac = sem("qkv_evac")
        rope_perm = sem("rope_perm")
        rope_step = sem("rope_step")
        rope_done = sem("rope_done")
        conv_step = sem("conv_step")
        pool_prod = sem("pool_prod")
        pool_sum = sem("pool_sum")
        conv_done = sem("conv_done")
        prod_step = sem("prod_step")
        conv_s_done = sem("conv_s_done")
        hist_out = sem("hist_out")
        v_out_done = sem("v_out_done")
        k_out_done = sem("k_out_done")
        ln_sum = sem("ln_sum")
        ln_centred = sem("ln_centred")
        ln_sq = sem("ln_sq")
        ln_sqsum = sem("ln_sqsum")
        ln_z = sem("ln_z")
        ln_out = sem("ln_out")
        v_turned = sem("v_turned")
        v_copied = sem("v_copied")
        cache_used = sem("cache_used")
        score_ready = sem("score_ready")
        masked = sem("masked")
        neg_max = sem("neg_max")
        exp_done = sem("exp_done")
        prob_ready = sem("prob_ready")
        prob_turned = sem("prob_turned")
        pT_ready = sem("pT_ready")
        zero_ready = sem("zero_ready")
        zq_ready = sem("zq_ready")
        o_rows = sem("o_rows")
        o_rows_copied = sem("o_rows_copied")
        o_ready = sem("o_ready")
        o_copied = sem("o_copied")
        o_sq = sem("o_sq")
        o_sum = sem("o_sum")
        inv_ready = sem("inv_ready")
        inv_spread = sem("inv_spread")
        o_normed = sem("o_normed")
        x1_step = sem("x1_step")
        x1_tile = sem("x1_tile")
        qp_copied = sem("qp_copied")
        s_ready = sem("s_ready")
        s_copied = sem("s_copied")
        s_read = sem("s_read")
        gate_in = sem("gate_in")
        gate_out = sem("gate_out")
        picks_ready = sem("picks_ready")
        picks_turned = sem("picks_turned")
        picks_copied = sem("picks_copied")
        spilled = sem("spilled")
        one_ready = sem("one_ready")
        distance = sem("distance")
        one_act_ready = sem("one_act_ready")
        g_ready = sem("g_ready")
        g_copied = sem("g_copied")
        g2_out = [sem(f"g2_out{b}") for b in range(2)]
        g2_in = sem("g2_in")
        acc_zero = sem("acc_zero")
        gelu_done = sem("gelu_done")
        w_mid = sem("w_mid")
        w_ready = sem("w_ready")
        vb_ready = sem("vb_ready")
        vb_free = sem("vb_free")
        x1_in = sem("x1_in")
        x2_ready = sem("x2_ready")
        y_ready = sem("y_ready")
        y_out = sem("y_out")
        dve_step = sem("dve_step")
        block = ctx.enter_context(nc.Block())

        def over(ap, n):
            return ap.unsqueeze(1).to_broadcast([ap.shape[0], n, ap.shape[1]])

        def load(sp, q, s, dst_src):
            sp.wait_ge(lo_ready, 4 * q + s + 1)
            sp.dma_start(raw[s][:, :] if dst_src[0] is None else dst_src[0], dst_src[1]).then_inc(raw_in[s], 16)

        def split_hi(act, q, s):
            act.wait_ge(raw_in[s], 16 * q + 16)
            act.wait_ge(unit_used, 4 * q + s + 1)
            act.activation(hi[s][:, :], raw[s][:, :], ACT.Copy).then_inc(hi_ready, 1)

        def split_lo(dve, q, s):
            dve.wait_ge(hi_ready, 4 * q + s + 1)
            dve.tensor_tensor(lo[s][:, :], raw[s][:, :], hi[s][:, :].bitcast(F32), ALU.subtract) \
                .then_inc(lo_ready, 1)

        def project(pe, q, parity, tile=None, both_halves=None):
            for s in range(4):
                bank = 2 * parity + s // 2
                if s % 2 == 0 and tile is not None:
                    pe.wait_ge(z_free, tile + s // 2 + 1)
                if s % 2 and both_halves is not None:
                    pe.wait_ge(h_split, both_halves)
                pe.wait_ge(lo_ready, 4 * q + s + 5)
                for j in range(8):
                    k = 8 * (s % 2) + j
                    w_h, w_l = hi[s][:, j * P:(j + 1) * P], lo[s][:, j * P:(j + 1) * P]
                    pe.matmul(zb[:, bank, 0:T], w_h, act_hi[:, k, :], start=(k == 0), stop=False)
                    pe.matmul(zb[:, bank, 0:T], w_h, act_lo[:, k, :], start=False, stop=False)
                    last = pe.matmul(zb[:, bank, 0:T], w_l, act_hi[:, k, :], start=False, stop=(k == KC - 1))
                last.then_inc(unit_used, 1)

        @block.sync
        def _(sp):
            def load_ada(q0, n0, count):
                with sp.Fori(0, count) as n:
                    for k in range(8):
                        load(sp, q0 + 2 * n + k // 4, k % 4, (None, w_ada_d[n + n0, k]))

            load_ada(0, 0, ADA_FIRST)
            with sp.Fori(0, CT) as j:
                for s in range(4):
                    load(sp, Q_GLU + j, s, (None, w_in_d[2 * j + s // 2][:, UNIT * (s % 2):UNIT * (s % 2 + 1)]))
            with sp.Fori(0, 12) as j:
                for s in range(4):
                    load(sp, Q_QKV + j, s,
                         (None, w_in_d[2 * CT + 2 * j + s // 2][:, UNIT * (s % 2):UNIT * (s % 2 + 1)]))
            def load_proj(q0, w_d):
                with sp.Fori(0, KC // 2) as j:
                    for s in range(4):
                        load(sp, q0 + j, s, (None, w_d[2 * j + s // 2][:, UNIT * (s % 2):UNIT * (s % 2 + 1)]))

            load_ada(Q_ADA_MIXER, ADA_FIRST, ADA_MIXER)
            load_proj(Q_OUT, w_out_d)
            load_proj(Q_WQ, w_q_d)
            load_ada(Q_ADA_LAST, ADA_FIRST + ADA_MIXER, ADA_LAST)

            def load_u(pair, q):
                for s in range(4):
                    i2 = 2 * pair + s // 2
                    load(sp, q, s, (None, u_d[i2][:, UNIT * (s % 2):UNIT * (s % 2 + 1)]))

            def load_v(pair, q):
                for s in range(4):
                    dst = raw[s][:, :].rearrange("p (a d) -> p a d", a=2)
                    load(sp, q, s, (dst, v_d[:, bass.ds(2 * pair, 2), 512 * s:512 * (s + 1)]))

            load_u(0, Q_PEER)
            with sp.Fori(0, PAIRS - 1) as i:
                load_u(i + 1, Q_PEER + 2 * i + 1)
                load_v(i, Q_PEER + 2 * i + 2)
            load_v(PAIRS - 1, Q_PEER + NK - 1)

        @block.gpsimd
        def _(pool):
            pool.wait_ge(x_in, 16)
            pool.tensor_tensor(sq[:, :, :], xT[:, :, :], xT[:, :, :], ALU.mult).then_inc(sq_ready, 1)
            pool.wait_ge(vecs_in, 16)
            pool.wait_ge(mods_ready, ADA_FIRST + 2)
            with pool.Fori(0, CT) as ct:
                pool.wait_ge(glu_ready, ct + 2)
                row = glu[:, bass.ds(ct, 1), GW_P:GW]
                window = bass.AP(row.tensor, row.offset, [list(row.ap[0]), [GW_S, DB], [1, DS], [1, CONV_W]])
                taps = vecs[:, bass.ds(V_CW + CONV_W * ct, CONV_W)]
                taps = bass.AP(taps.tensor, taps.offset, [list(taps.ap[0]), [0, DB], [0, DS], [1, CONV_W]])
                out = prod[:, :, :].rearrange("p (b s) w -> p b s w", b=DB)
                pool.tensor_tensor(out, window, taps, ALU.mult).then_inc(prod_step, 1)
                for k, n in enumerate((16, 8, 4, 2)):
                    pool.wait_ge(prod_step, 5 * ct + k + 1)
                    m = min(n, CONV_W - n)
                    pool.tensor_tensor(prod[:, :, 0:m], prod[:, :, 0:m], prod[:, :, n:n + m], ALU.add) \
                        .then_inc(prod_step, 1)
                pool.wait_ge(prod_step, 5 * ct + 5)
                pool.tensor_tensor(conv_y[:, bass.ds(ct, 1), SEQ:T].rearrange("p c t -> p t c"), prod[:, :, 0:1],
                                   prod[:, :, 1:2], ALU.add).then_inc(conv_s_done, 1)
                pool.wait_ge(conv_s_done, ct + 1)
            pool.wait_ge(z_half, CT)
            pool.wait_ge(sig_ready, CT)
            ct0 = CT - CT_POOL
            out = conv_y[:, ct0:CT, 0:SEQ]
            taps = vecs[:, V_CW + CONV_W * ct0:V_CW + CONV_W * CT].rearrange("p (c w) -> p c w", w=CONV_W)
            for w in range(CONV_W):
                tap = taps[:, :, w:w + 1].to_broadcast([P, CT_POOL, SEQ])
                window = glu[:, ct0:CT, w:w + SEQ]
                if w == 0:
                    pool.tensor_tensor(out, window, tap, ALU.mult).then_inc(pool_sum, 1)
                    continue
                if w >= 3:
                    pool.wait_ge(pool_sum, w - 1)
                pool.tensor_tensor(conv_p[w % 2][:, :, :], window, tap, ALU.mult).then_inc(pool_prod, 1)
                if w >= 2:
                    pool.wait_ge(pool_prod, w - 1)
                    pool.wait_ge(pool_sum, w - 1)
                    pool.tensor_tensor(out, out, conv_p[(w - 1) % 2][:, :, :], ALU.add).then_inc(pool_sum, 1)
            pool.wait_ge(pool_prod, CONV_W - 1)
            pool.wait_ge(pool_sum, CONV_W - 1)
            pool.tensor_tensor(out, out, conv_p[(CONV_W - 1) % 2][:, :, :], ALU.add).then_inc(pool_sum, 1)
            pool.wait_ge(pool_sum, CONV_W)
            pool.tensor_tensor(out, out, vecs[:, V_CB + ct0:V_CB + CT].unsqueeze(2).to_broadcast([P, CT_POOL, SEQ]),
                               ALU.add).then_inc(pool_sum, 1)
            pool.dma_start(convp_out, glu[:, :, SEQ:GW_P]).then_inc(hist_out, 16)
            for ct in range(CT):
                src = glu[:, ct, GW_P:GW].rearrange("p (b w) -> p b w", b=DB)[:, :, DS:GW_S]
                pool.dma_start(convs_out[:, ct], src).then_inc(hist_out, 16)
            pool.wait_ge(qkv_evac, KV_PAIRS)
            pool.dma_start(v_out, qkvT[:, 2 * H:3 * H, :]).then_inc(v_out_done, 16)
            pool.wait_ge(rope_done, 5)
            pool.dma_start(k_out, qkvT[:, H:2 * H, :]).then_inc(k_out_done, 16)

            pool.wait_ge(unit_used, 4 * Q_ADA_MIXER + 4)
            pool.memset(zq[:, :, :], 0.0).then_inc(zero_ready, 1)
            pool.memset(zp[:, :, :], 0.0).then_inc(zero_ready, 1)
            pool.wait_ge(conv_done, 1)
            pool.wait_ge(hist_out, 16 * (1 + CT))
            pool.wait_ge(zero_ready, 2)
            for n in range(32):
                if n in (4, 12):
                    g = n // 8
                    if g:
                        pool.wait_ge(score_ready, 5)
                    pool.tensor_copy(zq[:, :, :].rearrange("p h (b x) -> p h b x", x=ZB)[:, :, :, 0:DS],
                                     qkvT[:, 4 * g:4 * g + 4, SEQ:T].rearrange("p h (b s) -> p h b s", b=DB)) \
                        .then_inc(zq_ready, 1)
                if n >= 4:
                    pool.wait_ge(cache_used, n - 3)
                src = (ck_d, cv_d)[n // 8 % 2][4 * (n // 16) + n % 8 // 2, n % 2]
                pool.dma_start(cache[n % 4][:, :], src).then_inc(cache_in[n % 4], 16)

            pool.wait_ge(prob_ready, len(JOBS))
            pool.dma_start(keysT[:, :, :], keys_d).then_inc(keys_in, 16)

            pool.wait_ge(h_split, 3)
            pool.dma_start(spill_d, xT[:, :, :].rearrange("p k t -> p (k t)")).then_inc(spilled, 16)

            pool.wait_ge(lo_ready, 4 * Q_ADA_LAST + 8)
            with pool.Fori(0, 2 * ADA_LAST + 1) as q:
                for s in range(4):
                    split_lo(pool, Q_ADA_LAST + 1 + q, s)

            for blk in range(TBLKS):
                pool.wait_ge(g_copied, 4 * blk + 6)
                pool.dma_start(gates_d[blk], stage[blk % 2][:, :, :, :].rearrange("p c e t -> p c (e t)")) \
                    .then_inc(g2_out[blk % 2], 16)

            for b in range(2):
                pool.wait_ge(g2_out[b], 16 * ((TBLKS + 1 - b) // 2))
            pool.memset(acc[:, :, :], 0.0).then_inc(acc_zero, 1)
            with pool.Fori(0, CHUNKS) as c:
                pool.wait_ge(w_ready, 2 * c + 4)
                pool.dma_start(G[:, bass.ds(c, 1), :, :, :].rearrange("p c b e t -> p (c b) (e t)"),
                               gates_d[:, :, bass.ds(c, 1), :].rearrange("b p c x -> p (b c) x")).then_inc(g2_in, 16)
                pool.wait_ge(g2_in, 16 * c + 16)

            pool.wait_ge(w_ready, PAIRS // 2 + PAIRS // 4 + 2)
            pool.dma_start(x2[:, :, :].rearrange("p k t -> p (k t)"), spill_d).then_inc(x1_in, 16)
            pool.wait_ge(v_out_done, 16)
            pool.wait_ge(k_out_done, 16)
            pool.wait_ge(y_out, 16 * 4)

        @block.scalar
        def _(act):
            def quad_hi(q):
                for s in range(4):
                    split_hi(act, q, s)

            eps = consts[:, K_EPS:K_EPS + 1]

            def root(total, n, ready, k):
                act.wait_ge(ready, k)
                act.activation(rs[:, :], total, ACT.Sqrt, bias=eps, scale=1.0 / n).then_inc(root_ready, 1)

            for dst, src, arrived in ((cT[:, :, :], cT_d, c_in), (xT[:, :, :], xT_d, x_in),
                                      (consts[:, :], consts_d, consts_in), (vecs[:, :], vecs_d, vecs_in)):
                act.dma_start(dst, src).then_inc(arrived, 16)
            act.sem_inc(z_free, 4)
            act.sem_inc(row_copied, 2)
            act.sem_inc(g_copied, 2)
            act.sem_inc(gelu_done, 2)
            act.wait_ge(c_in, 16)
            act.activation(cT[:, :, :], cT[:, :, :], ACT.Silu).then_inc(silu_done, 1)
            quad_hi(0)

            def ada_out(n, b):
                act.wait_ge(row_turned, n + 1)
                act.activation(ada_row[b][:, :], zb[0:2 * NC, b, :], ACT.Copy).then_inc(row_copied, 1)

            def first_tile(n, b):
                quad_hi(2 * n + 1)
                quad_hi(2 * n + 2)
                ada_out(n, b)

            first_tile(0, 0)
            first_tile(1, 1)
            act.wait_ge(consts_in, 16)
            root(vb[:, 2, 0:T], D, stat_ready, 1)
            first_tile(2, 0)
            with act.Fori(1, ADA_FIRST // 2 - 1) as m:
                first_tile(2 * m + 1, 1)
                first_tile(2 * m + 2, 0)
            first_tile(ADA_FIRST - 1, 1)
            act.dma_start(glu[:, :, :], glu0_d).then_inc(glu0_in, 16)
            act.dma_start(masks[:, :], masks_d).then_inc(masks_in, 16)

            def norm_hi(done, scale, shift):
                for c in range(4):
                    act.wait_ge(h_ready, done + c + 1)
                    for k in range(4 * c, 4 * c + 4):
                        last = act.activation(hF[:, k, 0:SEQ], hF[:, k, 0:SEQ], ACT.Identity,
                                              scale=scale[:, k, 0:1], bias=mods[:, KC * shift + k, 0:1])
                    last.then_inc(h_mod, 1)
                    act.wait_ge(h_mod, done + c + 1)
                    act.activation(act_hi[:, 4 * c:4 * c + 4, :], hF[:, 4 * c:4 * c + 4, :], ACT.Copy) \
                        .then_inc(h_hi, 1)

            norm_hi(0, m_a1, 0)
            act.wait_ge(mods_ready, ADA_FIRST + 2)
            with act.Fori(0, CT // 2) as m:
                for b in range(2):
                    j = 2 * m + b
                    quad_hi(Q_GLU + 1 + j)
                    act.wait_ge(glu_ready, j + 1)
                    act.activation(sig[:, :], zb[:, 2 * b + 1, 0:T], ACT.Sigmoid).then_inc(sig_ready, 1)
            with act.Fori(0, 2) as m:
                for k in range(6):
                    j = 6 * m + k
                    quad_hi(Q_QKV + 1 + j)
                    pair = zb[:, 2 * (k % 2):2 * (k % 2) + 2, 0:T]
                    act.activation(qkvT[:, bass.ds(2 * j, 2), :], pair, ACT.Copy).then_inc(qkv_evac, 1)
            for g in range(6):
                n = TOK_TILES[g // 2][1]
                act.wait_ge(v_turned, g + 1)
                act.activation(v_tok[0:n, g // 2, 512 * (g % 2):512 * (g % 2) + 512], vb[0:n, g % 4, :], ACT.Copy) \
                    .then_inc(v_copied, 1)
            act.wait_ge(ln_centred, 1)
            act.activation(sq_ln[:, :, :], conv_y[:, :, :], ACT.Square).then_inc(ln_sq, 1)
            act.wait_ge(v_out_done, 16)

            def exps(n):
                sample = JOBS[n][1]
                act.wait_ge(neg_max, n + 1)
                if n >= 2:
                    act.wait_ge(prob_turned, n - 1)
                for lo_c, hi_c, c in JOB_COLS[sample]:
                    last = act.activation(ex[n % 2][:, lo_c:hi_c], sc[n % 2][:, lo_c:hi_c], ACT.Exp,
                                          bias=small[:, 6 * n + c:6 * n + c + 1])
                last.then_inc(exp_done, 1)

            def probs_out(n):
                sample = JOBS[n][1]
                act.wait_ge(prob_turned, n + 1)
                if n:
                    act.wait_ge(o_ready, n)
                if sample:
                    act.wait_ge(zero_ready, 2)
                    act.activation(zp[:, :, :].rearrange("p h (b x) -> p h b x", x=ZB)[:, :, :, 0:DS],
                                   vb[:, 2, 0:256].rearrange("p (h b s) -> p h b s", h=8, b=DB), ACT.Copy)
                    act.activation(pT[0:TS, 256:384], vb[0:TS, 2, 256:384], ACT.Copy).then_inc(pT_ready, 1)
                else:
                    act.activation(pT[:, :], vb[:, 2, 0:384], ACT.Copy).then_inc(pT_ready, 1)

            def attention_out(n):
                g, sample = JOBS[n]
                if sample:
                    act.wait_ge(o_rows, g + 1)
                    act.activation(o_row[:, :], vb[:, 3, 256:384], ACT.Copy).then_inc(o_rows_copied, 1)
                act.wait_ge(o_ready, n + 1)
                if sample:
                    act.activation(oT[:, 4 * g:4 * g + 4, SEQ:T],
                                   vb[:, 3, 256:384].rearrange("p (h t) -> p h t", h=4), ACT.Copy) \
                        .then_inc(o_copied, 1)
                else:
                    act.activation(oT[:, g, 0:SEQ], vb[:, 3, 0:256], ACT.Copy).then_inc(o_copied, 1)

            def ada_step(k):
                quad_hi(Q_ADA_MIXER + k + 1)
                if k % 2:
                    ada_out(ADA_FIRST + k // 2, k // 2 % 2)

            exps(0)
            root(zb[:, 1, 0:T], CT * P, ln_sqsum, 1)
            for n in range(len(JOBS)):
                ada = ada_steps(n)
                ada_step(ada[0])
                probs_out(n)
                ada_step(ada[1])
                if n + 1 < len(JOBS):
                    exps(n + 1)
                for k in ada[2:3]:
                    ada_step(k)
                if 0 < n <= SILU_JOBS:
                    act.wait_ge(ln_z, 1)
                    for ct in range(CT * (n - 1) // SILU_JOBS, CT * n // SILU_JOBS):
                        last = act.activation(conv_y[:, ct, :], conv_y[:, ct, :], ACT.Silu,
                                              bias=vecs[:, V_LNB + ct:V_LNB + ct + 1],
                                              scale=vecs[:, V_LNG + ct:V_LNG + ct + 1])
                    last.then_inc(ln_out, 1)
                if n == SILU_JOBS + 1:
                    act.wait_ge(ln_out, SILU_JOBS)
                    act.activation(act_hi[:, 0:CT, :], conv_y[:, :, :], ACT.Copy).then_inc(h_hi, 1)
                attention_out(n)
                for k in ada[3:4]:
                    ada_step(k)
            act.wait_ge(o_copied, len(JOBS))
            act.activation(sq_at[:, :, :], oT, ACT.Square).then_inc(o_sq, 1)
            act.activation(head_rows[:, :, :], ident[0:H, 0:H].unsqueeze(2).to_broadcast([H, H, P]), ACT.Copy)
            act.wait_ge(o_sum, 1)
            act.activation(head_inv[:, :], vb[0:H, 0, 0:T], ACT.Sqrt, bias=eps[0:H], scale=1.0 / E) \
                .then_inc(root_ready, 1)
            act.wait_ge(o_normed, 1)
            act.activation(act_hi[:, CT:KC, :], oT, ACT.Copy).then_inc(h_hi, 1)
            quad_hi(Q_OUT + 1)
            act.wait_ge(h_split, 2)
            act.wait_ge(k_out_done, 16)
            with act.Fori(0, KC // 2 - 1) as j:
                quad_hi(Q_OUT + 2 + j)
                act.wait_ge(x1_tile, j + 2)
                act.activation(hF[:, bass.ds(2 * j, 2), :], xT[:, bass.ds(2 * j, 2), :], ACT.Square) \
                    .then_inc(sq_ready, 1)
            act.wait_ge(x1_tile, KC // 2 + 1)
            act.activation(hF[:, KC - 2:KC, :], xT[:, KC - 2:KC, :], ACT.Square).then_inc(sq_ready, 1)
            root(vb[:, 0, 0:T], D, stat_ready, 2)
            norm_hi(4, m_a2, 3)
            act.wait_ge(h_split, 3)
            with act.Fori(0, KC // 4) as m:
                for b in range(2):
                    quad_hi(Q_WQ + 1 + 2 * m + b)
                    act.activation(qpT[:, bass.ds(4 * m + 2 * b, 2), :], zb[:, 2 * b:2 * b + 2, 0:T], ACT.Copy) \
                        .then_inc(qp_copied, 1)
            def score_copy(tt):
                n, banks = min(P, TOK_TILES[tt][1] * H // TOPK_HEADS[tt]), TOPK_HEADS[tt] // 2
                act.wait_ge(s_ready, tt + 1)
                if tt:
                    act.wait_ge(s_read, tt)
                act.activation(s_tm[0:n, 0:4 * banks, :].rearrange("p (b k) d -> p b (k d)", b=banks),
                               vb[0:n, 0:banks, :], ACT.Copy).then_inc(s_copied, 1)

            def gate_exp(tt):
                hn = TOPK_HEADS[tt]
                act.wait_ge(gate_in, tt + 1)
                act.activation(g_exp[:, 0:hn, :], g_exp[:, 0:hn, :], ACT.Exp).then_inc(gate_out, 1)

            def picks_out(tt):
                t0, n = TOK_TILES[tt]
                act.wait_ge(picks_turned, tt + 1)
                for c, dst, sign in ((0, i1T, 1.0), (1, i2T, 1.0), (2, gT, 1.0), (2, minus_gT, -1.0)):
                    act.activation(dst[:, t0:t0 + n], zb[:, 2, c * P:c * P + n], ACT.Copy, scale=sign) \
                        .then_inc(picks_copied, 1)

            def last_mods(k):
                n, b = ADA_FIRST + ADA_MIXER + k, k % 2
                act.wait_ge(row_turned, n + 3)
                for c in range(4):
                    last = act.activation(m_g5[:, 4 * k + c, :], zb[:, 3, 64 * b + NC * c:64 * b + NC * c + NC],
                                          ACT.Identity, bias=vecs[:, V_ADA + 4 * n + c:V_ADA + 4 * n + c + 1])
                last.then_inc(mods_ready, 1)

            def last_tile(k):
                quad_hi(Q_ADA_LAST + 2 * k + 1)
                if k:
                    last_mods(k - 1)
                quad_hi(Q_ADA_LAST + 2 * k + 2)
                ada_out(ADA_FIRST + ADA_MIXER + k, k % 2)

            score_copy(0)
            last_tile(0)
            score_copy(1)
            gate_exp(0)
            last_tile(1)
            picks_out(0)
            last_tile(2)
            score_copy(2)
            last_tile(3)
            last_mods(3)
            gate_exp(1)
            picks_out(1)
            gate_exp(2)
            quad_hi(Q_PEER + 1)
            picks_out(2)

            def one_hots(g, b):
                for t in range(8 - ON_ACT, 8):
                    last = act.activation(one1[b][:, t, :], iota, ACT.Abs, bias=i1T[:, bass.ds(8 * g + t, 1)],
                                          scale=-1.0)
                last.then_inc(distance, 1)
                act.wait_ge(distance, g + 1)
                for t in range(8 - ON_ACT, 8):
                    last = act.activation(one1[b][:, t, :], one1[b][:, t, :], ACT.Relu,
                                          bias=gT[:, bass.ds(8 * g + t, 1)], scale=minus_gT[:, bass.ds(8 * g + t, 1)])
                last.then_inc(one_act_ready, 1)

            def gate_block(blk, b, first, final=False):
                if not first:
                    act.wait_ge(g2_out[b], 8 * blk - 8 * b)
                for k in range(4):
                    g = 4 * blk + k
                    if not (final and k == 3):
                        act.wait_ge(g_ready, g + 2)
                        one_hots(g + 1, (k + 1) % 2)
                    act.wait_ge(g_ready, g + 3)
                    rows = vb[:, 2 * (k % 2):2 * (k % 2) + 2, :].rearrange("p a (t i) -> p (a t) i", t=4)
                    for half, out in enumerate((G[:, :, bass.ds(blk, 1), :, 8 * k:8 * k + 8]
                                                .rearrange("p c b e t -> p t (c b) e"),
                                                stage[b][:, :, :, 8 * k:8 * k + 8].rearrange("p c e t -> p t c e"))):
                        src = rows[:, :, HALF * half:HALF * (half + 1)].rearrange("p t (c e) -> p t c e", e=CHUNK)
                        last = act.activation(out, src, ACT.Copy)
                    last.then_inc(g_copied, 1)

            act.wait_ge(spilled, 16)
            act.wait_ge(picks_copied, 4 * 3)
            one_hots(0, 0)
            gate_block(0, 0, True)
            gate_block(1, 1, True)
            with act.Fori(0, (TBLKS - 3) // 2) as m:
                gate_block(2 * m + 2, 0, False)
                gate_block(2 * m + 3, 1, False)
            gate_block(TBLKS - 1, 0, False, True)

            def gelu(pair, b):
                act.wait_ge(w_ready, pair + 1)
                act.activation(gl[b][:, :, :], zb[:, 2 * b:2 * b + 2, 0:T], ACT.Gelu).then_inc(gelu_done, 1)

            def body(i, b):
                quad_hi(Q_PEER + 2 * i + 2)
                gelu(i + 1, (b + 1) % 2)
                quad_hi(Q_PEER + 2 * i + 3)

            gelu(0, 0)
            with act.Fori(0, (PAIRS - 2) // 2) as m:
                body(2 * m, 0)
                body(2 * m + 1, 1)
            body(PAIRS - 2, 0)
            for k in range(4):
                act.wait_ge(x2_ready, k + 1)
                act.activation(sq[:, 4 * k:4 * k + 4, :], x2[:, 4 * k:4 * k + 4, :], ACT.Square).then_inc(sq_ready, 1)
            root(zb[:, 0, 0:T], D, stat_ready, 3)
            for k in range(4):
                act.wait_ge(y_ready, k + 1)
                act.dma_start(y_d[:, 4 * k:4 * k + 4], fin[:, 4 * k:4 * k + 4, :]).then_inc(y_out, 16)

        @block.tensor
        def _(pe):
            pe.sem_inc(unit_used, 4)
            pe.sem_inc(row_turned, 2)
            pe.sem_inc(g_ready, 2)

            def channel_sum(out, src, chunks, done):
                for k in range(chunks):
                    last = pe.matmul(out, ones, src[:, k, :], start=(k == 0), stop=(k == chunks - 1))
                last.then_inc(done, 1)

            pe.wait_ge(consts_in, 16)
            pe.wait_ge(c_ready, 2)
            sel = consts[0:2 * NC, K_SEL:K_SEL + NC]

            def ada_quad(q, n, b, part):
                if part == 0:
                    pe.wait_ge(row_copied, n + 1)
                for s in range(4):
                    k = 4 * part + s
                    pe.wait_ge(lo_ready, 4 * q + s + 5)
                    for j in range(2):
                        c = c_split[:, 2 * k + j, :]
                        pe.matmul(zb[0:2 * NC, b, :], c, hi[s][:, 512 * j:512 * j + 512],
                                  start=(k == 0 and j == 0), stop=False)
                        last = pe.matmul(zb[0:2 * NC, b, :], c, lo[s][:, 512 * j:512 * j + 512],
                                         start=False, stop=(k == 7 and j == 1))
                    last.then_inc(unit_used, 1)

            def turn_row(n, b):
                pe.wait_ge(row_copied, n + 3)
                pe.wait_ge(mods_ready, n + 2)
                for c in range(4):
                    at_c = 64 * b + NC * c
                    last = pe.matmul(zb[:, 3, at_c:at_c + NC], ada_row[b][:, c * P:(c + 1) * P], sel,
                                     start=True, stop=True)
                last.then_inc(row_turned, 1)

            def first_tile(n, b, first):
                ada_quad(2 * n, n, b, 0)
                if not first:
                    turn_row(n - 1, 1 - b)
                ada_quad(2 * n + 1, n, b, 1)

            first_tile(0, 0, True)
            pe.wait_ge(sq_ready, 1)
            channel_sum(vb[:, 2, 0:T], sq, KC, stat_ready)
            with pe.Fori(0, ADA_FIRST // 2 - 1) as m:
                first_tile(2 * m + 1, 1, False)
                first_tile(2 * m + 2, 0, False)
            first_tile(ADA_FIRST - 1, 1, False)
            turn_row(ADA_FIRST - 1, 1)
            pe.wait_ge(h_half, 1)
            with pe.Fori(0, CT // 2) as m:
                for b in range(2):
                    project(pe, Q_GLU + 2 * m + b, b, 2 * (2 * m + b), 1)
            with pe.Fori(0, 6) as m:
                for b in range(2):
                    project(pe, Q_QKV + 2 * m + b, b, 2 * CT + 2 * (2 * m + b))

            pe.wait_ge(masks_in, 16)
            pe.wait_ge(qkv_evac, KV_PAIRS)
            for g in range(6):
                t0, n = TOK_TILES[g // 2]
                if g >= 4:
                    pe.wait_ge(v_copied, g - 3)
                for h in range(4):
                    last = pe.transpose(vb[0:n, g % 4, P * h:P * h + P],
                                        qkvT[:, 2 * H + 4 * (g % 2) + h, t0:t0 + n], ident)
                last.then_inc(v_turned, 1)
            for i in range(4):
                if i == 1:
                    pe.wait_ge(v_copied, 6)
                elif i >= 2:
                    pe.wait_ge(rope_done, i)
                for t in range(4):
                    last = pe.matmul((zb, vb)[i % 2][:, t, 0:T], masks[0:ROT, M_PERM:M_PERM + P],
                                     qkvT[0:ROT, 4 * i + t, :], start=True, stop=True)
                last.then_inc(rope_perm, 1)
            pe.wait_ge(rope_done, 5)
            pe.wait_ge(conv_done, 1)
            channel_sum(zb[:, 0, 0:T], conv_y, CT, ln_sum)
            pe.wait_ge(v_copied, 6)

            def scores(n, part):
                g, sample = JOBS[n]
                if part == 0 and n >= 2:
                    pe.wait_ge(masked, n - 1)
                if not sample:
                    if part == 0:
                        q, k = qkvT[:, g, :], qkvT[:, H + g, :]
                        pe.matmul(vb[:, n % 2, 0:128], q[:, 0:128], k[:, 0:128], start=True, stop=True)
                        pe.matmul(vb[:, n % 2, 128:384], q[:, 128:256], k[:, 0:256], start=True, stop=True) \
                            .then_inc(score_ready, 1)
                    return
                pe.wait_ge(zq_ready, g + 1)
                for hb in range(4 * part, 4 * part + 4):
                    u = 16 * g + hb
                    pe.wait_ge(cache_in[u % 4], 16 * (u // 4) + 16)
                    h = hb // 2
                    for j in range(4):
                        b = 4 * (hb % 2) + j
                        last = pe.matmul(vb[TS * h:TS * h + TS, n % 2, 0:PAST], zq[:, h, TS * b:TS * b + TS],
                                         cache[u % 4][:, PAST * j:PAST * j + PAST],
                                         start=(b == 0), stop=(b == DB - 1))
                    last.then_inc(cache_used, 1)
                for h in range(2 * part, 2 * part + 2):
                    last = pe.matmul(vb[TS * h:TS * h + TS, n % 2, PAST:PAST + TS], qkvT[:, 4 * g + h, SEQ:T],
                                     qkvT[:, H + 4 * g + h, SEQ:T], start=True, stop=True)
                if part:
                    last.then_inc(score_ready, 1)

            def turn(n):
                sample = JOBS[n][1]
                pe.wait_ge(prob_ready, n + 1)
                if n:
                    pe.wait_ge(pT_ready, n)
                pe.transpose(vb[:, 2, 0:128], ex[n % 2][:, 0:128], ident)
                pe.transpose(vb[:, 2, 128:256], ex[n % 2][:, 128:256], ident)
                if sample:
                    last = pe.transpose(vb[0:TS, 2, 256:384], ex[n % 2][:, 256:288], ident)
                else:
                    last = pe.transpose(vb[:, 2, 256:384], ex[n % 2][:, 256:384], ident)
                last.then_inc(prob_turned, 1)

            def mix_values(n, part):
                g, sample = JOBS[n]
                if part == 0:
                    pe.wait_ge(pT_ready, n + 1)
                    if n:
                        pe.wait_ge(o_copied, n)
                if not sample:
                    if part == 0:
                        v = v_tok[:, :, P * g:P * g + P]
                        pe.matmul(vb[:, 3, 0:256], v[:, 0, :], pT[:, 0:256], start=True, stop=False)
                        pe.matmul(vb[:, 3, 128:256], v[:, 1, :], pT[:, 256:384], start=False, stop=True) \
                            .then_inc(o_ready, 1)
                    return
                for h in range(2 * part, 2 * part + 2):
                    out = vb[TS * h:TS * h + TS, 3, 256:384]
                    for bh in range(2):
                        u = 16 * g + 8 + 2 * h + bh
                        pe.wait_ge(cache_in[u % 4], 16 * (u // 4) + 16)
                        for j in range(4):
                            b = 4 * bh + j
                            for c in range(2):
                                last = pe.matmul(out, zp[:, 4 * c + h, TS * b:TS * b + TS],
                                                 cache[u % 4][:, 512 * c + P * j:512 * c + P * j + P],
                                                 start=(b == 0 and c == 0), stop=False)
                        last.then_inc(cache_used, 1)
                    last = pe.matmul(out, pT[0:TS, 256 + TS * h:256 + TS * h + TS],
                                     v_tok[0:TS, 2, P * (4 * g + h):P * (4 * g + h) + P], start=False, stop=True)
                if part:
                    last.then_inc(o_rows, 1)
                    pe.wait_ge(o_rows_copied, g + 1)
                    pe.transpose(vb[:, 3, 256:384], o_row[:, :], ident).then_inc(o_ready, 1)

            def ada_step(k):
                t = k // 2
                ada_quad(Q_ADA_MIXER + k, ADA_FIRST + t, t % 2, k % 2)
                if k and k % 2 == 0:
                    turn_row(ADA_FIRST + t - 1, (t - 1) % 2)

            scores(0, 0)
            pe.wait_ge(ln_sq, 1)
            channel_sum(zb[:, 1, 0:T], sq_ln, CT, ln_sqsum)
            pe.wait_ge(root_ready, 2)
            for n in range(len(JOBS)):
                ada, more = ada_steps(n), n + 1 < len(JOBS)
                if more:
                    scores(n + 1, 0)
                ada_step(ada[0])
                if more:
                    scores(n + 1, 1)
                turn(n)
                ada_step(ada[1])
                mix_values(n, 0)
                for k in ada[2:3]:
                    ada_step(k)
                mix_values(n, 1)
                for k in ada[3:4]:
                    ada_step(k)
            turn_row(ADA_FIRST + ADA_MIXER - 1, 1)
            pe.wait_ge(o_sq, 1)
            pe.wait_ge(mods_ready, ADA_FIRST + ADA_MIXER + 2)
            for h in range(H):
                window = K_HEAD + H - 1 - h
                last = pe.matmul(vb[0:H, 0, 0:T], consts[:, window:window + H], sq_at[:, h, :], start=(h == 0),
                                 stop=(h == H - 1))
            last.then_inc(o_sum, 1)
            pe.wait_ge(inv_ready, 1)
            for h in range(H):
                last = pe.matmul((zb if h < 4 else vb)[:, h % 4, 0:T], head_rows[:, h, :], head_inv[:, :],
                                 start=True, stop=True)
            last.then_inc(inv_spread, 1)

            def out_pair(j, b):
                project(pe, Q_OUT + j, b, 2 * (CT + 12) + 2 * j)

            def square_sum(j, first, last):
                pe.wait_ge(sq_ready, j + 2)
                for k in range(2):
                    done = pe.matmul(vb[:, 0, 0:T], ones, hF[:, bass.ds(2 * j + k, 1), :], start=(first and k == 0),
                                     stop=(last and k == 1))
                return done

            pe.wait_ge(h_split, 2)
            out_pair(0, 0)
            out_pair(1, 1)
            square_sum(0, True, False)
            with pe.Fori(0, KC // 4 - 1) as m:
                out_pair(2 * m + 2, 0)
                square_sum(2 * m + 1, False, False)
                out_pair(2 * m + 3, 1)
                square_sum(2 * m + 2, False, False)
            square_sum(KC // 2 - 1, False, True).then_inc(stat_ready, 1)
            pe.wait_ge(h_half, 2)
            with pe.Fori(0, KC // 4) as m:
                for b in range(2):
                    project(pe, Q_WQ + 2 * m + b, b, 2 * (CT + 12 + KC // 2) + 2 * (2 * m + b), 3)

            def key_scores(tt):
                t0, n = TOK_TILES[tt]
                per_row = 2 * TOPK_HEADS[tt]
                if tt:
                    pe.wait_ge(s_copied, tt)
                for hp in range(2 * H):
                    r0, at_hp = n * (hp // per_row), hp % per_row
                    last = pe.matmul(vb[r0:r0 + n, at_hp // 4, P * (at_hp % 4):P * (at_hp % 4) + P],
                                     qpT[:, hp, t0:t0 + n], keysT[:, hp, :], start=True, stop=True)
                last.then_inc(s_ready, 1)

            def turn_picks(tt):
                n, groups = TOK_TILES[tt][1], H // TOPK_HEADS[tt]
                m = P // groups
                pe.wait_ge(picks_ready, tt + 1)
                if tt:
                    pe.wait_ge(picks_copied, 4 * tt)
                for c in range(3):
                    for g in range(groups):
                        rows = slice(n * g, n * g + n)
                        last = pe.matmul(zb[m * g:m * g + m, 2, c * P:c * P + n], picks[rows, c, 0:m],
                                         ident[rows, rows], start=True, stop=True)
                last.then_inc(picks_turned, 1)

            def last_tile(k):
                n = ADA_FIRST + ADA_MIXER + k
                ada_quad(Q_ADA_LAST + 2 * k, n, k % 2, 0)
                if k:
                    turn_row(n - 1, 1 - k % 2)
                ada_quad(Q_ADA_LAST + 2 * k + 1, n, k % 2, 1)

            pe.wait_ge(qp_copied, KC // 2)
            pe.wait_ge(keys_in, 16)
            key_scores(0)
            key_scores(1)
            last_tile(0)
            key_scores(2)
            last_tile(1)
            turn_picks(0)
            last_tile(2)
            last_tile(3)
            turn_row(ADA_TILES - 1, 1)
            pe.wait_ge(row_copied, ADA_TILES + 2)
            project(pe, Q_PEER, 0)
            turn_picks(1)
            turn_picks(2)
            pe.wait_ge(picks_copied, 4 * 3)

            with pe.Fori(0, G_GROUPS // 2) as i:
                for b in range(2):
                    g = 2 * i + b
                    pe.wait_ge(g_copied, g + 1)
                    pe.wait_ge(one_ready, g + 1)
                    pe.wait_ge(one_act_ready, g + 1)
                    for t in range(8):
                        last = pe.matmul(vb[:, 2 * b + t // 4, NK * (t % 4):NK * (t % 4) + NK], one1[b][:, t, :],
                                         one2[b][:, t, :], start=True, stop=True)
                    last.then_inc(g_ready, 1)

            def mix_experts(i, b, q):
                pe.wait_ge(w_ready, i + 3)
                for s in range(4):
                    pe.wait_ge(lo_ready, 4 * q + s + 5)
                    for d in range(4):
                        if d % 2 == 0:
                            pe.wait_ge(vb_free, 16 * i + 4 * s + d + 1)
                        for e in range(2):
                            v_h = hi[s][:, 512 * e + P * d:512 * e + P * d + P]
                            v_l = lo[s][:, 512 * e + P * d:512 * e + P * d + P]
                            pe.matmul(vb[:, d, 0:T], v_h, w_hi[b][:, e, :], start=(e == 0), stop=False)
                            pe.matmul(vb[:, d, 0:T], v_h, w_lo[b][:, e, :], start=False, stop=False)
                            last = pe.matmul(vb[:, d, 0:T], v_l, w_hi[b][:, e, :], start=False, stop=(e == 1))
                        if d == 1:
                            last.then_inc(vb_ready, 1)
                    last.then_inc(unit_used, 1)

            def body(i, b):
                pe.wait_ge(gelu_done, i + 2)
                project(pe, Q_PEER + 2 * i + 1, (b + 1) % 2)
                mix_experts(i, b, Q_PEER + 2 * i + 2)

            pe.wait_ge(g_copied, G_GROUPS + 2)
            with pe.Fori(0, (PAIRS - 2) // 2) as m:
                body(2 * m, 0)
                body(2 * m + 1, 1)
            body(PAIRS - 2, 0)
            mix_experts(PAIRS - 1, 1, Q_PEER + NK - 1)
            for k in range(KC):
                if k % 4 == 0:
                    pe.wait_ge(sq_ready, KC // 2 + 2 + k // 4)
                last = pe.matmul(zb[:, 0, 0:T], ones, sq[:, k, :], start=(k == 0), stop=(k == KC - 1))
            last.then_inc(stat_ready, 1)

        @block.vector
        def _(dve):
            steps = [0]

            def mark(ins):
                steps[0] += 1
                return ins.then_inc(dve_step, 1)

            def settle():
                dve.wait_ge(dve_step, steps[0])

            def quad_lo(q):
                for s in range(4):
                    split_lo(dve, q, s)

            def inverse_rms(k):
                dve.wait_ge(root_ready, k)
                mark(dve.reciprocal(rs[:, :], rs[:, :]))
                settle()

            def batches(ap):
                return ap[:, :, SEQ:T].rearrange("p k (b s) -> p k b s", b=DB)

            def norm_lo(done, hi_done, scale, shift, from_x):
                def front(c):
                    ks = slice(4 * c, 4 * c + 4)
                    if from_x:
                        mark(dve.tensor_tensor(hF[:, ks, :], xT[:, ks, :], over(rs[:, :], 4), ALU.mult))
                        settle()
                    h = batches(hF[:, ks, :])
                    mark(dve.tensor_tensor(h, h, scale[:, ks, 1:NC].unsqueeze(3).to_broadcast([P, 4, DB, DS]), ALU.mult))
                    settle()
                    dve.tensor_tensor(h, h, shift[:, ks, 1:NC].unsqueeze(3).to_broadcast([P, 4, DB, DS]), ALU.add) \
                        .then_inc(h_ready, 1)

                def back(c):
                    dve.wait_ge(h_ready, done + c + 1)
                    dve.wait_ge(h_hi, hi_done + c + 1)
                    return part_lo(4 * c, 4 * c + 4, hF[:, 4 * c:4 * c + 4, :])

                front(0)
                for c in range(1, 4):
                    front(c)
                    last = back(c - 1)
                    if c == 2:
                        last.then_inc(h_half, 1)
                back(3).then_inc(h_split, 1)

            def part_lo(k0, k1, src):
                return dve.tensor_tensor(act_lo[:, k0:k1, :], src, act_hi[:, k0:k1, :].bitcast(F32), ALU.subtract)

            dve.sem_inc(lo_ready, 4)
            dve.sem_inc(mods_ready, 2)
            dve.sem_inc(glu_ready, 1)
            dve.sem_inc(rope_done, 1)
            dve.sem_inc(vb_free, 4)
            dve.sem_inc(w_ready, 2)
            dve.sem_inc(x1_tile, 1)
            dve.wait_ge(silu_done, 1)
            dve.tensor_copy(c_split[:, :, 0:NC], cT[:, :, :]).then_inc(c_ready, 1)
            dve.wait_ge(c_ready, 1)
            dve.tensor_tensor(c_split[:, :, NC:2 * NC], cT[:, :, :], c_split[:, :, 0:NC].bitcast(F32), ALU.subtract) \
                .then_inc(c_ready, 1)
            quad_lo(0)
            dve.wait_ge(vecs_in, 16)

            def take_mods(n, b):
                dve.wait_ge(row_turned, n + 3)
                dve.tensor_tensor(mods[:, bass.ds(4 * n, 4), :],
                                  zb[:, 3, 64 * b:64 * b + 4 * NC].rearrange("p (c r) -> p c r", c=4),
                                  vecs[:, bass.ds(V_ADA + 4 * n, 4)].unsqueeze(2).to_broadcast([P, 4, NC]),
                                  ALU.add).then_inc(mods_ready, 1)

            def first_tile(n, b, first):
                quad_lo(2 * n + 1)
                if not first:
                    take_mods(n - 1, 1 - b)
                quad_lo(2 * n + 2)

            first_tile(0, 0, True)
            first_tile(1, 1, False)
            first_tile(2, 0, False)
            dve.wait_ge(x_in, 16)
            inverse_rms(1)
            mark(dve.tensor_tensor(hF[:, :, :], xT[:, :, :], over(rs[:, :], KC), ALU.mult))
            with dve.Fori(1, ADA_FIRST // 2 - 1) as m:
                first_tile(2 * m + 1, 1, False)
                first_tile(2 * m + 2, 0, False)
            first_tile(ADA_FIRST - 1, 1, False)
            take_mods(ADA_FIRST - 1, 1)
            dve.wait_ge(mods_ready, ADA_FIRST + 2)

            def mod(i):
                return mods[:, KC * i:KC * i + KC, :]

            def scale_rows(out, i, g):
                mark(dve.scalar_tensor_tensor(out[:, :, :], mod(i), 1.0,
                                              vecs[:, g:g + KC].unsqueeze(2).to_broadcast([P, KC, NC]),
                                              ALU.add, ALU.mult))

            def gate_rows(out, i):
                mark(dve.tensor_scalar(out[:, :, :], mod(i), 1.0, None, ALU.add))

            scale_rows(m_a1, 1, V_G1)
            settle()
            norm_lo(0, 0, m_a1, mod(0), False)

            dve.wait_ge(glu0_in, 16)
            with dve.Fori(0, CT // 2) as m:
                for b in range(2):
                    j = 2 * m + b
                    quad_lo(Q_GLU + 1 + j)
                    dve.wait_ge(sig_ready, j + 1)
                    row = glu[:, bass.ds(j, 1), :]
                    dve.tensor_tensor(row[:, :, HIST:GW_P], zb[:, 2 * b:2 * b + 1, 0:SEQ],
                                      sig[:, 0:SEQ].unsqueeze(1), ALU.mult).then_inc(z_half, 1)
                    new = row[:, :, GW_P:GW].rearrange("p c (b w) -> p (c b) w", b=DB)[:, :, HIST:GW_S]
                    dve.tensor_tensor(new, zb[:, 2 * b, SEQ:T].rearrange("p (b s) -> p b s", b=DB),
                                      sig[:, SEQ:T].rearrange("p (b s) -> p b s", b=DB), ALU.mult) \
                        .then_inc(glu_ready, 1)
                    dve.wait_ge(glu_ready, j + 2)
                    dve.sem_inc(z_free, 2)

            dve.wait_ge(z_half, CT)
            with dve.Fori(0, 2) as m:
                for k in range(6):
                    j = 6 * m + k
                    quad_lo(Q_QKV + 1 + j)
                    dve.wait_ge(qkv_evac, j + 1)
                    dve.sem_inc(z_free, 2)
                    taps = CT_TURN * CONV_W
                    for n in range(taps * k // 6, taps * (k + 1) // 6):
                        w, ct = n // CT_TURN, CT_TURN * m + n % CT_TURN
                        out = conv_y[:, bass.ds(ct, 1), 0:SEQ]
                        window = glu[:, bass.ds(ct, 1), w:w + SEQ]
                        tap = vecs[:, bass.ds(V_CW + CONV_W * ct + w, 1)]
                        if w == 0:
                            dve.tensor_scalar(out, window, tap, vecs[:, bass.ds(V_CB + ct, 1)], ALU.mult, ALU.add) \
                                .then_inc(conv_step, 1)
                        else:
                            dve.wait_ge(conv_step, taps * m + n - CT_TURN + 1)
                            dve.scalar_tensor_tensor(out, window, tap, out, ALU.mult, ALU.add).then_inc(conv_step, 1)
            dve.wait_ge(conv_s_done, CT)
            dve.wait_ge(pool_sum, CONV_W + 1)
            dve.tensor_tensor(conv_y[:, :, SEQ:T], conv_y[:, :, SEQ:T],
                              vecs[:, V_CB:V_CB + CT].unsqueeze(2).to_broadcast([P, CT, TS]), ALU.add) \
                .then_inc(conv_done, 1)

            dve.wait_ge(masks_in, 16)
            cos, sin = (over(masks[0:ROT, c:c + T], 4) for c in (M_RC, M_RS))
            for i in range(4):
                rows = qkvT[0:ROT, 4 * i:4 * i + 4, :]
                dve.wait_ge(rope_perm, i + 1)
                dve.wait_ge(rope_done, i + 1)
                dve.tensor_tensor(r_t[:, :, :], (zb, vb)[i % 2][0:ROT, :, 0:T], sin, ALU.mult).then_inc(rope_step, 1)
                dve.tensor_tensor(rows, rows, cos, ALU.mult).then_inc(rope_step, 1)
                dve.wait_ge(rope_step, 2 * i + 2)
                dve.tensor_tensor(rows, rows, r_t[:, :, :], ALU.add).then_inc(rope_done, 1)

            dve.wait_ge(ln_sum, 1)
            mark(dve.tensor_scalar(rs[:, :], zb[:, 0, 0:T], 1.0 / (CT * P), None, ALU.mult))
            settle()
            dve.tensor_tensor(conv_y[:, :, :], conv_y[:, :, :], over(rs[:, :], CT), ALU.subtract) \
                .then_inc(ln_centred, 1)

            def front(n):
                sample = JOBS[n][1]
                width, neg = (288, M_NS) if sample else (384, M_NP)
                if n >= 2:
                    dve.wait_ge(exp_done, n - 1)
                dve.wait_ge(score_ready, n + 1)
                dve.scalar_tensor_tensor(sc[n % 2][:, 0:width], vb[:, n % 2, 0:width], SCALE,
                                         masks[:, neg:neg + width], ALU.mult, ALU.add).then_inc(masked, 1)
                dve.wait_ge(masked, n + 1)
                for c0, c1, c in JOB_COLS[sample]:
                    last = dve.tensor_reduce(small[:, 6 * n + c:6 * n + c + 1], sc[n % 2][:, c0:c1], AX_X, ALU.max,
                                             negate=True)
                last.then_inc(neg_max, 1)

            def back(n):
                sample = JOBS[n][1]
                cnt = M_CS if sample else M_CP
                dve.wait_ge(exp_done, n + 1)
                for c0, c1, c in JOB_COLS[sample]:
                    col = small[:, 6 * n + c + 2:6 * n + c + 3]
                    mark(dve.tensor_tensor_reduce(ex[n % 2][:, c0:c1], ex[n % 2][:, c0:c1],
                                                  masks[:, cnt + c0:cnt + c1], 1.0, 0.0, ALU.mult, ALU.add, col))
                settle()
                for c0, c1, c in JOB_COLS[sample]:
                    mark(dve.reciprocal(small[:, 6 * n + c + 4:6 * n + c + 5], small[:, 6 * n + c + 2:6 * n + c + 3]))
                settle()
                for c0, c1, c in JOB_COLS[sample]:
                    last = dve.tensor_scalar(ex[n % 2][:, c0:c1], ex[n % 2][:, c0:c1],
                                             small[:, 6 * n + c + 4:6 * n + c + 5], None, ALU.mult)
                last.then_inc(prob_ready, 1)

            front(0)
            inverse_rms(2)
            dve.tensor_tensor(conv_y[:, :, :], conv_y[:, :, :], over(rs[:, :], CT), ALU.mult).then_inc(ln_z, 1)
            def ada_step(k):
                quad_lo(Q_ADA_MIXER + k + 1)
                if k and k % 2 == 0:
                    take_mods(ADA_FIRST + k // 2 - 1, (k // 2 - 1) % 2)

            for n in range(len(JOBS)):
                ada = ada_steps(n)
                ada_step(ada[0])
                back(n)
                ada_step(ada[1])
                if n + 1 < len(JOBS):
                    front(n + 1)
                for k in ada[2:4]:
                    ada_step(k)
                if n == SILU_JOBS + 1:
                    dve.wait_ge(h_hi, 5)
                    part_lo(0, CT, conv_y[:, :, :])
            take_mods(ADA_FIRST + ADA_MIXER - 1, 1)
            dve.wait_ge(mods_ready, ADA_FIRST + ADA_MIXER + 2)
            scale_rows(m_a2, 4, V_G2)
            gate_rows(m_g2, 2)
            dve.wait_ge(root_ready, 3)
            dve.reciprocal(head_inv[:, :], head_inv[:, :]).then_inc(inv_ready, 1)
            dve.wait_ge(inv_spread, 1)
            for h in range(H):
                last = dve.scalar_tensor_tensor(oT[:, h, :], oT[:, h, :], vecs[:, V_AG + h:V_AG + h + 1],
                                                (zb if h < 4 else vb)[:, h % 4, 0:T], ALU.mult, ALU.mult)
            last.then_inc(o_normed, 1)
            dve.wait_ge(h_hi, 6)
            dve.wait_ge(o_normed, 1)
            part_lo(CT, KC, oT).then_inc(h_split, 1)

            with dve.Fori(0, KC // 4) as m:
                for b in range(2):
                    j = 2 * m + b
                    quad_lo(Q_OUT + 1 + j)
                    dve.wait_ge(unit_used, 4 * (Q_OUT + j) + 8)
                    for t in range(2):
                        gate = m_g2[:, bass.ds(2 * j + t, 1), 0]
                        x = xT[:, bass.ds(2 * j + t, 1), 0:SEQ]
                        dve.scalar_tensor_tensor(x, zb[:, 2 * b + t:2 * b + t + 1, 0:SEQ], gate, x, ALU.mult, ALU.add)
                    dve.wait_ge(x1_tile, j + 1)
                    for t in range(2):
                        gate = m_g2[:, bass.ds(2 * j + t, 1), 1:NC].rearrange("p k b -> p (k b)")
                        last = dve.tensor_tensor(tmp_s[:, t, :].rearrange("p (b s) -> p b s", b=DB),
                                                 zb[:, 2 * b + t, SEQ:T].rearrange("p (b s) -> p b s", b=DB),
                                                 gate.unsqueeze(2).to_broadcast([P, DB, DS]), ALU.mult)
                    last.then_inc(x1_step, 1)
                    dve.wait_ge(x1_step, j + 1)
                    dve.sem_inc(z_free, 2)
                    x = xT[:, bass.ds(2 * j, 2), SEQ:T]
                    dve.tensor_tensor(x, x, tmp_s[:, :, :], ALU.add).then_inc(x1_tile, 1)
            dve.wait_ge(x1_tile, KC // 2 + 1)
            inverse_rms(4)
            norm_lo(4, 6, m_a2, mod(3), True)
            with dve.Fori(0, KC // 2) as j:
                quad_lo(Q_WQ + 1 + j)
                dve.wait_ge(qp_copied, j + 1)
                dve.sem_inc(z_free, 2)

            for tt, hn in enumerate(TOPK_HEADS):
                dve.wait_ge(s_copied, tt + 1)
                for hp in range(2 * hn):
                    mark(dve.max(sv[:, hp, 0:8], s_tm[:, hp, :]))
                settle()
                for hp in range(2 * hn):
                    dve.max_index(si_u[:, hp, 0:8], sv[:, hp, 0:8], s_tm[:, hp, :])
                    last = dve.match_replace(s_work[:, hp, :], sv[:, hp, 0:8], s_tm[:, hp, :], NEG)
                last.then_inc(s_read, 1)
                dve.wait_ge(s_read, tt + 1)
                for hp in range(2 * hn):
                    mark(dve.max(sv[:, hp, 8:16], s_work[:, hp, :]))
                settle()
                for hp in range(2 * hn):
                    last = dve.max_index(si_u[:, hp, 8:16], sv[:, hp, 8:16], s_work[:, hp, :])
                mark(last)
                s4 = sv[:, 0:2 * hn, :].rearrange("n (h p) k -> n h p k", p=2)
                mark(dve.tensor_tensor(cand[:, 0:hn, :].rearrange("n h (a b) -> n h a b", a=TOPK),
                                       s4[:, :, 0, :].unsqueeze(3).to_broadcast([P, hn, TOPK, TOPK]),
                                       s4[:, :, 1, :].unsqueeze(2).to_broadcast([P, hn, TOPK, TOPK]), ALU.add))
                settle()
                mark(dve.tensor_copy(si_f[:, 0:2 * hn, :], si_u[:, 0:2 * hn, :]))
                fi3 = fi_u[:, :].rearrange("n (h k) -> n h k", h=H)
                for h in range(hn):
                    mark(dve.max(fv[:, h, 0:8], cand[:, h, :]))
                settle()
                for h in range(hn):
                    dve.max_index(fi3[:, h, 0:8], fv[:, h, 0:8], cand[:, h, :])
                    mark(dve.match_replace(c_work[:, h, :], fv[:, h, 0:8], cand[:, h, :], NEG))
                settle()
                for h in range(hn):
                    mark(dve.max(fv[:, h, 8:16], c_work[:, h, :]))
                settle()
                for h in range(hn):
                    mark(dve.max_index(fi3[:, h, 8:16], fv[:, h, 8:16], c_work[:, h, :]))
                dve.tensor_tensor(g_exp[:, 0:hn, :], fv[:, 0:hn, :], fv[:, 0:hn, 0:1].to_broadcast([P, hn, TOPK]),
                                  ALU.subtract).then_inc(gate_in, 1)
                settle()
                mark(dve.tensor_single_scalar(f_au[:, 0:hn * TOPK], fi_u[:, 0:hn * TOPK], 4, ALU.logical_shift_right))
                mark(dve.tensor_single_scalar(f_bu[:, 0:hn * TOPK], fi_u[:, 0:hn * TOPK], 15, ALU.bitwise_and))
                settle()
                mark(dve.tensor_copy(f_a[:, 0:hn * TOPK], f_au[:, 0:hn * TOPK]))
                mark(dve.tensor_copy(f_b[:, 0:hn * TOPK], f_bu[:, 0:hn * TOPK]))
                if tt:
                    dve.wait_ge(picks_turned, tt)
                settle()
                io16 = over(consts[:, K_IO16:K_IO16 + TOPK], hn * TOPK)
                si4 = si_f[:, 0:2 * hn, :].rearrange("n (h p) k -> n h p k", p=2)
                for p, f in enumerate((f_a, f_b)):
                    mark(dve.tensor_tensor(oh[:, 0:hn * TOPK, :], f[:, 0:hn * TOPK].unsqueeze(2).to_broadcast([P, hn * TOPK, TOPK]),
                                           io16, ALU.is_equal))
                    settle()
                    oh4 = oh[:, 0:hn * TOPK, :].rearrange("n (h k) a -> n h k a", h=hn)
                    mark(dve.tensor_tensor(oh4, oh4, si4[:, :, p, :].unsqueeze(2).to_broadcast([P, hn, TOPK, TOPK]),
                                           ALU.mult))
                    settle()
                    mark(dve.tensor_reduce(picks[:, p, 0:hn * TOPK], oh[:, 0:hn * TOPK, :], AX_X, ALU.add))
                    settle()
                dve.wait_ge(gate_out, tt + 1)
                mark(dve.tensor_reduce(small[:, 0:hn], g_exp[:, 0:hn, :], AX_X, ALU.add))
                settle()
                mark(dve.reciprocal(small[:, H:H + hn], small[:, 0:hn]))
                settle()
                dve.tensor_tensor(picks[:, 2, 0:hn * TOPK].rearrange("n (h k) -> n h k", h=hn), g_exp[:, 0:hn, :],
                                  small[:, H:H + hn].unsqueeze(2).to_broadcast([P, hn, TOPK]), ALU.mult) \
                    .then_inc(picks_ready, 1)

            dve.wait_ge(mods_ready, ADA_TILES + 2)
            mark(dve.tensor_scalar(m_g5[:, :, :], m_g5[:, :, :], 1.0, None, ALU.add))
            dve.wait_ge(picks_copied, 4 * 3)
            with dve.Fori(0, G_GROUPS // 2) as i:
                for b in range(2):
                    g = 2 * i + b
                    dve.wait_ge(g_ready, g + 1)
                    for t in range(8 - ON_ACT):
                        dve.tensor_scalar(one1[b][:, t, :], iota, i1T[:, bass.ds(8 * g + t, 1)],
                                          gT[:, bass.ds(8 * g + t, 1)], ALU.is_equal, ALU.mult)
                    dve.tensor_tensor(one2[b][:, :, :], over(iota, 8),
                                      i2T[:, bass.ds(8 * g, 8)].unsqueeze(2).to_broadcast([P, 8, NK]),
                                      ALU.is_equal).then_inc(one_ready, 1)

            def weigh(pair, b, chunk):
                dve.wait_ge(gelu_done, pair + 3)
                dve.wait_ge(w_ready, pair + 2)
                gates = G[:, bass.ds(chunk, 1), :, 2 * b:2 * b + 2, :].rearrange("p c b e t -> p e (c b) t")
                values = gl[b][:, :, :].rearrange("p e (b t) -> p e b t", t=TB)
                for out in (w_f, w_hi[b]):
                    last = dve.tensor_tensor(out[:, :, :].rearrange("p e (b t) -> p e b t", t=TB), values, gates,
                                             ALU.mult)
                last.then_inc(w_mid, 1)
                dve.wait_ge(w_mid, pair + 1)
                dve.tensor_tensor(w_lo[b][:, :, :], w_f[:, :, :], w_hi[b][:, :, :].bitcast(F32), ALU.subtract) \
                    .then_inc(w_ready, 1)

            def add_sums(pair, q, s, q_next):
                for d in range(2):
                    if d == 0:
                        dve.wait_ge(vb_ready, 4 * pair + s + 1)
                    else:
                        if s and q_next is not None:
                            split_lo(dve, q_next, s - 1)
                        dve.wait_ge(unit_used, 4 * q + s + 5)
                    out = acc[:, 4 * s + 2 * d:4 * s + 2 * d + 2, :]
                    dve.tensor_tensor(out, out, vb[:, 2 * d:2 * d + 2, 0:T], ALU.add).then_inc(vb_free, 2)

            def body(i, b, chunk):
                weigh(i, b, chunk)
                quad_lo(Q_PEER + 2 * i + 2)
                dve.wait_ge(acc_zero, 1)
                for s in range(4):
                    add_sums(i, Q_PEER + 2 * i + 2, s, Q_PEER + 2 * i + 3)
                split_lo(dve, Q_PEER + 2 * i + 3, 3)

            dve.wait_ge(g_copied, G_GROUPS + 2)
            dve.wait_ge(lo_ready, 4 * (Q_PEER + 1) + 8)
            with dve.Fori(0, CHUNKS) as c:
                body(2 * c, 0, c)
                body(2 * c + 1, 1, c)
            with dve.Fori(0, CHUNKS - 1) as c:
                dve.wait_ge(g2_in, 16 * c + 16)
                body(2 * c + 2 * CHUNKS, 0, c)
                body(2 * c + 2 * CHUNKS + 1, 1, c)
            dve.wait_ge(g2_in, 16 * CHUNKS)
            body(PAIRS - 2, 0, CHUNKS - 1)
            weigh(PAIRS - 1, 1, CHUNKS - 1)
            dve.wait_ge(x1_in, 16)
            for s in range(4):
                add_sums(PAIRS - 1, Q_PEER + NK - 1, s, None)
                dve.wait_ge(vb_free, 16 * (PAIRS - 1) + 4 * s + 8)
                ks = slice(4 * s, 4 * s + 4)
                for k in range(4 * s, 4 * s + 4):
                    mark(dve.scalar_tensor_tensor(x2[:, k, 0:SEQ], acc[:, k, 0:SEQ], m_g5[:, k, 0:1], x2[:, k, 0:SEQ],
                                                  ALU.mult, ALU.add))
                new = acc[:, ks, SEQ:T].rearrange("p k (b s) -> p k b s", b=DB)
                mark(dve.tensor_tensor(new, new, m_g5[:, ks, 1:NC].unsqueeze(3).to_broadcast([P, 4, DB, DS]), ALU.mult))
                settle()
                dve.tensor_tensor(x2[:, ks, SEQ:T], x2[:, ks, SEQ:T], acc[:, ks, SEQ:T], ALU.add).then_inc(x2_ready, 1)
            inverse_rms(5)
            for k in range(KC):
                last = dve.scalar_tensor_tensor(fin[:, k, :], x2[:, k, :], vecs[:, V_GF + k:V_GF + k + 1], rs[:, :],
                                                ALU.mult, ALU.mult)
                if k % 4 == 3:
                    last.then_inc(y_ready, 1)


_OUTS = [("y", (P, KC, T)), ("k", (P, H, T)), ("v", (P, H, T)), ("conv_p", (P, CT, HIST)),
         ("conv_s", (P, CT, DB, HIST))]


def kernel(**a):
    import numpy as np
    import concourse.bacc as bacc
    from concourse.bass_utils import run_bass_kernel_spmd

    a = {k: np.asarray(v) for k, v in a.items()}

    def channels(x, *rest):
        return x.reshape(-1, x.shape[-1] // P, P).transpose(2, 1, 0)

    def tiles(w):
        return w.reshape(KC, P, -1, P).transpose(2, 1, 0, 3).reshape(-1, P, KC * P)

    x = np.concatenate([a["x_prompt"].reshape(SEQ, D), a["x_sample"].reshape(TS, D)])
    c = np.concatenate([a["c_prompt"], a["c_sample"]])
    glu0 = np.zeros((P, CT, GW), np.float32)
    hist = a["state_conv"][0].reshape(DB, HIST, CT, P).transpose(3, 2, 0, 1)
    glu0[:, :, GW_P:].reshape(P, CT, DB, GW_S)[..., :HIST] = hist
    w_in = tiles(a["w_in"][0])
    order = [t for j in range(CT) for t in (j, CT + j)] + list(range(2 * CT, 2 * CT + 3 * H))
    ck = a["cache_k"][0].reshape(2, 4, PAST, H, E).transpose(3, 0, 4, 1, 2).reshape(H, 2, E, UNIT)
    cv = a["cache_v"][0].reshape(2, 4, 2, P, H, E).transpose(4, 0, 3, 2, 1, 5).reshape(H, 2, P, UNIT)
    u = a["peer_u"][0].reshape(NK, NK, KC, P).transpose(1, 3, 2, 0).reshape(NK, P, KC * P)

    vecs = np.zeros((P, V_N), np.float32)
    for at, v in ((V_G1, a["norm1_g"]), (V_G2, a["norm2_g"]), (V_GF, a["final_g"]), (V_LNG, a["conv_ln_g"]),
                  (V_LNB, a["conv_ln_b"]), (V_CB, a["conv_b"]), (V_AG, a["attn_out_g"]), (V_ADA, a["b_ada"])):
        n = v.size // P
        vecs[:, at:at + n] = v.reshape(n, P).T
    vecs[:, V_CW:V_ADA] = a["conv_w"][0].reshape(CONV_W, CT, P).transpose(2, 1, 0).reshape(P, -1)

    consts = np.zeros((P, K_N), np.float32)
    consts[:, K_ID:K_ID + P] = np.eye(P)
    consts[:, K_ONE:K_ONE + P] = 1.0
    consts[:, K_IOTA:K_IOTA + NK] = np.arange(NK)
    consts[:2 * NC, K_SEL:K_SEL + NC] = np.tile(np.eye(NC), (2, 1))
    consts[:, K_IO16:K_IO16 + TOPK] = np.arange(TOPK)
    consts[:, K_EPS] = EPS
    consts[:, K_HEAD + H - 1] = 1.0

    def patterns(d):
        return sum(((d >= 0) & (d % dil == 0) & (d // dil <= win // dil)).astype(np.float32)
                   for win, dil in ((128, 1), (512, 4), (2048, 16)))

    masks = np.zeros((P, M_N), np.float32)
    r = np.arange(P)[:, None]
    prompt = np.concatenate([patterns(r - r.T), patterns(128 + r - np.arange(256)[None])], axis=1)
    b, s = r // DS % DB, r % DS
    new = np.arange(TS)[None]
    sample = np.concatenate([patterns(PAST + s - np.arange(PAST)[None]),
                             patterns(s - new % DS) * (b == new // DS)], axis=1)
    for cnt, neg, m in ((M_CP, M_NP, prompt), (M_CS, M_NS, sample)):
        masks[:, cnt:cnt + m.shape[1]] = m
        masks[:, neg:neg + m.shape[1]] = np.where(m > 0, 0.0, -1e30)
    pos = np.concatenate([np.arange(SEQ), PAST + np.arange(TS) % DS]).astype(np.float32)
    inv = np.float32(500000.0) ** (-np.arange(0, ROT, 2, dtype=np.float32) / np.float32(ROT))
    ang = (pos[None] * inv[:, None]).astype(np.float32)
    masks[:ROT, M_RC:M_RC + T] = np.tile(np.cos(ang), (2, 1))
    masks[:ROT // 2, M_RS:M_RS + T] = -np.sin(ang)
    masks[ROT // 2:ROT, M_RS:M_RS + T] = np.sin(ang)
    masks[np.arange(ROT), M_PERM + (np.arange(ROT) + ROT // 2) % ROT] = 1.0

    ins = {
        "xT": channels(x), "cT": channels(c), "glu0": glu0,
        "w_ada": a["w_ada"][0].reshape(8, 2, P, ADA_TILES, 512).transpose(3, 0, 2, 1, 4).reshape(ADA_TILES, 8, P, UNIT),
        "w_in": w_in[order], "w_out": tiles(a["w_out"][0]), "w_q": tiles(a["peer_wq"][0]),
        "keys": a["peer_keys"][0].reshape(2 * H, NK, P).transpose(2, 0, 1),
        "u": u, "v": a["peer_v"][0].reshape(NK, NK, D), "ck": ck, "cv": cv,
        "vecs": vecs, "consts": consts, "masks": masks,
    }
    nc = bacc.Bacc("TRN2", target_bir_lowering=False, num_devices=1)
    ins = {f"in_{k}": np.ascontiguousarray(v) for k, v in ins.items()}
    args = [nc.dram_tensor(k, v.shape, F32, kind="ExternalInput").ap() for k, v in ins.items()]
    args += [nc.dram_tensor(f"out_{k}", s, F32, kind="ExternalOutput").ap() for k, s in _OUTS]
    layer_kernel(nc, *args)
    got = run_bass_kernel_spmd(nc, [ins], core_ids=[0]).results[0]

    y = got["out_y"].transpose(2, 1, 0).reshape(T, D)
    k, v = (got[f"out_{n}"].transpose(2, 1, 0) for n in "kv")
    conv_p = got["out_conv_p"].transpose(2, 1, 0).reshape(1, 1, HIST, CT * P)
    conv_s = got["out_conv_s"].transpose(2, 3, 1, 0).reshape(1, DB, HIST, CT * P)
    y, k, v, conv_p, conv_s = (np.ascontiguousarray(z) for z in (y, k, v, conv_p, conv_s))
    return (y[:SEQ].reshape(1, SEQ, D), y[SEQ:].reshape(DB, DS, D),
            k[:SEQ].reshape(1, 1, SEQ, H, E), v[:SEQ].reshape(1, 1, SEQ, H, E), conv_p,
            k[SEQ:].reshape(1, DB, DS, H, E), v[SEQ:].reshape(1, DB, DS, H, E), conv_s)
```
